# Optimizing a Trainium2 kernel written in Bass

```python
import math
import jax
import jax.numpy as jnp
from jax import lax
import numpy as np

'''Hybrid YOCO-style decoder trunk: Mamba-2 SSD layers first, then sliding-window
GQA layers with attention sinks that all read ONE shared K/V computed from the
residual stream after the last SSD layer (including its MoE). Every layer also
cross-attends (4 heads) into 256 memory tokens, and every layer ends with a
hierarchical (top-1 group -> top-2 expert) MoE of gated MLPs.

Inputs:  x   (BATCH, SEQ, D_MODEL) float32
         mem (BATCH, MEM_LEN, D_MODEL) float32
         plus learned parameters (see setup_inputs)
Output:  (BATCH, SEQ, D_MODEL)
'''

D_MODEL = 1024
BATCH = 1
SEQ = 256
DEPTH = 2

N_A_LAYERS = DEPTH // 2
N_B_LAYERS = DEPTH - N_A_LAYERS
NORM_EPS = 1e-6

MEM_LEN = 256
MEM_HEADS = 4
MEM_HEAD_DIM = D_MODEL // 8
MEM_WIDTH = MEM_HEADS * MEM_HEAD_DIM

SSD_HEAD_DIM = 64
SSD_INNER = 3 * D_MODEL // 2
SSD_HEADS = SSD_INNER // SSD_HEAD_DIM
SSD_GROUPS = 4
SSD_STATE = 128
CONV_WIDTH = 4
SSD_CHUNK = 128
DT_MIN = 1e-3
DT_MAX = 1e-1
CONV_CH = SSD_INNER + 2 * SSD_GROUPS * SSD_STATE
A_IN_WIDTH = SSD_INNER + CONV_CH + SSD_HEADS + MEM_WIDTH
A_MIX_WIDTH = SSD_INNER + MEM_WIDTH

HEAD_DIM = 64
Q_HEADS = D_MODEL // HEAD_DIM
KV_HEADS = 4
WINDOW = 128
ATTN_BLOCK = 128
ROT_DIM = HEAD_DIM // 4
ROPE_THETA = 500000.0
Q_WIDTH = Q_HEADS * HEAD_DIM
KV_WIDTH = KV_HEADS * HEAD_DIM
B_MIX_WIDTH = Q_WIDTH + MEM_WIDTH

N_EXPERT_GROUPS = 4
EXPERTS_PER_GROUP = 8
N_EXPERTS = N_EXPERT_GROUPS * EXPERTS_PER_GROUP
TOP_K_IN_GROUP = 2
D_EXPERT = D_MODEL // 2

kernel_name = 'yoco_ssd_swa_sink_memory_hmoe'

def rms_norm(x, w):
    xf = x.astype(jnp.float32)
    y = xf * lax.rsqrt(jnp.mean(xf * xf, axis=-1, keepdims=True) + NORM_EPS)
    return (y * w.astype(jnp.float32)).astype(x.dtype)

def partial_rope(x, positions):
    half = ROT_DIM // 2
    inv_freq = ROPE_THETA ** (-2.0 * jnp.arange(half, dtype=jnp.float32) / ROT_DIM)
    ang = positions.astype(jnp.float32)[:, None] * inv_freq[None, :]
    cos = jnp.cos(ang)[None, :, None, :]
    sin = jnp.sin(ang)[None, :, None, :]
    xf = x.astype(jnp.float32)
    x1, x2, rest = xf[..., :half], xf[..., half:ROT_DIM], xf[..., ROT_DIM:]
    out = jnp.concatenate([x1 * cos - x2 * sin, x2 * cos + x1 * sin, rest], axis=-1)
    return out.astype(x.dtype)

def memory_cross_attention(q, mem, norm_w, w_kv):
    bsz, s, _ = q.shape
    m = mem.shape[1]
    kv = (rms_norm(mem, norm_w) @ w_kv).reshape(bsz, m, 2, MEM_HEADS, MEM_HEAD_DIM)
    k, v = kv[:, :, 0], kv[:, :, 1]
    qh = q.reshape(bsz, s, MEM_HEADS, MEM_HEAD_DIM)
    scores = jnp.einsum('bshd,bmhd->bhsm', qh, k, preferred_element_type=jnp.float32) * (MEM_HEAD_DIM ** -0.5)
    p = jax.nn.softmax(scores, axis=-1).astype(v.dtype)
    return jnp.einsum('bhsm,bmhd->bshd', p, v).reshape(bsz, s, MEM_WIDTH)

def causal_depthwise_conv(x, w, b):
    out = lax.conv_general_dilated(
        x, w[:, None, :].astype(x.dtype), window_strides=(1,),
        padding=((CONV_WIDTH - 1, 0),), dimension_numbers=('NWC', 'WIO', 'NWC'),
        feature_group_count=x.shape[-1])
    return out + b.astype(x.dtype)

def ssd_chunked_scan(x, dt, a, bmat, cmat):
    bsz, s = x.shape[0], x.shape[1]
    nc = s // SSD_CHUNK
    r = SSD_HEADS // SSD_GROUPS

    def to_chunks(t):
        return jnp.moveaxis(t.reshape(bsz, nc, SSD_CHUNK, *t.shape[2:]), 1, 0)

    xdt = (x * dt[..., None]).reshape(bsz, s, SSD_GROUPS, r, SSD_HEAD_DIM)
    adt = (dt * a).reshape(bsz, s, SSD_GROUPS, r)
    causal = jnp.tril(jnp.ones((SSD_CHUNK, SSD_CHUNK), dtype=bool))[None, :, :, None, None]

    def step(state, inp):
        xc, ac, bc, cc = inp
        acum = jnp.cumsum(ac, axis=1)
        seg = acum[:, :, None] - acum[:, None, :]
        decay = jnp.exp(jnp.where(causal, seg, -jnp.inf))
        cb = jnp.einsum('blgn,bsgn->blsg', cc, bc)
        y_diag = jnp.einsum('blsgr,bsgrp->blgrp', cb[..., None] * decay, xc)
        y_off = jnp.einsum('blgn,bgrpn->blgrp', cc, state) * jnp.exp(acum)[..., None]
        a_last = acum[:, -1]
        to_end = jnp.exp(a_last[:, None] - acum)
        new_state = state * jnp.exp(a_last)[..., None, None] + jnp.einsum(
            'bsgn,bsgrp->bgrpn', bc, xc * to_end[..., None])
        return new_state, y_diag + y_off

    state0 = jnp.zeros((bsz, SSD_GROUPS, r, SSD_HEAD_DIM, SSD_STATE), jnp.float32)
    _, y = lax.scan(step, state0, (to_chunks(xdt), to_chunks(adt), to_chunks(bmat), to_chunks(cmat)))
    return jnp.moveaxis(y, 0, 1).reshape(bsz, s, SSD_HEADS, SSD_HEAD_DIM)

def ssd_memory_mixer(h, mem, norm_w, in_w, conv_w, conv_b, dt_bias, a_log, d_skip, gnorm_w, out_w, mem_norm_w, mem_w_kv):
    bsz, s, _ = h.shape
    f32 = jnp.float32
    proj = rms_norm(h, norm_w) @ in_w
    z, xbc, dt, q_mem = jnp.split(proj, [SSD_INNER, SSD_INNER + CONV_CH, SSD_INNER + CONV_CH + SSD_HEADS], axis=-1)
    xbc = jax.nn.silu(causal_depthwise_conv(xbc, conv_w, conv_b))
    xs, bm, cm = jnp.split(xbc, [SSD_INNER, SSD_INNER + SSD_GROUPS * SSD_STATE], axis=-1)
    xs = xs.astype(f32).reshape(bsz, s, SSD_HEADS, SSD_HEAD_DIM)
    dt = jax.nn.softplus(dt.astype(f32) + dt_bias.astype(f32))
    a = -jnp.exp(a_log.astype(f32))
    y = ssd_chunked_scan(xs, dt, a,
                         bm.astype(f32).reshape(bsz, s, SSD_GROUPS, SSD_STATE),
                         cm.astype(f32).reshape(bsz, s, SSD_GROUPS, SSD_STATE))
    y = y + d_skip.astype(f32)[:, None] * xs
    y = y.reshape(bsz, s, SSD_INNER) * jax.nn.silu(z.astype(f32))
    yg = y.reshape(bsz, s, SSD_GROUPS, SSD_INNER // SSD_GROUPS)
    yg = yg * lax.rsqrt(jnp.mean(yg * yg, axis=-1, keepdims=True) + NORM_EPS)
    y = (yg.reshape(bsz, s, SSD_INNER) * gnorm_w.astype(f32)).astype(h.dtype)
    m = memory_cross_attention(q_mem, mem, mem_norm_w, mem_w_kv)
    return jnp.concatenate([y, m], axis=-1) @ out_w

def shared_kv(h, norm_w, w_kv, positions):
    bsz, s, _ = h.shape
    kv = (rms_norm(h, norm_w) @ w_kv).reshape(bsz, s, 2, KV_HEADS, HEAD_DIM)
    return partial_rope(kv[:, :, 0], positions), kv[:, :, 1]

def sliding_window_sink_attention(q, k, v, sinks):
    bsz, s = q.shape[0], q.shape[1]
    nblk = s // ATTN_BLOCK
    g = Q_HEADS // KV_HEADS
    f32 = jnp.float32
    qb = jnp.moveaxis(q.reshape(bsz, nblk, ATTN_BLOCK, KV_HEADS, g, HEAD_DIM), 1, 0)
    pad = ((0, 0), (ATTN_BLOCK, 0), (0, 0), (0, 0))
    kp, vp = jnp.pad(k, pad), jnp.pad(v, pad)
    t_idx = jnp.arange(ATTN_BLOCK)[:, None]
    s_idx = jnp.arange(2 * ATTN_BLOCK)[None, :]
    band = (s_idx > t_idx + ATTN_BLOCK - WINDOW) & (s_idx <= t_idx + ATTN_BLOCK)
    sink = sinks.astype(f32).reshape(KV_HEADS, g)[None, :, :, None]
    scale = HEAD_DIM ** -0.5

    def one_block(args):
        i, qi = args
        start = i * ATTN_BLOCK
        ki = lax.dynamic_slice_in_dim(kp, start, 2 * ATTN_BLOCK, axis=1)
        vi = lax.dynamic_slice_in_dim(vp, start, 2 * ATTN_BLOCK, axis=1)
        valid = band & (start - ATTN_BLOCK + s_idx >= 0)
        sc = jnp.einsum('bqhgd,bkhd->bhgqk', qi, ki, preferred_element_type=f32) * scale
        sc = jnp.where(valid, sc, -jnp.inf)
        mx = jnp.maximum(jnp.max(sc, axis=-1), sink)
        p = jnp.exp(sc - mx[..., None])
        denom = jnp.sum(p, axis=-1) + jnp.exp(sink - mx)
        return jnp.einsum('bhgqk,bkhd->bqhgd', (p / denom[..., None]).astype(vi.dtype), vi)

    out = lax.map(one_block, (jnp.arange(nblk), qb))
    return jnp.moveaxis(out, 0, 1).reshape(bsz, s, Q_WIDTH)

def swa_memory_mixer(h, k_sh, v_sh, mem, positions, norm_w, in_w, sinks, out_w, mem_norm_w, mem_w_kv):
    bsz, s, _ = h.shape
    proj = rms_norm(h, norm_w) @ in_w
    q, q_mem = jnp.split(proj, [Q_WIDTH], axis=-1)
    q = partial_rope(q.reshape(bsz, s, Q_HEADS, HEAD_DIM), positions)
    att = sliding_window_sink_attention(q, k_sh, v_sh, sinks)
    m = memory_cross_attention(q_mem, mem, mem_norm_w, mem_w_kv)
    return jnp.concatenate([att, m], axis=-1) @ out_w

def hierarchical_moe(h, norm_w, rg_w, rg_b, re_w, re_b, w_gate, w_up, w_down):
    bsz, s, d = h.shape
    f32 = jnp.float32
    xt = rms_norm(h, norm_w).reshape(-1, d)
    group_p = jax.nn.softmax((xt @ rg_w).astype(f32) + rg_b.astype(f32), axis=-1)
    g_w, g_idx = lax.top_k(group_p, 1)
    exp_logits = ((xt @ re_w).astype(f32) + re_b.astype(f32)).reshape(-1, N_EXPERT_GROUPS, EXPERTS_PER_GROUP)
    in_group = jnp.einsum('tg,tge->te', jax.nn.one_hot(g_idx[:, 0], N_EXPERT_GROUPS, dtype=f32), exp_logits)
    e_val, e_idx = lax.top_k(in_group, TOP_K_IN_GROUP)
    e_w = jax.nn.softmax(e_val, axis=-1) * g_w
    expert_id = g_idx * EXPERTS_PER_GROUP + e_idx
    gates = jnp.sum(jax.nn.one_hot(expert_id, N_EXPERTS, dtype=f32) * e_w[..., None], axis=1).astype(xt.dtype)
    out = jnp.zeros_like(xt)
    for e in range(N_EXPERTS):
        he = jax.nn.silu(xt @ w_gate[e]) * (xt @ w_up[e])
        out = out + gates[:, e:e + 1] * (he @ w_down[e])
    return out.reshape(bsz, s, d)

def setup_inputs(seed: int = 0) -> dict:
    key = jax.random.key(seed)
    ks = iter(jax.random.split(key, 40))
    f32 = jnp.float32
    d, na, nb = D_MODEL, N_A_LAYERS, N_B_LAYERS

    def nrm(shape, scale):
        return jax.random.normal(next(ks), shape, f32) * scale

    def gain(shape):
        return 1.0 + nrm(shape, 0.02)

    x = nrm((BATCH, SEQ, d), 1.0)
    mem = nrm((BATCH, MEM_LEN, d), 1.0)
    a_norm_w = gain((na, d))
    a_in_w = nrm((na, d, A_IN_WIDTH), d ** -0.5)
    a_conv_w = nrm((na, CONV_WIDTH, CONV_CH), CONV_WIDTH ** -0.5)
    a_conv_b = nrm((na, CONV_CH), 0.01)
    dt0 = jnp.exp(jax.random.uniform(next(ks), (na, SSD_HEADS), f32, math.log(DT_MIN), math.log(DT_MAX)))
    a_dt_bias = dt0 + jnp.log(-jnp.expm1(-dt0))
    a_a_log = jnp.log(jax.random.uniform(next(ks), (na, SSD_HEADS), f32, 1.0, 16.0))
    a_d_skip = gain((na, SSD_HEADS))
    a_gnorm_w = gain((na, SSD_INNER))
    a_out_w = nrm((na, A_MIX_WIDTH, d), A_MIX_WIDTH ** -0.5)
    kv_norm_w = gain((d,))
    w_kv = nrm((d, 2 * KV_WIDTH), d ** -0.5)
    b_norm_w = gain((nb, d))
    b_in_w = nrm((nb, d, B_MIX_WIDTH), d ** -0.5)
    b_sinks = nrm((nb, Q_HEADS), 0.5)
    b_out_w = nrm((nb, B_MIX_WIDTH, d), B_MIX_WIDTH ** -0.5)
    mem_norm_w = gain((DEPTH, d))
    mem_w_kv = nrm((DEPTH, d, 2 * MEM_WIDTH), d ** -0.5)
    ffn_norm_w = gain((DEPTH, d))
    router_group_w = nrm((DEPTH, d, N_EXPERT_GROUPS), d ** -0.5)
    router_group_b = nrm((DEPTH, N_EXPERT_GROUPS), 0.01)
    router_expert_w = nrm((DEPTH, d, N_EXPERTS), d ** -0.5)
    router_expert_b = nrm((DEPTH, N_EXPERTS), 0.01)
    w_gate = nrm((DEPTH, N_EXPERTS, d, D_EXPERT), d ** -0.5)
    w_up = nrm((DEPTH, N_EXPERTS, d, D_EXPERT), d ** -0.5)
    w_down = nrm((DEPTH, N_EXPERTS, D_EXPERT, d), D_EXPERT ** -0.5)
    final_norm_w = gain((d,))
    return {'x': x, 'mem': mem, 'a_norm_w': a_norm_w, 'a_in_w': a_in_w, 'a_conv_w': a_conv_w,
            'a_conv_b': a_conv_b, 'a_dt_bias': a_dt_bias, 'a_a_log': a_a_log, 'a_d_skip': a_d_skip,
            'a_gnorm_w': a_gnorm_w, 'a_out_w': a_out_w, 'kv_norm_w': kv_norm_w, 'w_kv': w_kv,
            'b_norm_w': b_norm_w, 'b_in_w': b_in_w, 'b_sinks': b_sinks, 'b_out_w': b_out_w,
            'mem_norm_w': mem_norm_w, 'mem_w_kv': mem_w_kv, 'ffn_norm_w': ffn_norm_w,
            'router_group_w': router_group_w, 'router_group_b': router_group_b,
            'router_expert_w': router_expert_w, 'router_expert_b': router_expert_b,
            'w_gate': w_gate, 'w_up': w_up, 'w_down': w_down, 'final_norm_w': final_norm_w}

def reference(x, mem, a_norm_w, a_in_w, a_conv_w, a_conv_b, a_dt_bias, a_a_log, a_d_skip,
              a_gnorm_w, a_out_w, kv_norm_w, w_kv, b_norm_w, b_in_w, b_sinks, b_out_w,
              mem_norm_w, mem_w_kv, ffn_norm_w, router_group_w, router_group_b,
              router_expert_w, router_expert_b, w_gate, w_up, w_down, final_norm_w):
    positions = jnp.arange(x.shape[1], dtype=jnp.int32)
    h = x
    k_sh = v_sh = None
    for layer in range(DEPTH):
        if layer < N_A_LAYERS:
            i = layer
            h = h + ssd_memory_mixer(h, mem, a_norm_w[i], a_in_w[i], a_conv_w[i], a_conv_b[i],
                                     a_dt_bias[i], a_a_log[i], a_d_skip[i], a_gnorm_w[i], a_out_w[i],
                                     mem_norm_w[layer], mem_w_kv[layer])
        else:
            j = layer - N_A_LAYERS
            if j == 0:
                k_sh, v_sh = shared_kv(h, kv_norm_w, w_kv, positions)
            h = h + swa_memory_mixer(h, k_sh, v_sh, mem, positions, b_norm_w[j], b_in_w[j],
                                     b_sinks[j], b_out_w[j], mem_norm_w[layer], mem_w_kv[layer])
        h = h + hierarchical_moe(h, ffn_norm_w[layer], router_group_w[layer], router_group_b[layer],
                                 router_expert_w[layer], router_expert_b[layer],
                                 w_gate[layer], w_up[layer], w_down[layer])
    return rms_norm(h, final_norm_w)


_drawn_inputs = setup_inputs


def setup_inputs(seed=0):
    import zlib

    import numpy as np

    out = dict(_drawn_inputs(seed))
    spreads = {}
    factors = {'kv_norm_w': 4.029,
     'b_norm_w': 8.0,
     'b_sinks': 38.834,
     'mem_norm_w': 4.036,
     'router_group_b': 4.23,
     'router_expert_b': 2.948,
     'final_norm_w': 9.728}
    for name, (base, spread) in spreads.items():
        noise = np.random.default_rng([zlib.crc32(name.encode()), seed]).standard_normal(out[name].shape)
        drawn = base * np.exp(spread * noise) if base else spread * noise
        out[name] = jnp.asarray(drawn.astype(out[name].dtype))
    for name, factor in factors.items():
        out[name] = (out[name] * factor).astype(out[name].dtype)
    return out
```

```python
from contextlib import ExitStack

import numpy as np

import concourse.bass as bass
from concourse import mybir

F32 = mybir.dt.float32
I32 = mybir.dt.int32
ALU = mybir.AluOpType
ACT = mybir.ActivationFunctionType
X = mybir.AxisListType.X

P = 128
D = 1024
KD = D // P
SEQ = 256
NT = SEQ // P
EPS = 1e-6
SSD_HEADS, SSD_GROUPS, HP = 24, 4, 64
HG = SSD_HEADS // SSD_GROUPS
INNER = SSD_HEADS * HP
GW = INNER // SSD_GROUPS
CONV_CH = INNER + 2 * SSD_GROUPS * P
NCONV = CONV_CH // P
MEM_HEADS = 4
MEM_SCALE = float(P) ** -0.5
Q_HEADS, KV_HEADS, HD, HALF_ROT = 16, 4, 64, 8
ATT_SCALE = float(HD) ** -0.5
NG, EG = 4, 8
NE = NG * EG
DE = D // 2
NEG = -1e30
SLOTS = 6
WT = 4096
TOKS = 64
ROUNDS = SEQ // TOKS
NBANK = 8

FIELDS = [("ident", P), ("tri", P), ("ones", P), ("iota", ROUNDS * TOKS), ("band_prev", P), ("band_cur", P),
          ("index8", EG), ("cos", NT * 16), ("sin", NT * 16),
          ("a_norm", KD), ("mem_norm0", KD), ("mem_norm1", KD), ("kv_norm", KD), ("b_norm", KD),
          ("ffn_norm0", KD), ("ffn_norm1", KD), ("conv_w", NCONV * 4), ("conv_b", NCONV), ("gnorm", INNER // P),
          ("dt_bias", SSD_HEADS), ("a_log", SSD_HEADS), ("d_skip", SSD_HEADS), ("sinks", Q_HEADS),
          ("route_b0", NG + NE), ("route_b1", NG + NE), ("route_w0", KD * (NG + NE)), ("route_w1", KD * (NG + NE)),
          ("dt_w", KD * SSD_HEADS)]
AT = {}
_n = 0
for _f, _w in FIELDS:
    AT[_f] = (_n, _w)
    _n += _w
SMALL = _n

TILES_A, TILES_B, TILES_MOE = 15, 9, 3 * NE
MOE0 = TILES_A
B0 = MOE0 + TILES_MOE
MOE1 = B0 + TILES_B
ALL_TILES = MOE1 + TILES_MOE


def cut(ap, **sizes):
    (name, size), = sizes.items()
    return ap.rearrange(f"p ({name} z) -> p {name} z", **{name: size})


def spread_last(ap, n):
    return ap.rearrange("p (a o) -> p a o", o=1).broadcast_to([ap.shape[0], ap.shape[1], n])


def spread_mid(ap, n):
    return ap.rearrange("p (o a) -> p o a", o=1).broadcast_to([ap.shape[0], n, ap.shape[1]])


class Core:

    def __init__(self, nc, ins, out, ctx):
        self.nc, self.ins, self.out, self.ctx = nc, ins, out, ctx
        self.ring = self.sb("ring", SLOTS * WT)
        self.small = self.sb("small", SMALL)
        self.h = self.sb("h", NT * D)
        self.xs = self.sb("xs", NT * D)
        self.norm_ss = self.sb("norm_ss", 8)
        self.norm_r = self.sb("norm_r", 8)
        self.pos = self.sb("pos", NT * (NE + 2))
        self.gates = self.sb("gates", NT * (NE + 2))
        self.most = ctx.enter_context(nc.sbuf_tensor("most", [P, 1], I32))
        self.banks = [ctx.enter_context(nc.psum_tensor(f"bank{i}", [P, 512], F32)) for i in range(NBANK)]
        self.units_done = self.sem("units_done")
        self.w_loaded = [self.sem(f"w_loaded{i}") for i in range(SLOTS)]
        self.first_unit = 0
        self.of_stage = {}

    def sb(self, name, n, ctx=None):
        return (ctx or self.ctx).enter_context(self.nc.sbuf_tensor(name, [P, n], F32))

    def sem(self, name):
        return self.ctx.enter_context(self.nc.semaphore(name))

    def sems(self, stage, names):
        for n in names.split():
            if (stage, n) not in self.of_stage:
                self.of_stage[stage, n] = self.sem(f"{stage}_{n}")
        return {n: self.of_stage[stage, n] for n in names.split()}

    def clear(self, eng, *stages):
        for (stage, _), sem in self.of_stage.items():
            if stage in stages:
                eng.sem_clear(sem)

    def f(self, name, a=0, b=None):
        at, w = AT[name]
        return self.small[:, at + a:at + (w if b is None else b)]

    def slot(self, n):
        s = n % SLOTS
        return self.ring[:, s * WT:(s + 1) * WT]

    def cols_tile(self, n):
        return cut(self.slot(n), k=KD)

    def rows_tile(self, n):
        return cut(self.slot(n), j=4)

    def wait_tile(self, eng, n):
        eng.wait_ge(self.w_loaded[n % SLOTS], 16 * (n // SLOTS + 1))

    def source(self, n):
        def cols(w, i):
            return w.rearrange("(p k) c -> p k c", k=KD)[:, :, 512 * i:512 * i + 512]

        def rows(w, i):
            return w[512 * i:512 * i + 512, :].rearrange("(j p) c -> p j c", p=P)

        g = self.ins
        if n < MOE0:
            in_w, mem_kv, out_w = g["a_in_w"][0], g["mem_w_kv"][0], g["a_out_w"][0]
            at_q = INNER + CONV_CH + SSD_HEADS
            if n < 5:
                return cols(in_w[:, INNER:], n)
            if n < 8:
                return cols(in_w, n - 5)
            if n == 8:
                return cols(in_w[:, at_q:at_q + 512], 0)
            if n < 11:
                return cols(mem_kv, n - 9)
            return rows(out_w, n - 11)
        n -= B0
        in_w, mem_kv, out_w = g["b_in_w"][0], g["mem_w_kv"][1], g["b_out_w"][0]
        if n == 0:
            return cols(g["w_kv"], 0)
        if n < 4:
            return cols(in_w, n - 1)
        if n < 6:
            return cols(mem_kv, n - 4)
        return rows(out_w, n - 6)

    def load_mixer_tile(self, sp, n):
        src = self.source(n)
        dst = self.rows_tile(n) if src.shape[1] == 4 else self.cols_tile(n)
        sp.dma_start(dst, src).then_inc(self.w_loaded[n % SLOTS], 16)

    def expert(self, layer, e):
        def one(w, k):
            return w[layer, bass.ds(e, 1)].rearrange("o (p k) c -> (o p) (k c)", k=k)

        g = self.ins
        down = g["w_down"][layer, bass.ds(e, 1)].rearrange("o (j p) c -> (o p) j c", p=P)
        return one(g["w_gate"], KD), one(g["w_up"], KD), down

    def load_expert(self, sp, layer, e, first, loaded, wait_gate_up=None, wait_down=None):
        gate, up, down = self.expert(layer, e)
        s = first % SLOTS
        if wait_gate_up:
            sp.wait_ge(*wait_gate_up)
        sp.dma_start(self.slot(s), gate).then_inc(loaded[s], 16)
        sp.dma_start(self.slot(s + 1), up).then_inc(loaded[s + 1], 16)
        if wait_down:
            sp.wait_ge(*wait_down)
        sp.dma_start(self.rows_tile(s + 2), down).then_inc(loaded[s + 2], 16)


class Units:

    def __init__(self, core, order, freed):
        self.core, self.order, self.first = core, order, core.first_unit
        self.at = {key: self.first + i for i, key in enumerate(order)}
        self.freed = freed
        assert len(self.at) == len(order)
        core.first_unit += len(order)

    def bank(self, key):
        return self.core.banks[self.at[key] % NBANK]

    def wait_free(self, pe, key):
        before = self.at[key] - NBANK - self.first
        if before >= 0:
            pe.wait_ge(*self.freed(*self.order[before]))

    def wait_done(self, eng, key):
        eng.wait_ge(self.core.units_done, self.at[key] + 1)


def transposes(c, pe, out, blocks, last_inc=True):
    for i, block in enumerate(blocks):
        ins = pe.transpose(out[:, i * P:(i + 1) * P], block, c.f("ident"))
    if last_inc:
        ins.then_inc(c.units_done, 1)


def attend_scores(c, pe, out, qT, kT, h):
    for t in range(NT):
        ins = pe.matmul(out[:, t * 256:(t + 1) * 256], cut(qT, h=4)[:, h, t * P:(t + 1) * P], cut(kT, h=4)[:, h, :],
                        start=True, stop=True)
    ins.then_inc(c.units_done, 1)


def attend_values(c, pe, out, v, pT, h):
    for m in range(2):
        ins = pe.matmul(out[:, 0:256], cut(v, m=2)[:, m, h * P:(h + 1) * P], cut(pT, m=2)[:, m, :],
                        start=(m == 0), stop=(m == 1))
    ins.then_inc(c.units_done, 1)


def project(c, pe, out, lhsT, rhs, n=KD):
    for k in range(n):
        ins = pe.matmul(out, lhsT(k), rhs(k), start=(k == 0), stop=(k == n - 1))
    ins.then_inc(c.units_done, 1)


def norm_squares(c, act, src, at, signal):
    for t in range(NT):
        act.activation(cut(c.xs, t=NT)[:, t, :], cut(src, t=NT)[:, t, :], ACT.Square,
                       accum_out=c.norm_ss[:, at + t:at + t + 1]).then_inc(signal, 1)


def norm_scaled(c, dve, src, at, signal, base):
    v = cut(src, t=NT)
    o = cut(c.xs, t=NT)
    for t in range(NT):
        dve.tensor_scalar(o[:, t, :].rearrange("q (k p) -> q p k", k=KD), v[:, t, :].rearrange("q (p k) -> q p k", k=KD),
                          c.norm_r[:, at + t:at + t + 1], None, ALU.mult).then_inc(signal, 1)


def norm_T_units(c, pe, out, i):
    xs = c.xs[:, :].rearrange("q (t k p) -> q t k p", t=NT, k=KD)
    transposes(c, pe, out, [xs[:, t, 2 * i + kk, :] for kk in range(2) for t in range(NT)])



class Router:

    UNITS = [("x2T", i) for i in range(4)] + [("router", 0), ("places", 0)]
    SEMS = "h_new n2_act n2_dve x2T_ev rt_dve rt_act"
    GROUP_LOGITS, TOP_TWO, MASK, PLACES = 3, 22, 31, 39

    def __init__(self, c, U, s, layer, xnT, work):
        self.c, self.U, self.s, self.layer, self.xnT = c, U, s, layer, xnT
        w = [NT * (NG + NE), NT * NG, NT * NE, NT * NG] + [NT * EG] * 5 + [16 * NT, NT * NE, 1]
        (self.lg, self.ge, self.sel, self.g1, self.ig, self.ig2, self.eq, self.o1, self.o2, self.col, self.mask,
         self.mf) = (work[:, sum(w[:i]):sum(w[:i + 1])] for i in range(len(w)))

    @staticmethod
    def freed(s, kind, i):
        return {"x2T": (s["x2T_ev"], 2 * i + 2), "router": (s["rt_dve"], 1), "places": (s["rt_dve"], Router.PLACES)}[kind]

    def act(self, act):
        c, U, s = self.c, self.U, self.s
        act.wait_ge(s["h_new"], 4)
        norm_squares(c, act, c.h, 4, s["n2_act"])
        act.wait_ge(s["n2_dve"], 1)
        act.activation(c.norm_r[:, 4:6], c.norm_ss[:, 4:6], ACT.Sqrt).then_inc(s["n2_act"], 1)
        for i in range(4):
            U.wait_done(act, ("x2T", i))
            for kk in range(2):
                k = 2 * i + kk
                act.activation(cut(self.xnT, k=KD)[:, k, :], U.bank(("x2T", i))[:, kk * 256:(kk + 1) * 256], ACT.Copy,
                               scale=c.f(f"ffn_norm{self.layer}", k, k + 1)).then_inc(s["x2T_ev"], 1)
        act.wait_ge(s["rt_dve"], self.GROUP_LOGITS)
        act.activation(self.ge[:, :], self.ge[:, :], ACT.Exp).then_inc(s["rt_act"], 1)
        act.wait_ge(s["rt_dve"], self.TOP_TWO)
        act.activation(self.col[:, 16:18], self.col[:, 14:16], ACT.Exp).then_inc(s["rt_act"], 1)

    def pe(self, pe, key):
        c, U, s = self.c, self.U, self.s
        kind, i = key
        out = U.bank(key)
        if kind == "x2T":
            pe.wait_ge(s["n2_dve"], 4)
            norm_T_units(c, pe, out, i)
        elif kind == "router":
            pe.wait_ge(s["x2T_ev"], 8)
            w = NG + NE
            for t in range(NT):
                for k in range(KD):
                    ins = pe.matmul(out[:, t * w:(t + 1) * w], cut(self.xnT, k=KD)[:, k, t * P:(t + 1) * P],
                                    cut(c.f(f"route_w{self.layer}"), k=KD)[:, k, :], start=(k == 0), stop=(k == KD - 1))
            ins.then_inc(c.units_done, 1)
        else:
            pe.wait_ge(s["rt_dve"], self.MASK)
            m = cut(self.mask, t=NT)
            pe.matmul(out[:, 0:NE], c.f("tri"), m[:, 0, :], start=True, stop=True)
            pe.matmul(out[:, NE:2 * NE], c.f("ones"), m[:, 0, :], start=True, stop=False)
            pe.matmul(out[:, NE:2 * NE], c.f("tri"), m[:, 1, :], start=False, stop=True)
            pe.matmul(out[:, 2 * NE:3 * NE], c.f("ones"), m[:, 0, :], start=True, stop=False)
            pe.matmul(out[:, 2 * NE:3 * NE], c.f("ones"), m[:, 1, :], start=False, stop=True).then_inc(c.units_done, 1)

    def dve(self, dve):
        c, U, s = self.c, self.U, self.s
        n = [0]

        def step(ins):
            n[0] += 1
            ins.then_inc(s["rt_dve"], 1)
            dve.wait_ge(s["rt_dve"], n[0])

        dve.wait_ge(s["n2_act"], 2)
        dve.tensor_scalar(c.norm_ss[:, 4:6], c.norm_ss[:, 4:6], 1.0 / D, EPS, ALU.mult, ALU.add).then_inc(s["n2_dve"], 1)
        dve.wait_ge(s["n2_act"], 3)
        dve.reciprocal(c.norm_r[:, 4:6], c.norm_r[:, 4:6]).then_inc(s["n2_dve"], 1)
        dve.wait_ge(s["n2_dve"], 2)
        norm_scaled(c, dve, c.h, 4, s["n2_dve"], 2)

        col = self.col
        gm, gi, m1, m2, i1, i2, gs, dd, ed, w1, w2 = (col[:, 2 * i:2 * i + 2] for i in range(11))
        lg, ge, g1, ig, ig2, eq, o1, o2 = (cut(v, t=NT) for v in (self.lg, self.ge, self.g1, self.ig, self.ig2, self.eq,
                                                                  self.o1, self.o2))
        sel, mask, gates, pos = cut(self.sel, t=NT), cut(self.mask, t=NT), cut(c.gates, t=NT), cut(c.pos, t=NT)
        index4, index8 = spread_mid(c.f("index8", 0, NG), NT), spread_mid(c.f("index8"), NT)
        key = ("router", 0)
        U.wait_done(dve, key)
        step(dve.tensor_tensor(lg, cut(U.bank(key)[:, 0:NT * (NG + NE)], t=NT), spread_mid(c.f(f"route_b{self.layer}"), NT), ALU.add))
        step(dve.tensor_reduce(gm, lg[:, :, 0:NG], X, ALU.max))
        step(dve.tensor_tensor(ge, lg[:, :, 0:NG], spread_last(gm, NG), ALU.subtract))
        assert n[0] == self.GROUP_LOGITS
        step(dve.tensor_tensor(g1, lg[:, :, 0:NG], spread_last(gm, NG), ALU.is_ge))
        step(dve.tensor_tensor(g1, g1, index4, ALU.mult))
        step(dve.tensor_reduce(gi, g1, X, ALU.min))
        step(dve.tensor_tensor(g1, index4, spread_last(gi, NG), ALU.is_equal))
        for t in range(NT):
            step(dve.tensor_tensor(cut(sel[:, t, :], g=NG), cut(lg[:, t, NG:], g=NG), spread_last(g1[:, t, :], EG), ALU.mult))
        step(dve.tensor_reduce(ig, self.sel[:, :].rearrange("p (t g e) -> p t e g", t=NT, g=NG), X, ALU.add))
        for m, i_, o, src in ((m1, i1, o1, ig), (m2, i2, o2, ig2)):
            step(dve.tensor_reduce(m, src, X, ALU.max))
            step(dve.tensor_tensor(eq, src, spread_last(m, EG), ALU.is_ge))
            step(dve.tensor_tensor(eq, eq, index8, ALU.mult))
            step(dve.tensor_reduce(i_, eq, X, ALU.min))
            step(dve.tensor_tensor(o, index8, spread_last(i_, EG), ALU.is_equal))
            if src is ig:
                step(dve.scalar_tensor_tensor(out=self.ig2[:, :], in0=self.o1[:, :], scalar=NEG, in1=self.ig[:, :],
                                              op0=ALU.mult, op1=ALU.add))
        step(dve.tensor_tensor(dd, m2, m1, ALU.subtract))
        assert n[0] == self.TOP_TWO
        dve.wait_ge(s["rt_act"], 1)
        step(dve.tensor_reduce(gs, ge, X, ALU.add))
        step(dve.reciprocal(gs, gs))
        dve.wait_ge(s["rt_act"], 2)
        step(dve.tensor_scalar(w2, ed, 1.0, None, ALU.add))
        step(dve.reciprocal(w1, w2))
        step(dve.tensor_tensor(w1, w1, gs, ALU.mult))
        step(dve.tensor_tensor(w2, w1, ed, ALU.mult))
        step(dve.tensor_tensor(eq, o1, o2, ALU.add))
        for t in range(NT):
            step(dve.tensor_tensor(cut(mask[:, t, :], g=NG), spread_last(g1[:, t, :], EG), spread_mid(eq[:, t, :], NG), ALU.mult))
        assert n[0] == self.MASK
        step(dve.tensor_tensor(o1, o1, spread_last(w1, EG), ALU.mult))
        step(dve.tensor_tensor(o2, o2, spread_last(w2, EG), ALU.mult))
        step(dve.tensor_tensor(ig, o1, o2, ALU.add))
        for t in range(NT):
            step(dve.tensor_tensor(cut(gates[:, t, 0:NE], g=NG), spread_last(g1[:, t, :], EG), spread_mid(ig[:, t, :], NG), ALU.mult))
        key = ("places", 0)
        U.wait_done(dve, key)
        step(dve.tensor_tensor(pos[:, :, 0:NE], cut(U.bank(key)[:, 0:NT * NE], t=NT), mask, ALU.mult))
        step(dve.tensor_scalar(pos[:, :, 0:NE], pos[:, :, 0:NE], -1.0, None, ALU.add))
        step(dve.tensor_reduce(self.mf[:, :], U.bank(key)[:, 2 * NE:3 * NE], X, ALU.max))
        assert n[0] == self.PLACES
        step(dve.tensor_copy(c.most[:, :], self.mf[:, :]))


def mixer_a(c):
    ctx = ExitStack()
    g = c.ins
    names = ("ld x_act x_dve xT_ev dt_dve dt_act conv_dve conv_act z_ev q_ev m_act m_dve memT_ev mk_ev mv_ev xtok_ev bt_ev "
             "ac_dve ac_act cb_dve seg_dve exp_act m_dve2 pool_x st_ev y_dve sm_dve sm_act pt_ev pv_ev g_act g_dve yT_ev "
             "out_tile " + Router.SEMS)
    s = c.sems("mixer", names)
    ld_x, ld_mem, ld_small = c.sem("a_ld_x"), c.sem("a_ld_mem"), c.sem("a_ld_small")
    with ctx:
        sb = lambda name, n: c.sb("a_" + name, n, ctx)
        xbcT = sb("xbcT", NCONV * SEQ)
        zs, xtok = sb("zs", NT * INNER), sb("xtok", NT * INNER)
        xnT, memnT = sb("xnT", KD * SEQ), sb("memnT", KD * SEQ)
        mem = memnT
        mkT, mv, qT = sb("mkT", 1024), sb("mv", 1024), sb("qT", 1024)
        sq = [mkT[:, 0:GW], mkT[:, GW:2 * GW]]
        mT = qT
        bt = sb("bt", 512)
        acc = sb("acc", 3 * SEQ)
        E = [c.xs[:, GW * i:GW * i + GW] for i in range(4)]
        yt = c.xs[:, 4 * GW:5 * GW]
        cbm = [sb(f"cbm{i}", P) for i in range(2)]
        xdt, xd = ([sb(f"{n}{i}", GW) for i in range(2)] for n in ("xdt", "xd"))
        xw = [acc[:, i * GW:(i + 1) * GW] for i in range(2)]
        state, ex, pTs = xbcT[:, 0:4 * GW], xbcT[:, 4 * GW:4 * GW + 512], xbcT[:, 4 * GW + 512:4 * GW + 1024]
        yT = xbcT[:, 0:12 * SEQ]
        dtb = [sb(f"dt{i}", 2 * SSD_HEADS) for i in range(6)]
        dtx, t_, s_, s2, dt, adt = dtb
        ea, eac, toend, acum = sb("ea", 24), sb("eac", 24), sb("toend", 24), sb("acum", 48)
        smc = sb("smc", 64)
        gss = sb("gss", 8)

        steps = [(ch, gr) for ch in range(NT) for gr in range(SSD_GROUPS)]
        order = [("xT", i) for i in range(4)] + [("dt", 0)]
        order += [("conv", j) for j in range(NCONV)]
        order += [("xtok", i) for i in range(6)] + [("bt", 0), ("ac", 0)]
        order += [("z", i) for i in range(6)]
        order += [("q", h) for h in range(4)] + [("memT", i) for i in range(4)]
        order += [("mk", h) for h in range(4)] + [("mv", m) for m in range(2)]
        for i in range(len(steps) + 1):
            if i < 8:
                order += [("cb", i), ("A", 2 * i), ("A", 2 * i + 1)]
            if 2 <= i <= 5:
                order += [("pv", i - 2)]
            if 1 <= i <= 4:
                order += [("pT", i - 1)]
            if i < 4:
                order += [("sc", i)]
            if i >= 1:
                order += [("st", i - 1)] if i <= 4 else [("yo", i - 5)]
                order += [("yd", i - 1)]
        order += [("yT", i) for i in range(6)] + [("out", i) for i in range(4)] + Router.UNITS

        def freed(kind, i):
            if kind in ("x2T", "router", "places"):
                return Router.freed(s, kind, i)
            return {"xT": (s["xT_ev"], 2 * i + 2), "dt": (s["dt_dve"], 1), "conv": (s["conv_dve"], 4 * i + 4),
                    "xtok": (s["xtok_ev"], i + 1), "bt": (s["bt_ev"], 1), "ac": (s["ac_dve"], 2), "z": (s["z_ev"], i + 1),
                    "q": (s["q_ev"], i + 1), "memT": (s["memT_ev"], 2 * i + 2), "mk": (s["mk_ev"], i + 1),
                    "mv": (s["mv_ev"], i + 1), "cb": (s["cb_dve"], i + 1), "A": (s["seg_dve"], 3 * i + 3),
                    "sc": (s["sm_act"], 2 * i + 2), "pT": (s["pt_ev"], i + 1), "pv": (s["pv_ev"], i + 1),
                    "st": (s["st_ev"], i + 1), "yo": (s["y_dve"], 8 + 4 * i + 1),
                    "yd": (s["y_dve"], 2 * i + 1 if i < 4 else 8 + 4 * (i - 4) + 2),
                    "yT": (s["yT_ev"], 2 * i + 2), "out": (s["h_new"], i + 1)}[kind]

        U = Units(c, order, freed)
        R = Router(c, U, s, 0, xnT, memnT)

        def tile_used(n):
            if n < 5:
                return c.units_done, U.at["conv", 4 * n + 3] + 1
            if n < 8:
                return c.units_done, U.at["z", 2 * (n - 5) + 1] + 1
            last = {8: ("q", 3), 9: ("mk", 3), 10: ("mv", 1)}
            if n in last:
                return c.units_done, U.at[last[n]] + 1
            if n < 14:
                return s["out_tile"], n - 10
            return c.units_done, U.at["out", 3] + 1

        def heads(ap, n=HG):
            return cut(ap, h=n)

        block = ctx.enter_context(c.nc.Block())

        @block.sync
        def _(sp):
            for t in range(NT):
                sp.dma_start(cut(c.h, t=NT)[:, t, :], g["x"][0, t * P:(t + 1) * P, :]).then_inc(ld_x, 16)
            sp.dma_start(c.small[:, :], g["small"]).then_inc(ld_small, 16)
            for n in range(2):
                c.load_mixer_tile(sp, n)
            for t in range(NT):
                sp.dma_start(cut(mem, t=NT)[:, t, :], g["mem"][0, t * P:(t + 1) * P, :]).then_inc(ld_mem, 16)
            for n in range(2, TILES_A + SLOTS):
                if n >= SLOTS:
                    sp.wait_ge(*tile_used(n - SLOTS))
                if n < TILES_A:
                    c.load_mixer_tile(sp, n)
                elif (n - TILES_A) % 3 == 0:
                    gate = c.expert(0, (n - TILES_A) // 3)[0]
                    sp.dma_start(c.slot(n), gate).then_inc(c.w_loaded[n % SLOTS], 16)
                elif (n - TILES_A) % 3 == 1:
                    up = c.expert(0, (n - TILES_A) // 3)[1]
                    sp.dma_start(c.slot(n), up).then_inc(c.w_loaded[n % SLOTS], 16)
                else:
                    down = c.expert(0, (n - TILES_A) // 3)[2]
                    sp.dma_start(c.rows_tile(n), down).then_inc(c.w_loaded[n % SLOTS], 16)

        @block.scalar
        def _(act):
            act.wait_ge(ld_x, 32)
            norm_squares(c, act, c.h, 0, s["x_act"])
            act.wait_ge(s["x_dve"], 1)
            act.activation(c.norm_r[:, 0:2], c.norm_ss[:, 0:2], ACT.Sqrt).then_inc(s["x_act"], 1)
            for key in order:
                kind, i = key
                if kind in ("out", "x2T", "router", "places"):
                    continue
                bank = U.bank(key)
                if kind in ("xT", "memT"):
                    if key == ("memT", 0):
                        act.wait_ge(ld_small, 16)
                    U.wait_done(act, key)
                    if kind == "xT" and i == 0:
                        act.wait_ge(ld_small, 16)
                    if kind == "memT" and i == 0:
                        act.wait_ge(s["m_dve"], 4)
                    dst, w = (xnT, "a_norm") if kind == "xT" else (memnT, "mem_norm0")
                    for kk in range(2):
                        k = 2 * i + kk
                        act.activation(cut(dst, k=KD)[:, k, :], bank[:, kk * 256:(kk + 1) * 256], ACT.Copy,
                                       scale=c.f(w, k, k + 1)).then_inc(s[kind + "_ev"], 1)
                elif kind == "dt":
                    act.wait_ge(s["dt_dve"], 2)
                    act.activation(t_[:, :], t_[:, :], ACT.Exp, scale=-1.0).then_inc(s["dt_act"], 1)
                    act.activation(ea[:, :], c.f("a_log"), ACT.Exp).then_inc(s["dt_act"], 1)
                elif kind == "conv":
                    act.wait_ge(s["conv_dve"], 4 * i + 4)
                    act.activation(cut(xbcT, j=NCONV)[:, i, :], cut(acc, b=3)[:, i % 3, :], ACT.Silu).then_inc(s["conv_act"], 1)
                elif kind == "z":
                    U.wait_done(act, key)
                    act.activation(cut(zs, t=NT)[:, i % 2, 512 * (i // 2):512 * (i // 2) + 512], bank[:, :], ACT.Silu).then_inc(s["z_ev"], 1)
                elif kind == "xtok":
                    U.wait_done(act, key)
                    act.activation(cut(xtok, t=NT)[:, i // 3, 512 * (i % 3):512 * (i % 3) + 512], bank[:, :], ACT.Copy).then_inc(s["xtok_ev"], 1)
                elif kind == "bt":
                    U.wait_done(act, key)
                    act.activation(bt[:, :], bank[:, :], ACT.Copy).then_inc(s["bt_ev"], 1)
                elif kind == "ac":
                    act.wait_ge(s["ac_dve"], 2)
                    act.activation(eac[:, :], acum[:, 24:48], ACT.Exp).then_inc(s["ac_act"], 1)
                    act.activation(toend[:, :], toend[:, :], ACT.Exp).then_inc(s["ac_act"], 1)
                elif kind == "q":
                    U.wait_done(act, key)
                    act.activation(cut(qT, h=4)[:, i, :], bank[:, 0:256], ACT.Copy).then_inc(s["q_ev"], 1)
                elif kind == "mk":
                    U.wait_done(act, key)
                    act.activation(cut(mkT, h=4)[:, i, :], bank[:, 0:256], ACT.Copy).then_inc(s["mk_ev"], 1)
                elif kind == "mv":
                    U.wait_done(act, key)
                    act.activation(cut(mv, m=2)[:, i, :], bank[:, :], ACT.Copy).then_inc(s["mv_ev"], 1)
                elif kind == "A":
                    act.wait_ge(s["seg_dve"], 3 * i + 3)
                    act.activation(E[i % 4][:, :], E[i % 4][:, :], ACT.Exp).then_inc(s["exp_act"], 1)
                elif kind == "st":
                    U.wait_done(act, key)
                    act.activation(cut(state, g=4)[:, i, :], bank[:, 0:GW], ACT.Copy).then_inc(s["st_ev"], 1)
                elif kind == "sc":
                    U.wait_done(act, key)
                    act.wait_ge(s["sm_dve"], 4 * i + 2)
                    for t in range(NT):
                        act.activation(cut(ex, t=NT)[:, t, :], cut(bank, t=NT)[:, t, :], ACT.Exp, scale=MEM_SCALE,
                                       bias=smc[:, 16 + 2 * i + t:17 + 2 * i + t],
                                       accum_out=smc[:, 32 + 2 * i + t:33 + 2 * i + t]).then_inc(s["sm_act"], 1)
                elif kind == "pT":
                    U.wait_done(act, key)
                    act.activation(pTs, bank[:, :], ACT.Copy).then_inc(s["pt_ev"], 1)
                elif kind == "pv":
                    U.wait_done(act, key)
                    act.activation(cut(mT, h=4)[:, i, :], bank[:, 0:256], ACT.Copy).then_inc(s["pv_ev"], 1)
                elif kind == "yT":
                    if i == 0:
                        for st in range(8):
                            act.wait_ge(s["y_dve"], 2 * st + 2 if st < 4 else 8 + 4 * (st - 4) + 4)
                            if st >= 2:
                                act.wait_ge(s["g_act"], st - 1)
                            act.activation(sq[st % 2], cut(zs, t=NT)[:, st // 4, GW * (st % 4):GW * (st % 4) + GW], ACT.Square,
                                           accum_out=gss[:, st:st + 1]).then_inc(s["g_act"], 1)
                        act.wait_ge(s["g_dve"], 1)
                        act.activation(gss[:, :], gss[:, :], ACT.Sqrt).then_inc(s["g_act"], 1)
                    U.wait_done(act, key)
                    for jj in range(2):
                        j = 2 * i + jj
                        act.activation(cut(yT, j=12)[:, j, :], bank[:, jj * 256:(jj + 1) * 256], ACT.Copy,
                                       scale=c.f("gnorm", j, j + 1)).then_inc(s["yT_ev"], 1)
                if kind == "z" and i == 5:
                    act.wait_ge(ld_mem, 32)
                    act.wait_ge(c.units_done, U.at["xT", 3] + 1)
                    norm_squares(c, act, mem, 2, s["m_act"])
                    act.wait_ge(s["m_dve"], 1)
                    act.activation(c.norm_r[:, 2:4], c.norm_ss[:, 2:4], ACT.Sqrt).then_inc(s["m_act"], 1)
            R.act(act)

        @block.gpsimd
        def _(pool):
            n = [0]

            def step(ins):
                n[0] += 1
                ins.then_inc(s["pool_x"], 1)

            pool.wait_ge(s["dt_dve"], 17)
            pool.wait_ge(s["ac_act"], 2)
            pool.wait_ge(ld_small, 16)
            pool.wait_ge(s["conv_act"], NCONV)
            for st, (ch, gr) in enumerate(steps):
                pool.wait_ge(s["xtok_ev"], 3 * ch + 3)
                if st >= 2:
                    pool.wait_ge(c.units_done, U.at["yd", st - 2] + 1)
                    pool.wait_ge(s["y_dve"], 2 * (st - 2) + 1 if st - 2 < 4 else 8 + 4 * (st - 6) + 3)
                x = cut(xtok, t=NT)[:, ch, GW * gr:GW * gr + GW]
                step(pool.tensor_tensor(heads(xdt[st % 2][:, :]), heads(x),
                                        spread_last(cut(dt, t=NT)[:, ch, HG * gr:HG * gr + HG], HP), ALU.mult))
                if ch == 0:
                    pool.wait_ge(s["pool_x"], n[0])
                    step(pool.tensor_tensor(heads(xw[st % 2][:, :]), heads(xdt[st % 2][:, :]),
                                            spread_last(toend[:, HG * gr:HG * gr + HG], HP), ALU.mult))
                step(pool.tensor_tensor(heads(xd[st % 2][:, :]), heads(x),
                                        spread_last(c.f("d_skip", HG * gr, HG * gr + HG), HP), ALU.mult))

        def pool_done(st, what):
            base = 3 * st if st < 4 else 12 + 2 * (st - 4)
            return base + {"xdt": 1, "xw": 2, "xd": 3 if st < 4 else 2}[what]

        @block.tensor
        def _(pe):
            for key in order:
                kind, i = key
                out = U.bank(key)
                if kind != "out":
                    U.wait_free(pe, key)
                if kind == "xT":
                    if i == 0:
                        pe.wait_ge(ld_small, 16)
                        pe.wait_ge(s["x_dve"], 4)
                    norm_T_units(c, pe, out, i)
                elif kind == "memT":
                    if i == 0:
                        pe.wait_ge(s["m_dve"], 4)
                    norm_T_units(c, pe, out, i)
                elif kind == "dt":
                    pe.wait_ge(s["xT_ev"], 8)
                    for t in range(NT):
                        for k in range(KD):
                            ins = pe.matmul(out[:, 24 * t:24 * t + 24], cut(xnT, k=KD)[:, k, t * P:(t + 1) * P],
                                            cut(c.f("dt_w"), k=KD)[:, k, :], start=(k == 0), stop=(k == KD - 1))
                    ins.then_inc(c.units_done, 1)
                elif kind in ("conv", "q", "mk"):
                    n = {"conv": i // 4, "q": 8, "mk": 9}[kind]
                    if i % 4 == 0:
                        c.wait_tile(pe, n)
                    if kind == "mk" and i == 0:
                        pe.wait_ge(s["memT_ev"], 8)
                    w, x = c.cols_tile(n), cut(memnT if kind == "mk" else xnT, k=KD)
                    project(c, pe, out[:, 0:256], lambda k: w[:, k, P * (i % 4):P * (i % 4) + P], lambda k: x[:, k, :])
                elif kind in ("z", "mv"):
                    n = 5 + i // 2 if kind == "z" else 10
                    if i % 2 == 0:
                        c.wait_tile(pe, n)
                    w, x, t = c.cols_tile(n), cut(memnT if kind == "mv" else xnT, k=KD), i % 2
                    project(c, pe, out[:, :], lambda k: x[:, k, t * P:(t + 1) * P], lambda k: w[:, k, :])
                elif kind == "xtok":
                    ch, j = i // 3, 4 * (i % 3)
                    pe.wait_ge(s["conv_act"], j + 4)
                    transposes(c, pe, out, [cut(xbcT, j=NCONV)[:, j + q, ch * P:(ch + 1) * P] for q in range(4)])
                elif kind == "bt":
                    pe.wait_ge(s["conv_act"], NCONV)
                    transposes(c, pe, out, [cut(xbcT, j=NCONV)[:, 12 + q, 0:P] for q in range(4)])
                elif kind == "ac":
                    pe.wait_ge(s["dt_dve"], 17)
                    for ch in range(NT):
                        pe.matmul(out[:, 24 * ch:24 * ch + 24], c.f("tri"), cut(adt, t=NT)[:, ch, :], start=True, stop=True)
                    pe.matmul(out[:, 48:72], c.f("ones"), cut(adt, t=NT)[:, 0, :], start=True, stop=True).then_inc(c.units_done, 1)
                elif kind == "cb":
                    ch, gr = steps[i]
                    x = cut(xbcT, j=NCONV)
                    pe.matmul(out[:, 0:P], x[:, 12 + gr, ch * P:(ch + 1) * P], x[:, 16 + gr, ch * P:(ch + 1) * P],
                              start=True, stop=True).then_inc(c.units_done, 1)
                elif kind == "A":
                    ch, gr = steps[i // 2]
                    for hh in range(3):
                        hd = HG * gr + 3 * (i % 2) + hh
                        ins = pe.matmul(out[:, hh * P:(hh + 1) * P], cut(adt, t=NT)[:, ch, hd:hd + 1].broadcast_to([P, P]),
                                        c.f("tri"), start=True, stop=True)
                    ins.then_inc(c.units_done, 1)
                elif kind == "sc":
                    pe.wait_ge(s["q_ev"], i + 1)
                    pe.wait_ge(s["mk_ev"], i + 1)
                    attend_scores(c, pe, out, qT, mkT, i)
                elif kind == "pT":
                    pe.wait_ge(s["sm_dve"], 4 * i + 4)
                    transposes(c, pe, out, [cut(ex, t=NT)[:, t, m * P:(m + 1) * P] for m in range(2) for t in range(NT)])
                elif kind == "pv":
                    pe.wait_ge(s["pt_ev"], i + 1)
                    pe.wait_ge(s["mv_ev"], 2)
                    attend_values(c, pe, out, mv, pTs, i)
                elif kind == "st":
                    pe.wait_ge(s["bt_ev"], 1)
                    pe.wait_ge(s["pool_x"], pool_done(i, "xw"))
                    pe.matmul(out[:, 0:GW], cut(bt, g=4)[:, i, :], xw[i % 2][:, :], start=True, stop=True).then_inc(c.units_done, 1)
                elif kind == "yo":
                    pe.wait_ge(s["st_ev"], i + 1)
                    pe.matmul(out[:, 0:GW], cut(xbcT, j=NCONV)[:, 16 + i, P:2 * P], cut(state, g=4)[:, i, :],
                              start=True, stop=True).then_inc(c.units_done, 1)
                elif kind == "yd":
                    pe.wait_ge(s["m_dve2"], 2 * i + 2)
                    pe.wait_ge(s["pool_x"], pool_done(i, "xdt"))
                    for hd in range(HG):
                        ins = pe.matmul(out[:, hd * HP:(hd + 1) * HP], cut(E[(2 * i + hd // 3) % 4], h=3)[:, hd % 3, :],
                                        xdt[i % 2][:, hd * HP:(hd + 1) * HP], start=True, stop=True)
                    ins.then_inc(c.units_done, 1)
                elif kind == "yT":
                    pe.wait_ge(s["g_dve"], 10)
                    transposes(c, pe, out, [cut(zs, t=NT)[:, ch, (2 * i + jj) * P:(2 * i + jj + 1) * P]
                                            for jj in range(2) for ch in range(NT)])
                elif kind == "out":
                    if i:
                        continue
                    for q in range(4):
                        U.wait_free(pe, ("out", q))
                    pe.wait_ge(s["yT_ev"], 12)
                    pe.wait_ge(s["pv_ev"], 4)
                    for n in range(4):
                        c.wait_tile(pe, 11 + n)
                        for j in range(4):
                            jj = 4 * n + j
                            src = cut(yT, j=12)[:, jj, :] if jj < 12 else cut(mT, h=4)[:, jj - 12, :]
                            for q in range(4):
                                t, half = q // 2, q % 2
                                ins = pe.matmul(U.bank(("out", q))[:, :], src[:, t * P:(t + 1) * P],
                                                c.rows_tile(11 + n)[:, j, 512 * half:512 * half + 512],
                                                start=(jj == 0), stop=(jj == 15))
                                if jj == 15:
                                    ins.then_inc(c.units_done, 1)
                        if n < 3:
                            ins.then_inc(s["out_tile"], 1)
                else:
                    R.pe(pe, key)

        @block.vector
        def _(dve):
            def chain(signal, start=0):
                n = [start]

                def step(ins):
                    n[0] += 1
                    ins.then_inc(signal, 1)
                    dve.wait_ge(signal, n[0])
                return step

            dve.memset(c.pos[:, :], -1.0)
            dve.memset(c.gates[:, :], 0.0)
            dve.wait_ge(s["x_act"], 2)
            dve.tensor_scalar(c.norm_ss[:, 0:2], c.norm_ss[:, 0:2], 1.0 / D, EPS, ALU.mult, ALU.add).then_inc(s["x_dve"], 1)
            dve.wait_ge(s["x_act"], 3)
            dve.reciprocal(c.norm_r[:, 0:2], c.norm_r[:, 0:2]).then_inc(s["x_dve"], 1)
            dve.wait_ge(s["x_dve"], 2)
            norm_scaled(c, dve, c.h, 0, s["x_dve"], 2)
            y_step = chain(s["y_dve"])

            def decay_scores(i):
                dve.wait_ge(s["exp_act"], i + 1)
                dve.tensor_tensor(cut(E[i % 4], h=3), cut(E[i % 4], h=3), spread_mid(cbm[(i // 2) % 2][:, :], 3),
                                  ALU.mult).then_inc(s["m_dve2"], 1)

            for key in order:
                kind, i = key
                bank = U.bank(key)
                if kind == "dt":
                    step = chain(s["dt_dve"])
                    U.wait_done(dve, key)
                    dve.wait_ge(ld_small, 16)
                    step(dve.tensor_tensor(cut(dtx, t=NT), cut(bank[:, 0:48], t=NT), spread_mid(c.f("dt_bias"), NT), ALU.add))
                    step(dve.scalar_tensor_tensor(out=t_[:, :], in0=dtx[:, :], scalar=-1.0, in1=dtx[:, :], op0=ALU.mult, op1=ALU.max))
                    dve.wait_ge(s["dt_act"], 2)
                    step(dve.tensor_scalar(s_[:, :], t_[:, :], 2.0, None, ALU.add))
                    step(dve.reciprocal(s_[:, :], s_[:, :]))
                    step(dve.tensor_tensor(s_[:, :], s_[:, :], t_[:, :], ALU.mult))
                    step(dve.tensor_tensor(s2[:, :], s_[:, :], s_[:, :], ALU.mult))
                    step(dve.tensor_scalar(t_[:, :], s2[:, :], 1.0 / 15, None, ALU.mult))
                    for q in (13, 11, 9, 7, 5, 3):
                        step(dve.scalar_tensor_tensor(out=t_[:, :], in0=t_[:, :], scalar=1.0 / q, in1=s2[:, :], op0=ALU.add, op1=ALU.mult))
                    step(dve.scalar_tensor_tensor(out=t_[:, :], in0=t_[:, :], scalar=1.0, in1=s_[:, :], op0=ALU.add, op1=ALU.mult))
                    step(dve.tensor_scalar(dt[:, :], dtx[:, :], 0.0, None, ALU.max))
                    step(dve.scalar_tensor_tensor(out=dt[:, :], in0=t_[:, :], scalar=2.0, in1=dt[:, :], op0=ALU.mult, op1=ALU.add))
                    step(dve.scalar_tensor_tensor(out=cut(adt, t=NT), in0=cut(dt, t=NT), scalar=-1.0, in1=spread_mid(ea[:, :], NT),
                                                  op0=ALU.mult, op1=ALU.mult))
                elif kind == "conv":
                    step = chain(s["conv_dve"], 4 * i)
                    U.wait_done(dve, key)
                    if i >= 3:
                        dve.wait_ge(s["conv_act"], i - 2)
                    a = cut(acc, b=3)[:, i % 3, :]
                    step(dve.tensor_scalar(a, bank[:, 0:SEQ], c.f("conv_w", 4 * i + 3, 4 * i + 4), c.f("conv_b", i, i + 1), ALU.mult, ALU.add))
                    for back in (1, 2, 3):
                        step(dve.scalar_tensor_tensor(out=a[:, back:], in0=bank[:, 0:SEQ - back], scalar=c.f("conv_w", 4 * i + 3 - back, 4 * i + 4 - back),
                                                      in1=a[:, back:], op0=ALU.mult, op1=ALU.add))
                elif kind == "ac":
                    U.wait_done(dve, key)
                    step = chain(s["ac_dve"])
                    step(dve.tensor_copy(acum[:, :], bank[:, 0:48]))
                    step(dve.tensor_tensor(toend[:, :], bank[:, 48:72], acum[:, 0:24], ALU.subtract))
                elif kind == "z" and i == 5:
                    dve.wait_ge(s["m_act"], 2)
                    dve.tensor_scalar(c.norm_ss[:, 2:4], c.norm_ss[:, 2:4], 1.0 / D, EPS, ALU.mult, ALU.add).then_inc(s["m_dve"], 1)
                    dve.wait_ge(s["m_act"], 3)
                    dve.reciprocal(c.norm_r[:, 2:4], c.norm_r[:, 2:4]).then_inc(s["m_dve"], 1)
                    dve.wait_ge(s["m_dve"], 2)
                    norm_scaled(c, dve, mem, 2, s["m_dve"], 2)
                elif kind == "cb":
                    U.wait_done(dve, key)
                    dve.tensor_tensor(cbm[i % 2][:, :], bank[:, 0:P], c.f("tri"), ALU.mult).then_inc(s["cb_dve"], 1)
                elif kind == "A":
                    ch, gr = steps[i // 2]
                    U.wait_done(dve, key)
                    if i >= 4:
                        dve.wait_ge(c.units_done, U.at["yd", (i - 4) // 2] + 1)
                    for hh in range(3):
                        hd = 24 * ch + HG * gr + 3 * (i % 2) + hh
                        dve.tensor_scalar(cut(E[i % 4], h=3)[:, hh, :], cut(bank[:, 0:GW], h=3)[:, hh, :], acum[:, hd:hd + 1], 0.0,
                                          ALU.subtract, ALU.min).then_inc(s["seg_dve"], 1)
                    if i == 0:
                        dve.wait_ge(s["cb_dve"], 1)
                    else:
                        dve.wait_ge(s["cb_dve"], (i - 1) // 2 + 1)
                        decay_scores(i - 1)
                    if i == 15:
                        decay_scores(15)
                elif kind == "sc":
                    U.wait_done(dve, key)
                    step = chain(s["sm_dve"], 4 * i)
                    if i:
                        dve.wait_ge(c.units_done, U.at["pT", i - 1] + 1)
                    step(dve.tensor_reduce(smc[:, 2 * i:2 * i + 2], cut(bank, t=NT), X, ALU.max))
                    step(dve.tensor_scalar(smc[:, 16 + 2 * i:18 + 2 * i], smc[:, 2 * i:2 * i + 2], -MEM_SCALE, None, ALU.mult))
                elif kind == "pT":
                    step = chain(s["sm_dve"], 4 * i + 2)
                    dve.wait_ge(s["sm_act"], 2 * i + 2)
                    step(dve.reciprocal(smc[:, 48 + 2 * i:50 + 2 * i], smc[:, 32 + 2 * i:34 + 2 * i]))
                    step(dve.tensor_tensor(cut(ex, t=NT), cut(ex, t=NT), spread_last(smc[:, 48 + 2 * i:50 + 2 * i], 256), ALU.mult))
                elif kind == "yd":
                    ch, gr = steps[i]
                    z = cut(zs, t=NT)[:, ch, GW * gr:GW * gr + GW]
                    if ch:
                        yo = ("yo", gr)
                        U.wait_done(dve, yo)
                        y_step(dve.tensor_tensor(heads(yt[:, :]), heads(U.bank(yo)[:, 0:GW]), spread_last(eac[:, HG * gr:HG * gr + HG], HP), ALU.mult))
                    U.wait_done(dve, key)
                    dve.wait_ge(s["pool_x"], pool_done(i, "xd"))
                    if ch:
                        y_step(dve.tensor_tensor(yt[:, :], bank[:, 0:GW], yt[:, :], ALU.add))
                        y_step(dve.tensor_tensor(yt[:, :], xd[i % 2][:, :], yt[:, :], ALU.add))
                    else:
                        dve.wait_ge(s["z_ev"], 6)
                        y_step(dve.tensor_tensor(yt[:, :], bank[:, 0:GW], xd[i % 2][:, :], ALU.add))
                    y_step(dve.tensor_tensor(z, z, yt[:, :], ALU.mult))
                elif kind == "yT" and i == 0:
                    step = chain(s["g_dve"])
                    dve.wait_ge(s["g_act"], 8)
                    step(dve.tensor_scalar(gss[:, :], gss[:, :], 1.0 / GW, EPS, ALU.mult, ALU.add))
                    dve.wait_ge(s["g_act"], 9)
                    step(dve.reciprocal(gss[:, :], gss[:, :]))
                    for st, (ch, gr) in enumerate(steps):
                        z = cut(zs, t=NT)[:, ch, GW * gr:GW * gr + GW]
                        dve.tensor_scalar(z, z, gss[:, st:st + 1], None, ALU.mult).then_inc(s["g_dve"], 1)
                elif kind == "out":
                    U.wait_done(dve, key)
                    hv = cut(c.h, t=NT)[:, i // 2, 512 * (i % 2):512 * (i % 2) + 512]
                    dve.tensor_tensor(hv, hv, bank[:, :], ALU.add).then_inc(s["h_new"], 1)
            R.dve(dve)


class Experts:

    SEMS = "zeroed pick picked_T gathered xg_ready gu_done silu_done hid_ready turned turned_ready down_done y_ready scattered"
    HALF = NE // 2

    def __init__(self, c, layer, ctx):
        self.c, self.layer = c, layer
        self.first = MOE1 if layer else MOE0
        sb = lambda name, n: c.sb(f"e{layer}_{name}", n, ctx)
        self.pick = [sb(f"pick{i}", NT * TOKS) for i in range(2)]
        self.gated = sb("gated", NT * 2 * TOKS)
        self.xg = [sb(f"xg{i}", KD * TOKS) for i in range(2)]
        self.silu = sb("silu", 256)
        self.hid = sb("hid", 256)
        self.turned = [sb(f"turned{i}", 512) for i in range(2)]
        self.y = [sb(f"y{i}", 512) for i in range(2)]
        self.sums, (self.b_gu, self.b_gather, self.b_turn, self.b_down) = c.banks[0:4], c.banks[4:8]

    def scatter(self, pe, b):
        for t in range(NT):
            for half in range(2):
                r = slice(half * TOKS, (half + 1) * TOKS)
                ins = pe.matmul(self.sums[2 * t + half][:, :], self.turned[b][r, 256 + t * P:256 + (t + 1) * P], self.y[b][r, :],
                                start=False, stop=False, skip_group_check=True)
        return ins

    def rounds(self, eng, sets, body):
        body(0, None)
        most = eng.value_load(self.c.most[0:1, 0:1], min_val=0, max_val=SEQ)
        for rnd in range(1, ROUNDS):
            with eng.If(most > rnd * TOKS):
                body(rnd, sets[rnd - 1])
        eng.nop()

    def block(self):
        c, layer = self.c, self.layer
        xs = c.xs[:, :].rearrange("q (t k p) -> q t k p", t=NT, k=KD)
        slot = lambda b, j: (self.first + 3 * b + j) % SLOTS
        sets = [(c.sems("moe", self.SEMS), c.w_loaded, lambda b, j: (self.first + 3 * b + j) // SLOTS + 1)]
        for r in range(1, ROUNDS):
            loaded = c.sems(f"round{r}", " ".join(f"loaded{i}" for i in range(SLOTS)))
            sets.append((c.sems(f"round{r}", self.SEMS), [loaded[f"loaded{i}"] for i in range(SLOTS)], lambda b, j: 1))
        with c.nc.Block() as block:

            @block.sync
            def _(sp):
                def body(rnd, prev):
                    s, loaded, _ = sets[rnd]
                    if rnd:
                        sp.wait_ge(prev[0]["gu_done"], NE)
                        sp.wait_ge(prev[0]["down_done"], NE)
                        for b in range(2):
                            c.load_expert(sp, layer, b, slot(b, 0), loaded)
                    with sp.Fori(0, self.HALF - 1) as i:
                        for b in range(2):
                            c.load_expert(sp, layer, i * 2 + (b + 2), slot(b, 0), loaded,
                                          (s["gu_done"], i * 2 + (b + 1)), (s["down_done"], i * 2 + (b + 1)))
                    if rnd:
                        sp.wait_ge(s["gu_done"], NE)
                        sp.wait_ge(s["down_done"], NE)

                self.rounds(sp, sets, body)
                if layer == 0:
                    s = sets[0][0]
                    for b in range(2):
                        for j in range(3):
                            sp.wait_ge(s["down_done" if j == 2 else "gu_done"], NE - 1 + b)
                            c.load_mixer_tile(sp, B0 + 3 * b + j)

            @block.vector
            def _(dve):
                def body(rnd, prev):
                    s = sets[rnd][0]
                    iota = c.f("iota", rnd * TOKS, (rnd + 1) * TOKS)

                    def pick(b, e):
                        for t in range(NT):
                            ins = dve.tensor_scalar(cut(self.pick[b], t=NT)[:, t, :], iota, c.pos[:, bass.ds(e + t * (NE + 2), 1)], None, ALU.is_equal)
                            ins.then_inc(s["pick"], 1)

                    def weighed(e):
                        g = self.gated[:, :].rearrange("p (t d j) -> p t d j", t=NT, d=2)
                        for t in range(NT):
                            dve.tensor_scalar(g[:, t, :, :], spread_mid(iota, 2), c.pos[:, bass.ds(e + t * (NE + 2), 1)],
                                              c.gates[:, bass.ds(e + t * (NE + 2), 1)], ALU.is_equal, ALU.mult).then_inc(s["picked_T"], 1)

                    def gathered(b):
                        dve.tensor_tensor(cut(self.xg[b], k=KD), cut(self.b_gather, k=KD), spread_last(c.f(f"ffn_norm{layer}"), TOKS),
                                          ALU.mult).then_inc(s["xg_ready"], 1)

                    if prev:
                        dve.wait_ge(prev[0]["scattered"], NE + 1)
                        dve.wait_ge(prev[0]["gathered"], NE + 1)
                        dve.wait_ge(prev[0]["gu_done"], NE)
                    dve.memset(self.y[1][:, :], 0.0).then_inc(s["zeroed"], 1)
                    dve.memset(self.turned[1][:, :], 0.0).then_inc(s["zeroed"], 1)
                    pick(0, 0)
                    dve.wait_ge(s["gathered"], 1)
                    gathered(0)
                    with dve.Fori(0, self.HALF) as i:
                        for b in range(2):
                            e = i * 2 + b
                            dve.wait_ge(s["gathered"], e + 1)
                            pick(1 - b, e + 1)
                            dve.wait_ge(s["turned"], e)
                            weighed(e)
                            dve.wait_ge(s["silu_done"], e + 1)
                            dve.tensor_tensor(self.hid[:, :], self.silu[:, :], self.b_gu[:, 256:512], ALU.mult).then_inc(s["hid_ready"], 1)
                            dve.wait_ge(s["gathered"], e + 2)
                            gathered(1 - b)
                            dve.wait_ge(s["down_done"], e + 1)
                            dve.wait_ge(s["scattered"], e)
                            dve.tensor_copy(self.y[b][:, :], self.b_down[:, :]).then_inc(s["y_ready"], 1)
                    dve.wait_ge(s["scattered"], NE + 1)

                self.rounds(dve, sets, body)
                for q in range(4):
                    dve.tensor_copy(c.h[:, 512 * q:512 * q + 512], self.sums[q][:, :])

            @block.scalar
            def _(act):
                def body(rnd, prev):
                    s = sets[rnd][0]
                    act.wait_ge(s["zeroed"], 2)
                    if prev:
                        act.wait_ge(prev[0]["hid_ready"], NE)
                    with act.Fori(0, self.HALF) as i:
                        for b in range(2):
                            e = i * 2 + b
                            act.wait_ge(s["gu_done"], e + 1)
                            act.wait_ge(s["hid_ready"], e)
                            act.activation(self.silu[:, :], self.b_gu[:, 0:256], ACT.Silu).then_inc(s["silu_done"], 1)
                            act.wait_ge(s["turned"], e + 1)
                            act.wait_ge(s["scattered"], e)
                            act.activation(self.turned[b][:, :], self.b_turn[:, :], ACT.Copy).then_inc(s["turned_ready"], 1)

                self.rounds(act, sets, body)

            @block.tensor
            def _(pe):
                def body(rnd, prev):
                    s, loaded, landed = sets[rnd]

                    def gather(b):
                        for k in range(KD):
                            for t in range(NT):
                                ins = pe.matmul(self.b_gather[:, k * TOKS:(k + 1) * TOKS], xs[:, t, k, :], cut(self.pick[b], t=NT)[:, t, :],
                                                start=(t == 0), stop=(t == NT - 1))
                        ins.then_inc(s["gathered"], 1)

                    if prev:
                        pe.wait_ge(prev[0]["xg_ready"], NE + 1)
                    else:
                        for q in range(4):
                            pe.matmul(self.sums[q][:, :], c.f("ident"), c.h[:, 512 * q:512 * q + 512], start=True, stop=False, skip_group_check=True)
                    pe.wait_ge(s["pick"], 2)
                    gather(0)
                    pe.wait_ge(s["zeroed"], 2)
                    with pe.Fori(0, self.HALF) as i:
                        for b in range(2):
                            e = i * 2 + b
                            gate_up = self.c.ring[:, slot(b, 0) * WT:(slot(b, 0) + 2) * WT].rearrange("p (w k f) -> p w k f", w=2, k=KD)
                            pe.wait_ge(s["xg_ready"], e + 1)
                            pe.wait_ge(s["hid_ready"], e)
                            for j in range(2):
                                pe.wait_ge(loaded[slot(b, j)], i * 16 + 16 * landed(b, j))
                            for k in range(KD):
                                for half in range(2):
                                    ins = pe.matmul(self.b_gu[half * TOKS:(half + 1) * TOKS, :], cut(self.xg[b], k=KD)[:, k, :],
                                                    gate_up[:, :, k, 256 * half:256 * half + 256], start=(k == 0), stop=(k == KD - 1))
                            ins.then_inc(s["gu_done"], 1)
                            pe.wait_ge(s["pick"], i * 4 + (2 * b + 4))
                            gather(1 - b)
                            pe.wait_ge(s["picked_T"], i * 4 + (2 * b + 2))
                            pe.wait_ge(s["turned_ready"], e)
                            for t in range(NT):
                                pe.transpose(self.b_turn[:, 256 + t * P:256 + (t + 1) * P], cut(self.gated, t=NT)[:, t, :], c.f("ident"))
                            pe.wait_ge(s["hid_ready"], e + 1)
                            for j in range(2):
                                ins = pe.transpose(self.b_turn[:, j * P:(j + 1) * P], self.hid[:, j * P:(j + 1) * P], c.f("ident"))
                            ins.then_inc(s["turned"], 1)
                            pe.wait_ge(s["y_ready"], e)
                            self.scatter(pe, 1 - b).then_inc(s["scattered"], 1)
                            pe.wait_ge(s["turned_ready"], e + 1)
                            pe.wait_ge(loaded[slot(b, 2)], i * 16 + 16 * landed(b, 2))
                            down = c.rows_tile(slot(b, 2))
                            for j in range(4):
                                at = (j % 2) * P + (j // 2) * TOKS
                                for half in range(2):
                                    ins = pe.matmul(self.b_down[half * TOKS:(half + 1) * TOKS, :], self.turned[b][:, at:at + TOKS],
                                                    down[:, j, 512 * half:512 * half + 512], start=(j == 0), stop=(j == 3))
                            ins.then_inc(s["down_done"], 1)
                    pe.wait_ge(s["y_ready"], NE)
                    self.scatter(pe, 1).then_inc(s["scattered"], 1)

                self.rounds(pe, sets, body)

            if layer == 0:
                @block.gpsimd
                def _(pool):
                    c.clear(pool, "mixer")


def moe(c, layer):
    with ExitStack() as ctx:
        Experts(c, layer, ctx).block()


def mixer_b(c):
    g = c.ins
    names = ("x_act x_dve xT_ev xk_dve kv_ev kr_dve kT_ev q_ev qr_dve qT_ev qm_ev m_act m_dve memT_ev mk_ev mv_ev as_dve as_act "
             "an_dve aT_ev av_ev sm_dve sm_act pt_ev pv_ev out_tile " + Router.SEMS)
    s = c.sems("mixer", names)
    ld_mem = c.sem("b_ld_mem")
    with ExitStack() as ctx:
        sb = lambda name, n: c.sb("b_" + name, n, ctx)
        xnT, xkT, memnT = sb("xnT", KD * SEQ), sb("xkT", KD * SEQ), sb("memnT", KD * SEQ)
        mem = memnT
        qtok, qT = sb("qtok", NT * 1024), sb("qT", 8 * SEQ)
        attT = qtok
        kd, vt, kT = sb("kd", NT * 512), sb("vt", NT * 256), sb("kT", 4 * SEQ)
        mkT, mv, qmT = sb("mkT", 1024), sb("mv", 1024), sb("qmT", 1024)
        mT = qmT
        ex, pTs = sb("ex", 512), sb("pTs", 512)
        ee = [sb(f"ee{i}", 512) for i in range(3)]
        aTs = [sb(f"aTs{i}", 512) for i in range(2)]
        rot_c, rot_s = sb("rot_c", P), sb("rot_s", P)
        smc = sb("smc", 64)
        col = sb("col", 16 * 12)

        parts = [(t, kv, odd) for t in range(NT) for kv in range(KV_HEADS) for odd in range(2)]
        NA = len(parts)
        width = lambda n: P if parts[n][0] == 0 else 2 * P
        order = [("xT", i) for i in range(4)] + [("kv", t) for t in range(NT)] + [("q", i) for i in range(4)]
        order += [("kT", t) for t in range(NT)] + [("qT", i) for i in range(4)]
        fill = [("qm", h) for h in range(4)] + [("memT", i) for i in range(4)] + [("mk", h) for h in range(4)] + [("mv", m) for m in range(2)]
        fill += [(kind, h) for h in range(4) for kind in ("sc", "pT", "pv")]
        for n in range(NA + 2):
            if n < NA:
                order += [("as", n)]
            order += fill[2 * n:2 * n + 1]
            if 1 <= n <= NA:
                order += [("aT", n - 1)]
            order += fill[2 * n + 1:2 * n + 2]
            if n >= 2:
                order += [("av", n - 2)]
        order += [("out", i) for i in range(4)] + Router.UNITS

        def freed(kind, i):
            if kind in ("x2T", "router", "places"):
                return Router.freed(s, kind, i)
            return {"xT": (s["xk_dve"], i + 1), "kv": (s["kv_ev"], 2 * i + 2), "q": (s["q_ev"], i + 1), "kT": (s["kT_ev"], i + 1),
                    "qT": (s["qT_ev"], i + 1), "qm": (s["qm_ev"], i + 1), "memT": (s["memT_ev"], 2 * i + 2), "mk": (s["mk_ev"], i + 1),
                    "mv": (s["mv_ev"], i + 1), "as": (s["as_dve"], 5 * i + 1), "aT": (s["aT_ev"], i + 1), "av": (s["av_ev"], i + 1),
                    "sc": (s["sm_act"], 2 * i + 2), "pT": (s["pt_ev"], i + 1), "pv": (s["pv_ev"], i + 1),
                    "out": (s["h_new"], i + 1)}[kind]

        U = Units(c, order, freed)
        R = Router(c, U, s, 1, xnT, memnT)

        def tile_used(n):
            last = [("kv", 1), ("q", 1), ("q", 3), ("qm", 3), ("mk", 3), ("mv", 1)]
            if n - B0 < 6:
                return c.units_done, U.at[last[n - B0]] + 1
            if n - B0 < 8:
                return s["out_tile"], n - B0 - 5
            return c.units_done, U.at["out", 3] + 1

        def kd_heads(t, dup):
            return kd[:, :].rearrange("p (t h d c) -> p t h d c", t=NT, h=KV_HEADS, d=2)[:, t, :, dup, :]

        block = ctx.enter_context(c.nc.Block())

        @block.sync
        def _(sp):
            for t in range(NT):
                sp.dma_start(cut(mem, t=NT)[:, t, :], g["mem"][0, t * P:(t + 1) * P, :]).then_inc(ld_mem, 16)
            for n in range(B0 + SLOTS, MOE1 + SLOTS):
                sp.wait_ge(*tile_used(n - SLOTS))
                if n < MOE1:
                    c.load_mixer_tile(sp, n)
                    continue
                weights = c.expert(1, (n - MOE1) // 3)
                j = (n - MOE1) % 3
                sp.dma_start(c.rows_tile(n) if j == 2 else c.slot(n), weights[j]).then_inc(c.w_loaded[n % SLOTS], 16)

        @block.gpsimd
        def _(pool):
            c.clear(pool, "moe", *(f"round{r}" for r in range(1, ROUNDS)))

        @block.scalar
        def _(act):
            norm_squares(c, act, c.h, 0, s["x_act"])
            act.wait_ge(s["x_dve"], 1)
            act.activation(c.norm_r[:, 0:2], c.norm_ss[:, 0:2], ACT.Sqrt).then_inc(s["x_act"], 1)
            for key in order:
                kind, i = key
                if kind in ("out", "x2T", "router", "places"):
                    continue
                bank = U.bank(key)
                if kind == "qm" and i == 0:
                    act.wait_ge(ld_mem, 32)
                    act.wait_ge(c.units_done, U.at["xT", 3] + 1)
                    norm_squares(c, act, mem, 2, s["m_act"])
                    act.wait_ge(s["m_dve"], 1)
                    act.activation(c.norm_r[:, 2:4], c.norm_ss[:, 2:4], ACT.Sqrt).then_inc(s["m_act"], 1)
                if kind in ("xT", "memT"):
                    U.wait_done(act, key)
                    if kind == "memT" and i == 0:
                        act.wait_ge(s["m_dve"], 4)
                    dst, w = (xnT, "b_norm") if kind == "xT" else (memnT, "mem_norm1")
                    for kk in range(2):
                        k = 2 * i + kk
                        act.activation(cut(dst, k=KD)[:, k, :], bank[:, kk * 256:(kk + 1) * 256], ACT.Copy,
                                       scale=c.f(w, k, k + 1)).then_inc(s[kind + "_ev"], 1)
                elif kind == "as":
                    act.wait_ge(s["as_dve"], 5 * i + 5)
                    w = width(i)
                    k = 12 * i
                    for q in range(2):
                        act.activation(ee[i % 3][:, q * w:(q + 1) * w], ee[i % 3][:, q * w:(q + 1) * w], ACT.Exp,
                                       bias=col[:, k + 2 + q:k + 3 + q], accum_out=col[:, k + 4 + q:k + 5 + q]).then_inc(s["as_act"], 1)
                    act.activation(col[:, k + 6:k + 8], col[:, k + 6:k + 8], ACT.Exp).then_inc(s["as_act"], 1)
                elif kind == "sc":
                    U.wait_done(act, key)
                    act.wait_ge(s["sm_dve"], 4 * i + 2)
                    for t in range(NT):
                        act.activation(cut(ex, t=NT)[:, t, :], cut(bank, t=NT)[:, t, :], ACT.Exp, scale=MEM_SCALE,
                                       bias=smc[:, 16 + 2 * i + t:17 + 2 * i + t],
                                       accum_out=smc[:, 32 + 2 * i + t:33 + 2 * i + t]).then_inc(s["sm_act"], 1)
                else:
                    U.wait_done(act, key)
                    if kind == "kv":
                        act.activation(cut(vt, t=NT)[:, i, :], bank[:, 256:512], ACT.Copy).then_inc(s["kv_ev"], 1)
                        act.activation(kd_heads(i, 0), cut(bank[:, 0:256], h=4), ACT.Copy).then_inc(s["kv_ev"], 1)
                    elif kind == "q":
                        act.activation(cut(qtok, t=NT)[:, i % 2, 512 * (i // 2):512 * (i // 2) + 512], bank[:, :], ACT.Copy).then_inc(s["q_ev"], 1)
                    elif kind == "kT":
                        act.activation(cut(kT, g=4)[:, :, i * P:(i + 1) * P], cut(bank, g=4), ACT.Copy).then_inc(s["kT_ev"], 1)
                    elif kind == "qT":
                        act.activation(cut(qT, g=8)[:, 4 * (i // 2):4 * (i // 2) + 4, (i % 2) * P:(i % 2) * P + P], cut(bank, g=4),
                                       ACT.Copy).then_inc(s["qT_ev"], 1)
                    elif kind == "qm":
                        act.activation(cut(qmT, h=4)[:, i, :], bank[:, 0:256], ACT.Copy).then_inc(s["qm_ev"], 1)
                    elif kind == "mk":
                        act.activation(cut(mkT, h=4)[:, i, :], bank[:, 0:256], ACT.Copy).then_inc(s["mk_ev"], 1)
                    elif kind == "mv":
                        act.activation(cut(mv, m=2)[:, i, :], bank[:, :], ACT.Copy).then_inc(s["mv_ev"], 1)
                    elif kind == "aT":
                        if i >= 2:
                            act.wait_ge(c.units_done, U.at["av", i - 2] + 1)
                        act.activation(aTs[i % 2][:, 0:2 * width(i)], bank[:, 0:2 * width(i)], ACT.Copy).then_inc(s["aT_ev"], 1)
                    elif kind == "av":
                        t, kv, odd = parts[i]
                        r = slice(64 * odd, 64 * odd + 64)
                        act.activation(cut(attT, j=8)[r, 2 * kv:2 * kv + 2, t * P:(t + 1) * P], cut(bank[r, 0:256], j=2),
                                       ACT.Copy).then_inc(s["av_ev"], 1)
                    elif kind == "pT":
                        act.activation(pTs[:, :], bank[:, :], ACT.Copy).then_inc(s["pt_ev"], 1)
                    elif kind == "pv":
                        act.activation(cut(mT, h=4)[:, i, :], bank[:, 0:256], ACT.Copy).then_inc(s["pv_ev"], 1)
            R.act(act)

        @block.tensor
        def _(pe):
            for key in order:
                kind, i = key
                out = U.bank(key)
                if kind != "out":
                    U.wait_free(pe, key)
                if kind in ("xT", "memT"):
                    if i == 0:
                        pe.wait_ge(s["x_dve" if kind == "xT" else "m_dve"], 4)
                    norm_T_units(c, pe, out, i)
                elif kind in ("kv", "q", "mv"):
                    n = B0 + {"kv": 0, "q": 1 + i // 2, "mv": 5}[kind]
                    t = i % 2
                    if t == 0:
                        c.wait_tile(pe, n)
                    if key == ("kv", 0):
                        pe.wait_ge(s["xk_dve"], 4)
                    w, x = c.cols_tile(n), cut({"kv": xkT, "q": xnT, "mv": memnT}[kind], k=KD)
                    project(c, pe, out[:, :], lambda k: x[:, k, t * P:(t + 1) * P], lambda k: w[:, k, :])
                elif kind in ("qm", "mk"):
                    n = B0 + (3 if kind == "qm" else 4)
                    if i == 0:
                        c.wait_tile(pe, n)
                        if kind == "mk":
                            pe.wait_ge(s["memT_ev"], 8)
                    w, x = c.cols_tile(n), cut(memnT if kind == "mk" else xnT, k=KD)
                    project(c, pe, out[:, 0:256], lambda k: w[:, k, P * i:P * i + P], lambda k: x[:, k, :])
                elif kind == "kT":
                    pe.wait_ge(s["kr_dve"], 5 * i + 5)
                    transposes(c, pe, out, [kd[:, 512 * i + P * q:512 * i + P * q + P] for q in range(4)])
                elif kind == "qT":
                    pe.wait_ge(s["qr_dve"], 4 * i + 4)
                    at = 1024 * (i % 2) + 512 * (i // 2)
                    transposes(c, pe, out, [qtok[:, at + P * q:at + P * q + P] for q in range(4)])
                elif kind == "as":
                    t, kv, odd = parts[i]
                    r, w = slice(64 * odd, 64 * odd + 64), width(i)
                    pe.wait_ge(s["qT_ev"], 4)
                    pe.wait_ge(s["kT_ev"], 2)
                    for q in range(2):
                        ins = pe.matmul(out[:, q * w:(q + 1) * w], cut(qT, g=8)[r, 2 * kv + q, t * P:(t + 1) * P], cut(kT, g=4)[r, kv, 0:w],
                                        start=True, stop=True)
                    ins.then_inc(c.units_done, 1)
                elif kind == "aT":
                    pe.wait_ge(s["an_dve"], 3 * i + 3)
                    transposes(c, pe, out, [ee[i % 3][:, q * P:(q + 1) * P] for q in range(2 * width(i) // P)])
                elif kind == "av":
                    t, kv, odd = parts[i]
                    r, nb = slice(64 * odd, 64 * odd + 64), width(i) // P
                    pe.wait_ge(s["aT_ev"], i + 1)
                    for q in range(2):
                        for m in range(nb):
                            ins = pe.matmul(out[r, q * P:(q + 1) * P], cut(vt, t=NT)[:, m, 64 * kv:64 * kv + 64],
                                            aTs[i % 2][:, (q * nb + m) * P:(q * nb + m + 1) * P], start=(m == 0), stop=(m == nb - 1))
                    ins.then_inc(c.units_done, 1)
                elif kind == "sc":
                    pe.wait_ge(s["qm_ev"], i + 1)
                    pe.wait_ge(s["mk_ev"], i + 1)
                    attend_scores(c, pe, out, qmT, mkT, i)
                elif kind == "pT":
                    pe.wait_ge(s["sm_dve"], 4 * i + 4)
                    transposes(c, pe, out, [cut(ex, t=NT)[:, t, m * P:(m + 1) * P] for m in range(2) for t in range(NT)])
                elif kind == "pv":
                    pe.wait_ge(s["pt_ev"], i + 1)
                    pe.wait_ge(s["mv_ev"], 2)
                    attend_values(c, pe, out, mv, pTs, i)
                elif kind == "out":
                    if i:
                        continue
                    for q in range(4):
                        U.wait_free(pe, ("out", q))
                    pe.wait_ge(s["av_ev"], NA)
                    pe.wait_ge(s["pv_ev"], 4)
                    for n in range(3):
                        c.wait_tile(pe, B0 + 6 + n)
                        for j in range(4):
                            jj = 4 * n + j
                            src = cut(attT, j=8)[:, jj, :] if jj < 8 else cut(mT, h=4)[:, jj - 8, :]
                            for q in range(4):
                                t, half = q // 2, q % 2
                                ins = pe.matmul(U.bank(("out", q))[:, :], src[:, t * P:(t + 1) * P],
                                                c.rows_tile(B0 + 6 + n)[:, j, 512 * half:512 * half + 512],
                                                start=(jj == 0), stop=(jj == 11))
                                if jj == 11:
                                    ins.then_inc(c.units_done, 1)
                        if n < 2:
                            ins.then_inc(s["out_tile"], 1)
                else:
                    R.pe(pe, key)

        @block.vector
        def _(dve):
            def chain(signal, start=0):
                n = [start]

                def step(ins):
                    n[0] += 1
                    ins.then_inc(signal, 1)
                    dve.wait_ge(signal, n[0])
                return step

            def turn(step, x, t, heads):
                a, b = cut(rot_c[:, 0:16 * heads], h=heads), cut(rot_s[:, 0:16 * heads], h=heads)
                step(dve.tensor_tensor(a, x[:, :, 0:16], spread_mid(c.f("cos", 16 * t, 16 * t + 16), heads), ALU.mult))
                step(dve.tensor_tensor(b, x[:, :, 0:16], spread_mid(c.f("sin", 16 * t, 16 * t + 16), heads), ALU.mult))
                step(dve.tensor_tensor(x[:, :, 0:8], a[:, :, 0:8], b[:, :, 8:16], ALU.subtract))
                step(dve.tensor_tensor(x[:, :, 8:16], a[:, :, 8:16], b[:, :, 0:8], ALU.add))

            dve.wait_ge(s["x_act"], 2)
            dve.tensor_scalar(c.norm_ss[:, 0:2], c.norm_ss[:, 0:2], 1.0 / D, EPS, ALU.mult, ALU.add).then_inc(s["x_dve"], 1)
            dve.wait_ge(s["x_act"], 3)
            dve.reciprocal(c.norm_r[:, 0:2], c.norm_r[:, 0:2]).then_inc(s["x_dve"], 1)
            dve.wait_ge(s["x_dve"], 2)
            norm_scaled(c, dve, c.h, 0, s["x_dve"], 2)
            for key in order:
                kind, i = key
                bank = U.bank(key)
                if kind == "qm" and i == 0:
                    dve.wait_ge(s["m_act"], 2)
                    dve.tensor_scalar(c.norm_ss[:, 2:4], c.norm_ss[:, 2:4], 1.0 / D, EPS, ALU.mult, ALU.add).then_inc(s["m_dve"], 1)
                    dve.wait_ge(s["m_act"], 3)
                    dve.reciprocal(c.norm_r[:, 2:4], c.norm_r[:, 2:4]).then_inc(s["m_dve"], 1)
                    dve.wait_ge(s["m_dve"], 2)
                    norm_scaled(c, dve, mem, 2, s["m_dve"], 2)
                elif kind == "xT":
                    dve.wait_ge(s["xT_ev"], 2 * i + 2)
                    dve.tensor_tensor(cut(xkT, k=KD)[:, 2 * i:2 * i + 2, :], cut(bank, k=2), spread_last(c.f("kv_norm", 2 * i, 2 * i + 2), SEQ),
                                      ALU.mult).then_inc(s["xk_dve"], 1)
                elif kind == "kv":
                    step = chain(s["kr_dve"], 5 * i)
                    dve.wait_ge(s["kv_ev"], 2 * i + 2)
                    turn(step, kd_heads(i, 0), i, KV_HEADS)
                    step(dve.tensor_copy(kd_heads(i, 1), kd_heads(i, 0)))
                elif kind == "q":
                    dve.wait_ge(s["q_ev"], i + 1)
                    at = 1024 * (i % 2) + 512 * (i // 2)
                    turn(chain(s["qr_dve"], 4 * i), cut(qtok[:, at:at + 512], h=8), i % 2, 8)
                elif kind == "as":
                    t, kv, odd = parts[i]
                    w = width(i)
                    step = chain(s["as_dve"], 5 * i)
                    U.wait_done(dve, key)
                    if i >= 3:
                        dve.wait_ge(c.units_done, U.at["aT", i - 3] + 1)
                    mask = c.f("band_cur") if t == 0 else c.small[:, AT["band_prev"][0]:AT["band_prev"][0] + 2 * P]
                    e, k = cut(ee[i % 3][:, 0:2 * w], q=2), 12 * i
                    sinks = c.f("sinks", 4 * kv + odd, 4 * kv + odd + 3)[:, ::2]
                    step(dve.scalar_tensor_tensor(out=e, in0=cut(bank[:, 0:2 * w], q=2), scalar=ATT_SCALE, in1=spread_mid(mask, 2),
                                                  op0=ALU.mult, op1=ALU.add))
                    step(dve.tensor_reduce(col[:, k:k + 2], e, X, ALU.max))
                    step(dve.tensor_tensor(col[:, k:k + 2], col[:, k:k + 2], sinks, ALU.max))
                    step(dve.tensor_scalar(col[:, k + 2:k + 4], col[:, k:k + 2], -1.0, None, ALU.mult))
                    step(dve.tensor_tensor(col[:, k + 6:k + 8], sinks, col[:, k:k + 2], ALU.subtract))
                elif kind == "aT":
                    w, k = width(i), 12 * i
                    step = chain(s["an_dve"], 3 * i)
                    dve.wait_ge(s["as_act"], 3 * i + 3)
                    step(dve.tensor_tensor(col[:, k + 8:k + 10], col[:, k + 4:k + 6], col[:, k + 6:k + 8], ALU.add))
                    step(dve.reciprocal(col[:, k + 8:k + 10], col[:, k + 8:k + 10]))
                    e = cut(ee[i % 3][:, 0:2 * w], q=2)
                    step(dve.tensor_tensor(e, e, spread_last(col[:, k + 8:k + 10], w), ALU.mult))
                elif kind == "sc":
                    U.wait_done(dve, key)
                    step = chain(s["sm_dve"], 4 * i)
                    if i:
                        dve.wait_ge(c.units_done, U.at["pT", i - 1] + 1)
                    step(dve.tensor_reduce(smc[:, 2 * i:2 * i + 2], cut(bank, t=NT), X, ALU.max))
                    step(dve.tensor_scalar(smc[:, 16 + 2 * i:18 + 2 * i], smc[:, 2 * i:2 * i + 2], -MEM_SCALE, None, ALU.mult))
                elif kind == "pT":
                    step = chain(s["sm_dve"], 4 * i + 2)
                    dve.wait_ge(s["sm_act"], 2 * i + 2)
                    step(dve.reciprocal(smc[:, 48 + 2 * i:50 + 2 * i], smc[:, 32 + 2 * i:34 + 2 * i]))
                    step(dve.tensor_tensor(cut(ex, t=NT), cut(ex, t=NT), spread_last(smc[:, 48 + 2 * i:50 + 2 * i], 256), ALU.mult))
                elif kind == "out":
                    U.wait_done(dve, key)
                    hv = cut(c.h, t=NT)[:, i // 2, 512 * (i % 2):512 * (i % 2) + 512]
                    dve.tensor_tensor(hv, hv, bank[:, :], ALU.add).then_inc(s["h_new"], 1)
            R.dve(dve)


def final_norm(c):
    s = c.sems("f", "ld act dve")
    stored = [c.sem(f"f_stored{t}") for t in range(NT)]
    with ExitStack() as ctx:
        w = c.sb("f_w", D, ctx)
        with c.nc.Block() as block:

            @block.sync
            def _(sp):
                sp.dma_start(w[:, :], c.ins["final_norm_w"].rearrange("(o n) -> o n", o=1).broadcast_to([P, D])).then_inc(s["ld"], 16)
                for t in range(NT):
                    sp.wait_ge(s["dve"], 3 + t)
                    sp.dma_start(c.out[0, t * P:(t + 1) * P, :], cut(c.h, t=NT)[:, t, :]).then_inc(stored[t], 16)
                for t in range(NT):
                    sp.wait_ge(stored[t], 16)

            @block.scalar
            def _(act):
                norm_squares(c, act, c.h, 0, s["act"])
                act.wait_ge(s["dve"], 1)
                act.activation(c.norm_r[:, 0:2], c.norm_ss[:, 0:2], ACT.Sqrt).then_inc(s["act"], 1)

            @block.vector
            def _(dve):
                dve.wait_ge(s["act"], 2)
                dve.tensor_scalar(c.norm_ss[:, 0:2], c.norm_ss[:, 0:2], 1.0 / D, EPS, ALU.mult, ALU.add).then_inc(s["dve"], 1)
                dve.wait_ge(s["act"], 3)
                dve.reciprocal(c.norm_r[:, 0:2], c.norm_r[:, 0:2]).then_inc(s["dve"], 1)
                dve.wait_ge(s["dve"], 2)
                dve.wait_ge(s["ld"], 16)
                for t in range(NT):
                    hv = cut(c.h, t=NT)[:, t, :]
                    dve.scalar_tensor_tensor(out=hv, in0=hv, scalar=c.norm_r[:, t:t + 1], in1=w[:, :], op0=ALU.mult,
                                             op1=ALU.mult).then_inc(s["dve"], 1)


def build(nc, ins, out):
    with ExitStack() as ctx:
        c = Core(nc, ins, out, ctx)
        mixer_a(c)
        moe(c, 0)
        mixer_b(c)
        moe(c, 1)
        final_norm(c)


INPUTS = ["x", "mem", "a_in_w", "a_out_w", "w_kv", "b_in_w", "b_out_w", "mem_w_kv", "w_gate", "w_up", "w_down", "final_norm_w"]


def pack_small(v):
    a = np.zeros((P, SMALL), np.float32)

    def put(name, x):
        at, w = AT[name]
        a[:, at:at + w] = x

    def by_row(w):
        return np.asarray(w).reshape(P, -1)

    i = np.arange(P)
    put("ident", np.eye(P))
    put("tri", i[:, None] <= i[None, :])
    put("ones", 1.0)
    put("iota", np.arange(ROUNDS * TOKS)[None, :])
    put("band_prev", np.where(i[None, :] > i[:, None], 0.0, NEG))
    put("band_cur", np.where(i[None, :] <= i[:, None], 0.0, NEG))
    put("index8", np.arange(EG)[None, :] - 100.0)
    freq = np.float32(500000.0) ** (np.float32(-2.0) * np.arange(HALF_ROT, dtype=np.float32) / np.float32(2 * HALF_ROT))
    angle = np.arange(SEQ, dtype=np.float32)[:, None] * freq[None, :].astype(np.float32)
    for name, fn in (("cos", np.cos), ("sin", np.sin)):
        table = np.concatenate([fn(angle), fn(angle)], axis=1).astype(np.float32)
        put(name, table.reshape(NT, P, 16).transpose(1, 0, 2).reshape(P, NT * 16))
    put("a_norm", by_row(v["a_norm_w"][0]))
    put("kv_norm", by_row(v["kv_norm_w"]))
    put("b_norm", by_row(v["b_norm_w"][0]))
    for n in (0, 1):
        put(f"mem_norm{n}", by_row(v["mem_norm_w"][n]))
        put(f"ffn_norm{n}", by_row(v["ffn_norm_w"][n]))
        put(f"route_b{n}", np.concatenate([v["router_group_b"][n], v["router_expert_b"][n]])[None, :])
        put(f"route_w{n}", by_row(np.concatenate([v["router_group_w"][n], v["router_expert_w"][n]], axis=1)))
    put("conv_w", np.asarray(v["a_conv_w"][0]).reshape(4, NCONV, P).transpose(2, 1, 0).reshape(P, NCONV * 4))
    put("conv_b", np.asarray(v["a_conv_b"][0]).reshape(NCONV, P).T)
    put("gnorm", np.asarray(v["a_gnorm_w"][0]).reshape(INNER // P, P).T)
    put("dt_bias", np.asarray(v["a_dt_bias"][0])[None, :])
    put("a_log", np.asarray(v["a_a_log"][0])[None, :])
    put("d_skip", np.asarray(v["a_d_skip"][0])[None, :])
    put("sinks", np.asarray(v["b_sinks"][0])[None, :])
    put("dt_w", by_row(np.asarray(v["a_in_w"][0])[:, INNER + CONV_CH:INNER + CONV_CH + SSD_HEADS]))
    return a


def kernel(**inputs):
    import concourse.bacc as bacc
    from concourse.bass_utils import run_bass_kernel_spmd

    nc = bacc.Bacc("TRN2", target_bir_lowering=False, num_devices=1)
    arrays = {name: np.ascontiguousarray(inputs[name]) for name in INPUTS}
    arrays["small"] = pack_small({k: np.asarray(x) for k, x in inputs.items()})
    aps = {}
    for name, a in arrays.items():
        aps[name] = nc.dram_tensor(f"in_{name}", a.shape, mybir.dt.from_np(a.dtype), kind="ExternalInput").ap()
    out = nc.dram_tensor("out", (1, SEQ, D), F32, kind="ExternalOutput").ap()
    build(nc, aps, out)
    result = run_bass_kernel_spmd(nc, [{f"in_{name}": a for name, a in arrays.items()}], core_ids=[0])
    return result.results[0]["out"]
```

```python
from contextlib import ExitStack

import numpy as np

import concourse.bass as bass
from concourse import mybir

F32 = mybir.dt.float32
I32 = mybir.dt.int32
ALU = mybir.AluOpType
ACT = mybir.ActivationFunctionType
X = mybir.AxisListType.X

P = 128
D = 1024
KD = D // P
SEQ = 256
NT = SEQ // P
EPS = 1e-6
SSD_HEADS, SSD_GROUPS, HP = 24, 4, 64
HG = SSD_HEADS // SSD_GROUPS
INNER = SSD_HEADS * HP
GW = INNER // SSD_GROUPS
CONV_CH = INNER + 2 * SSD_GROUPS * P
NCONV = CONV_CH // P
MEM_HEADS = 4
MEM_SCALE = float(P) ** -0.5
Q_HEADS, KV_HEADS, HD, HALF_ROT = 16, 4, 64, 8
ATT_SCALE = float(HD) ** -0.5
NG, EG = 4, 8
NE = NG * EG
DE = D // 2
NEG = -1e30
SLOTS = 6
WT = 4096
TOKS = 64
ROUNDS = SEQ // TOKS
NBANK = 8

FIELDS = [("ident", P), ("tri", P), ("ones", P), ("iota", ROUNDS * TOKS), ("band_prev", P), ("band_cur", P),
          ("index8", EG), ("cos", NT * 16), ("sin", NT * 16),
          ("a_norm", KD), ("mem_norm0", KD), ("mem_norm1", KD), ("kv_norm", KD), ("b_norm", KD),
          ("ffn_norm0", KD), ("ffn_norm1", KD), ("conv_w", NCONV * 4), ("conv_b", NCONV), ("gnorm", INNER // P),
          ("dt_bias", SSD_HEADS), ("a_log", SSD_HEADS), ("d_skip", SSD_HEADS), ("sinks", Q_HEADS),
          ("route_b0", NG + NE), ("route_b1", NG + NE), ("route_w0", KD * (NG + NE)), ("route_w1", KD * (NG + NE)),
          ("dt_w", KD * SSD_HEADS)]
AT = {}
_n = 0
for _f, _w in FIELDS:
    AT[_f] = (_n, _w)
    _n += _w
SMALL = _n

TILES_A, TILES_B = 15, 9
B0 = TILES_A
FIRST_SLOT = [TILES_A % SLOTS, (TILES_A + TILES_B) % SLOTS]


def cut(ap, **sizes):
    (name, size), = sizes.items()
    return ap.rearrange(f"p ({name} z) -> p {name} z", **{name: size})


def spread_last(ap, n):
    return ap.rearrange("p (a o) -> p a o", o=1).broadcast_to([ap.shape[0], ap.shape[1], n])


def spread_mid(ap, n):
    return ap.rearrange("p (o a) -> p o a", o=1).broadcast_to([ap.shape[0], n, ap.shape[1]])


class Core:

    def __init__(self, nc, ins, out, ctx):
        self.nc, self.ins, self.out, self.ctx = nc, ins, out, ctx
        self.ring = self.sb("ring", SLOTS * WT)
        self.small = self.sb("small", SMALL)
        self.h = self.sb("h", NT * D)
        self.xs = self.sb("xs", NT * D)
        self.norm_ss = self.sb("norm_ss", 8)
        self.norm_r = self.sb("norm_r", 8)
        self.pos = self.sb("pos", NT * NE)
        self.gates = self.sb("gates", NT * NE)
        self.most = ctx.enter_context(nc.sbuf_tensor("most", [P, 1], I32))
        self.banks = [ctx.enter_context(nc.psum_tensor(f"bank{i}", [P, 512], F32)) for i in range(NBANK)]
        self.units_done = self.sem("units_done")
        self.w_loaded = [self.sem(f"w_loaded{i}") for i in range(SLOTS)]
        self.first_unit = 0
        self.of_stage = {}

    def sb(self, name, n, ctx=None):
        return (ctx or self.ctx).enter_context(self.nc.sbuf_tensor(name, [P, n], F32))

    def sem(self, name):
        return self.ctx.enter_context(self.nc.semaphore(name))

    def sems(self, stage, names):
        for n in names.split():
            if (stage, n) not in self.of_stage:
                self.of_stage[stage, n] = self.sem(f"{stage}_{n}")
        return {n: self.of_stage[stage, n] for n in names.split()}

    def clear(self, eng, *stages):
        for (stage, _), sem in self.of_stage.items():
            if stage in stages:
                eng.sem_clear(sem)

    def f(self, name, a=0, b=None):
        at, w = AT[name]
        return self.small[:, at + a:at + (w if b is None else b)]

    def slot(self, n):
        s = n % SLOTS
        return self.ring[:, s * WT:(s + 1) * WT]

    def cols_tile(self, n):
        return cut(self.slot(n), k=KD)

    def rows_tile(self, n):
        return cut(self.slot(n), j=4)

    def wait_tile(self, eng, n):
        eng.wait_ge(self.w_loaded[n % SLOTS], 16 * (n // SLOTS + 1))

    def source(self, n):
        def cols(w, i):
            return w.rearrange("(p k) c -> p k c", k=KD)[:, :, 512 * i:512 * i + 512]

        def rows(w, i):
            return w[512 * i:512 * i + 512, :].rearrange("(j p) c -> p j c", p=P)

        g = self.ins
        if n < TILES_A:
            in_w, mem_kv, out_w = g["a_in_w"][0], g["mem_w_kv"][0], g["a_out_w"][0]
            at_q = INNER + CONV_CH + SSD_HEADS
            if n < 5:
                return cols(in_w[:, INNER:], n)
            if n < 8:
                return cols(in_w, n - 5)
            if n == 8:
                return cols(in_w[:, at_q:at_q + 512], 0)
            if n < 11:
                return cols(mem_kv, n - 9)
            return rows(out_w, n - 11)
        n -= B0
        in_w, mem_kv, out_w = g["b_in_w"][0], g["mem_w_kv"][1], g["b_out_w"][0]
        if n == 0:
            return cols(g["w_kv"], 0)
        if n < 4:
            return cols(in_w, n - 1)
        if n < 6:
            return cols(mem_kv, n - 4)
        return rows(out_w, n - 6)

    def load_mixer_tile(self, sp, n):
        src = self.source(n)
        dst = self.rows_tile(n) if src.shape[1] == 4 else self.cols_tile(n)
        sp.dma_start(dst, src).then_inc(self.w_loaded[n % SLOTS], 16)


class Units:

    def __init__(self, core, order, freed):
        self.core, self.order, self.first = core, order, core.first_unit
        self.at = {key: self.first + i for i, key in enumerate(order)}
        self.freed = freed
        assert len(self.at) == len(order)
        core.first_unit += len(order)

    def bank(self, key):
        return self.core.banks[self.at[key] % NBANK]

    def wait_free(self, pe, key):
        before = self.at[key] - NBANK - self.first
        if before >= 0:
            pe.wait_ge(*self.freed(*self.order[before]))

    def wait_done(self, eng, key):
        eng.wait_ge(self.core.units_done, self.at[key] + 1)


def transposes(c, pe, out, blocks, last_inc=True):
    for i, block in enumerate(blocks):
        ins = pe.transpose(out[:, i * P:(i + 1) * P], block, c.f("ident"))
    if last_inc:
        ins.then_inc(c.units_done, 1)


def attend_scores(c, pe, out, qT, kT, h):
    for t in range(NT):
        ins = pe.matmul(out[:, t * 256:(t + 1) * 256], cut(qT, h=4)[:, h, t * P:(t + 1) * P], cut(kT, h=4)[:, h, :],
                        start=True, stop=True)
    ins.then_inc(c.units_done, 1)


def attend_values(c, pe, out, v, pT, h):
    for m in range(2):
        ins = pe.matmul(out[:, 0:256], cut(v, m=2)[:, m, h * P:(h + 1) * P], cut(pT, m=2)[:, m, :],
                        start=(m == 0), stop=(m == 1))
    ins.then_inc(c.units_done, 1)


def project(c, pe, out, lhsT, rhs, n=KD):
    for k in range(n):
        ins = pe.matmul(out, lhsT(k), rhs(k), start=(k == 0), stop=(k == n - 1))
    ins.then_inc(c.units_done, 1)


def norm_squares(c, act, src, at, signal):
    for t in range(NT):
        act.activation(cut(c.xs, t=NT)[:, t, :], cut(src, t=NT)[:, t, :], ACT.Square,
                       accum_out=c.norm_ss[:, at + t:at + t + 1]).then_inc(signal, 1)


def norm_scaled(c, dve, src, at, signal, base):
    v = cut(src, t=NT)
    o = cut(c.xs, t=NT)
    for t in range(NT):
        dve.tensor_scalar(o[:, t, :].rearrange("q (k p) -> q p k", k=KD), v[:, t, :].rearrange("q (p k) -> q p k", k=KD),
                          c.norm_r[:, at + t:at + t + 1], None, ALU.mult).then_inc(signal, 1)


def norm_T_units(c, pe, out, i):
    xs = c.xs[:, :].rearrange("q (t k p) -> q t k p", t=NT, k=KD)
    transposes(c, pe, out, [xs[:, t, 2 * i + kk, :] for kk in range(2) for t in range(NT)])



class Router:

    UNITS = [("x2T", i) for i in range(4)] + [("router", 0), ("places", 0)]
    SEMS = "h_new n2_act n2_dve x2T_ev rt_dve rt_act"
    GROUP_LOGITS, TOP_TWO, MASK, PLACES = 3, 22, 31, 39

    def __init__(self, c, U, s, layer, xnT, work):
        self.c, self.U, self.s, self.layer, self.xnT = c, U, s, layer, xnT
        w = [NT * (NG + NE), NT * NG, NT * NE, NT * NG] + [NT * EG] * 5 + [16 * NT, NT * NE, 1]
        (self.lg, self.ge, self.sel, self.g1, self.ig, self.ig2, self.eq, self.o1, self.o2, self.col, self.mask,
         self.mf) = (work[:, sum(w[:i]):sum(w[:i + 1])] for i in range(len(w)))

    @staticmethod
    def freed(s, kind, i):
        return {"x2T": (s["x2T_ev"], 2 * i + 2), "router": (s["rt_dve"], 1), "places": (s["rt_dve"], Router.PLACES)}[kind]

    def act(self, act):
        c, U, s = self.c, self.U, self.s
        act.wait_ge(s["h_new"], 4)
        norm_squares(c, act, c.h, 4, s["n2_act"])
        act.wait_ge(s["n2_dve"], 1)
        act.activation(c.norm_r[:, 4:6], c.norm_ss[:, 4:6], ACT.Sqrt).then_inc(s["n2_act"], 1)
        for i in range(4):
            U.wait_done(act, ("x2T", i))
            for kk in range(2):
                k = 2 * i + kk
                act.activation(cut(self.xnT, k=KD)[:, k, :], U.bank(("x2T", i))[:, kk * 256:(kk + 1) * 256], ACT.Copy,
                               scale=c.f(f"ffn_norm{self.layer}", k, k + 1)).then_inc(s["x2T_ev"], 1)
        act.wait_ge(s["rt_dve"], self.GROUP_LOGITS)
        act.activation(self.ge[:, :], self.ge[:, :], ACT.Exp).then_inc(s["rt_act"], 1)
        act.wait_ge(s["rt_dve"], self.TOP_TWO)
        act.activation(self.col[:, 16:18], self.col[:, 14:16], ACT.Exp).then_inc(s["rt_act"], 1)

    def pe(self, pe, key):
        c, U, s = self.c, self.U, self.s
        kind, i = key
        out = U.bank(key)
        if kind == "x2T":
            pe.wait_ge(s["n2_dve"], 4)
            norm_T_units(c, pe, out, i)
        elif kind == "router":
            pe.wait_ge(s["x2T_ev"], 8)
            w = NG + NE
            for t in range(NT):
                for k in range(KD):
                    ins = pe.matmul(out[:, t * w:(t + 1) * w], cut(self.xnT, k=KD)[:, k, t * P:(t + 1) * P],
                                    cut(c.f(f"route_w{self.layer}"), k=KD)[:, k, :], start=(k == 0), stop=(k == KD - 1))
            ins.then_inc(c.units_done, 1)
        else:
            pe.wait_ge(s["rt_dve"], self.MASK)
            m = cut(self.mask, t=NT)
            pe.matmul(out[:, 0:NE], c.f("tri"), m[:, 0, :], start=True, stop=True)
            pe.matmul(out[:, NE:2 * NE], c.f("ones"), m[:, 0, :], start=True, stop=False)
            pe.matmul(out[:, NE:2 * NE], c.f("tri"), m[:, 1, :], start=False, stop=True)
            pe.matmul(out[:, 2 * NE:3 * NE], c.f("ones"), m[:, 0, :], start=True, stop=False)
            pe.matmul(out[:, 2 * NE:3 * NE], c.f("ones"), m[:, 1, :], start=False, stop=True).then_inc(c.units_done, 1)

    def dve(self, dve):
        c, U, s = self.c, self.U, self.s
        n = [0]

        def step(ins):
            n[0] += 1
            ins.then_inc(s["rt_dve"], 1)
            dve.wait_ge(s["rt_dve"], n[0])

        dve.wait_ge(s["n2_act"], 2)
        dve.tensor_scalar(c.norm_ss[:, 4:6], c.norm_ss[:, 4:6], 1.0 / D, EPS, ALU.mult, ALU.add).then_inc(s["n2_dve"], 1)
        dve.wait_ge(s["n2_act"], 3)
        dve.reciprocal(c.norm_r[:, 4:6], c.norm_r[:, 4:6]).then_inc(s["n2_dve"], 1)
        dve.wait_ge(s["n2_dve"], 2)
        norm_scaled(c, dve, c.h, 4, s["n2_dve"], 2)

        col = self.col
        gm, gi, m1, m2, i1, i2, gs, dd, ed, w1, w2 = (col[:, 2 * i:2 * i + 2] for i in range(11))
        lg, ge, g1, ig, ig2, eq, o1, o2 = (cut(v, t=NT) for v in (self.lg, self.ge, self.g1, self.ig, self.ig2, self.eq,
                                                                  self.o1, self.o2))
        sel, mask, gates, pos = cut(self.sel, t=NT), cut(self.mask, t=NT), cut(c.gates, t=NT), cut(c.pos, t=NT)
        index4, index8 = spread_mid(c.f("index8", 0, NG), NT), spread_mid(c.f("index8"), NT)
        key = ("router", 0)
        U.wait_done(dve, key)
        step(dve.tensor_tensor(lg, cut(U.bank(key)[:, 0:NT * (NG + NE)], t=NT), spread_mid(c.f(f"route_b{self.layer}"), NT), ALU.add))
        step(dve.tensor_reduce(gm, lg[:, :, 0:NG], X, ALU.max))
        step(dve.tensor_tensor(ge, lg[:, :, 0:NG], spread_last(gm, NG), ALU.subtract))
        assert n[0] == self.GROUP_LOGITS
        step(dve.tensor_tensor(g1, lg[:, :, 0:NG], spread_last(gm, NG), ALU.is_ge))
        step(dve.tensor_tensor(g1, g1, index4, ALU.mult))
        step(dve.tensor_reduce(gi, g1, X, ALU.min))
        step(dve.tensor_tensor(g1, index4, spread_last(gi, NG), ALU.is_equal))
        for t in range(NT):
            step(dve.tensor_tensor(cut(sel[:, t, :], g=NG), cut(lg[:, t, NG:], g=NG), spread_last(g1[:, t, :], EG), ALU.mult))
        step(dve.tensor_reduce(ig, self.sel[:, :].rearrange("p (t g e) -> p t e g", t=NT, g=NG), X, ALU.add))
        for m, i_, o, src in ((m1, i1, o1, ig), (m2, i2, o2, ig2)):
            step(dve.tensor_reduce(m, src, X, ALU.max))
            step(dve.tensor_tensor(eq, src, spread_last(m, EG), ALU.is_ge))
            step(dve.tensor_tensor(eq, eq, index8, ALU.mult))
            step(dve.tensor_reduce(i_, eq, X, ALU.min))
            step(dve.tensor_tensor(o, index8, spread_last(i_, EG), ALU.is_equal))
            if src is ig:
                step(dve.scalar_tensor_tensor(out=self.ig2[:, :], in0=self.o1[:, :], scalar=NEG, in1=self.ig[:, :],
                                              op0=ALU.mult, op1=ALU.add))
        step(dve.tensor_tensor(dd, m2, m1, ALU.subtract))
        assert n[0] == self.TOP_TWO
        dve.wait_ge(s["rt_act"], 1)
        step(dve.tensor_reduce(gs, ge, X, ALU.add))
        step(dve.reciprocal(gs, gs))
        dve.wait_ge(s["rt_act"], 2)
        step(dve.tensor_scalar(w2, ed, 1.0, None, ALU.add))
        step(dve.reciprocal(w1, w2))
        step(dve.tensor_tensor(w1, w1, gs, ALU.mult))
        step(dve.tensor_tensor(w2, w1, ed, ALU.mult))
        step(dve.tensor_tensor(eq, o1, o2, ALU.add))
        for t in range(NT):
            step(dve.tensor_tensor(cut(mask[:, t, :], g=NG), spread_last(g1[:, t, :], EG), spread_mid(eq[:, t, :], NG), ALU.mult))
        assert n[0] == self.MASK
        step(dve.tensor_tensor(o1, o1, spread_last(w1, EG), ALU.mult))
        step(dve.tensor_tensor(o2, o2, spread_last(w2, EG), ALU.mult))
        step(dve.tensor_tensor(ig, o1, o2, ALU.add))
        for t in range(NT):
            step(dve.tensor_tensor(cut(gates[:, t, :], g=NG), spread_last(g1[:, t, :], EG), spread_mid(ig[:, t, :], NG), ALU.mult))
        key = ("places", 0)
        U.wait_done(dve, key)
        step(dve.tensor_tensor(pos[:, :, :], cut(U.bank(key)[:, 0:NT * NE], t=NT), mask, ALU.mult))
        step(dve.tensor_scalar(pos[:, :, :], pos[:, :, :], -1.0, None, ALU.add))
        step(dve.tensor_reduce(self.mf[:, :], U.bank(key)[:, 2 * NE:3 * NE], X, ALU.max))
        assert n[0] == self.PLACES
        step(dve.tensor_copy(c.most[:, :], self.mf[:, :]))


def mixer_a(c):
    ctx = ExitStack()
    g = c.ins
    names = ("ld x_act x_dve xT_ev dt_dve dt_act conv_dve conv_act z_ev q_ev m_act m_dve memT_ev mk_ev mv_ev xtok_ev bt_ev "
             "ac_dve ac_act cb_dve seg_dve exp_act m_dve2 pool_x st_ev y_dve sm_dve sm_act pt_ev pv_ev g_act g_dve yT_ev "
             "out_tile " + Router.SEMS)
    s = c.sems("mixer", names)
    ld_x, ld_mem, ld_small = c.sem("a_ld_x"), c.sem("a_ld_mem"), c.sem("a_ld_small")
    with ctx:
        sb = lambda name, n: c.sb("a_" + name, n, ctx)
        xbcT = sb("xbcT", NCONV * SEQ)
        zs, xtok = sb("zs", NT * INNER), sb("xtok", NT * INNER)
        xnT, memnT = sb("xnT", KD * SEQ), sb("memnT", KD * SEQ)
        mem = memnT
        mkT, mv, qT = sb("mkT", 1024), sb("mv", 1024), sb("qT", 1024)
        sq = [mkT[:, 0:GW], mkT[:, GW:2 * GW]]
        mT = qT
        bt = sb("bt", 512)
        acc = sb("acc", 3 * SEQ)
        E = [c.xs[:, GW * i:GW * i + GW] for i in range(4)]
        yt = c.xs[:, 4 * GW:5 * GW]
        cbm = [sb(f"cbm{i}", P) for i in range(2)]
        xdt, xd = ([sb(f"{n}{i}", GW) for i in range(2)] for n in ("xdt", "xd"))
        xw = [acc[:, i * GW:(i + 1) * GW] for i in range(2)]
        state, ex, pTs = xbcT[:, 0:4 * GW], xbcT[:, 4 * GW:4 * GW + 512], xbcT[:, 4 * GW + 512:4 * GW + 1024]
        yT = xbcT[:, 0:12 * SEQ]
        dtb = [sb(f"dt{i}", 2 * SSD_HEADS) for i in range(6)]
        dtx, t_, s_, s2, dt, adt = dtb
        ea, eac, toend, acum = sb("ea", 24), sb("eac", 24), sb("toend", 24), sb("acum", 48)
        smc = sb("smc", 64)
        gss = sb("gss", 8)

        steps = [(ch, gr) for ch in range(NT) for gr in range(SSD_GROUPS)]
        order = [("xT", i) for i in range(4)] + [("dt", 0)]
        order += [("conv", j) for j in range(NCONV)]
        order += [("xtok", i) for i in range(6)] + [("bt", 0), ("ac", 0)]
        order += [("z", i) for i in range(6)]
        order += [("q", h) for h in range(4)] + [("memT", i) for i in range(4)]
        order += [("mk", h) for h in range(4)] + [("mv", m) for m in range(2)]
        for i in range(len(steps) + 1):
            if i < 8:
                order += [("cb", i), ("A", 2 * i), ("A", 2 * i + 1)]
            if 2 <= i <= 5:
                order += [("pv", i - 2)]
            if 1 <= i <= 4:
                order += [("pT", i - 1)]
            if i < 4:
                order += [("sc", i)]
            if i >= 1:
                order += [("st", i - 1)] if i <= 4 else [("yo", i - 5)]
                order += [("yd", i - 1)]
        order += [("yT", i) for i in range(6)] + [("out", i) for i in range(4)] + Router.UNITS

        def freed(kind, i):
            if kind in ("x2T", "router", "places"):
                return Router.freed(s, kind, i)
            return {"xT": (s["xT_ev"], 2 * i + 2), "dt": (s["dt_dve"], 1), "conv": (s["conv_dve"], 4 * i + 4),
                    "xtok": (s["xtok_ev"], i + 1), "bt": (s["bt_ev"], 1), "ac": (s["ac_dve"], 2), "z": (s["z_ev"], i + 1),
                    "q": (s["q_ev"], i + 1), "memT": (s["memT_ev"], 2 * i + 2), "mk": (s["mk_ev"], i + 1),
                    "mv": (s["mv_ev"], i + 1), "cb": (s["cb_dve"], i + 1), "A": (s["seg_dve"], 3 * i + 3),
                    "sc": (s["sm_act"], 2 * i + 2), "pT": (s["pt_ev"], i + 1), "pv": (s["pv_ev"], i + 1),
                    "st": (s["st_ev"], i + 1), "yo": (s["y_dve"], 8 + 4 * i + 1),
                    "yd": (s["y_dve"], 2 * i + 1 if i < 4 else 8 + 4 * (i - 4) + 2),
                    "yT": (s["yT_ev"], 2 * i + 2), "out": (s["h_new"], i + 1)}[kind]

        U = Units(c, order, freed)
        R = Router(c, U, s, 0, xnT, memnT)

        def tile_used(n):
            if n < 5:
                return c.units_done, U.at["conv", 4 * n + 3] + 1
            if n < 8:
                return c.units_done, U.at["z", 2 * (n - 5) + 1] + 1
            last = {8: ("q", 3), 9: ("mk", 3), 10: ("mv", 1)}
            if n in last:
                return c.units_done, U.at[last[n]] + 1
            if n < 14:
                return s["out_tile"], n - 10
            return c.units_done, U.at["out", 3] + 1

        def heads(ap, n=HG):
            return cut(ap, h=n)

        first_pair = first_pair_loader(c, 0)
        block = ctx.enter_context(c.nc.Block())

        @block.sync
        def _(sp):
            for t in range(NT):
                sp.dma_start(cut(c.h, t=NT)[:, t, :], g["x"][0, t * P:(t + 1) * P, :]).then_inc(ld_x, 16)
            sp.dma_start(c.small[:, :], g["small"]).then_inc(ld_small, 16)
            for n in range(2):
                c.load_mixer_tile(sp, n)
            for t in range(NT):
                sp.dma_start(cut(mem, t=NT)[:, t, :], g["mem"][0, t * P:(t + 1) * P, :]).then_inc(ld_mem, 16)
            for n in range(2, TILES_A + SLOTS):
                if n >= SLOTS:
                    sp.wait_ge(*tile_used(n - SLOTS))
                if n < TILES_A:
                    c.load_mixer_tile(sp, n)
                else:
                    first_pair(sp, n - TILES_A)

        @block.scalar
        def _(act):
            act.wait_ge(ld_x, 32)
            norm_squares(c, act, c.h, 0, s["x_act"])
            act.wait_ge(s["x_dve"], 1)
            act.activation(c.norm_r[:, 0:2], c.norm_ss[:, 0:2], ACT.Sqrt).then_inc(s["x_act"], 1)
            for key in order:
                kind, i = key
                if kind in ("out", "x2T", "router", "places"):
                    continue
                bank = U.bank(key)
                if kind in ("xT", "memT"):
                    if key == ("memT", 0):
                        act.wait_ge(ld_small, 16)
                    U.wait_done(act, key)
                    if kind == "xT" and i == 0:
                        act.wait_ge(ld_small, 16)
                    if kind == "memT" and i == 0:
                        act.wait_ge(s["m_dve"], 4)
                    dst, w = (xnT, "a_norm") if kind == "xT" else (memnT, "mem_norm0")
                    for kk in range(2):
                        k = 2 * i + kk
                        act.activation(cut(dst, k=KD)[:, k, :], bank[:, kk * 256:(kk + 1) * 256], ACT.Copy,
                                       scale=c.f(w, k, k + 1)).then_inc(s[kind + "_ev"], 1)
                elif kind == "dt":
                    act.wait_ge(s["dt_dve"], 2)
                    act.activation(t_[:, :], t_[:, :], ACT.Exp, scale=-1.0).then_inc(s["dt_act"], 1)
                    act.activation(ea[:, :], c.f("a_log"), ACT.Exp).then_inc(s["dt_act"], 1)
                elif kind == "conv":
                    act.wait_ge(s["conv_dve"], 4 * i + 4)
                    act.activation(cut(xbcT, j=NCONV)[:, i, :], cut(acc, b=3)[:, i % 3, :], ACT.Silu).then_inc(s["conv_act"], 1)
                elif kind == "z":
                    U.wait_done(act, key)
                    act.activation(cut(zs, t=NT)[:, i % 2, 512 * (i // 2):512 * (i // 2) + 512], bank[:, :], ACT.Silu).then_inc(s["z_ev"], 1)
                elif kind == "xtok":
                    U.wait_done(act, key)
                    act.activation(cut(xtok, t=NT)[:, i // 3, 512 * (i % 3):512 * (i % 3) + 512], bank[:, :], ACT.Copy).then_inc(s["xtok_ev"], 1)
                elif kind == "bt":
                    U.wait_done(act, key)
                    act.activation(bt[:, :], bank[:, :], ACT.Copy).then_inc(s["bt_ev"], 1)
                elif kind == "ac":
                    act.wait_ge(s["ac_dve"], 2)
                    act.activation(eac[:, :], acum[:, 24:48], ACT.Exp).then_inc(s["ac_act"], 1)
                    act.activation(toend[:, :], toend[:, :], ACT.Exp).then_inc(s["ac_act"], 1)
                elif kind == "q":
                    U.wait_done(act, key)
                    act.activation(cut(qT, h=4)[:, i, :], bank[:, 0:256], ACT.Copy).then_inc(s["q_ev"], 1)
                elif kind == "mk":
                    U.wait_done(act, key)
                    act.activation(cut(mkT, h=4)[:, i, :], bank[:, 0:256], ACT.Copy).then_inc(s["mk_ev"], 1)
                elif kind == "mv":
                    U.wait_done(act, key)
                    act.activation(cut(mv, m=2)[:, i, :], bank[:, :], ACT.Copy).then_inc(s["mv_ev"], 1)
                elif kind == "A":
                    act.wait_ge(s["seg_dve"], 3 * i + 3)
                    act.activation(E[i % 4][:, :], E[i % 4][:, :], ACT.Exp).then_inc(s["exp_act"], 1)
                elif kind == "st":
                    U.wait_done(act, key)
                    act.activation(cut(state, g=4)[:, i, :], bank[:, 0:GW], ACT.Copy).then_inc(s["st_ev"], 1)
                elif kind == "sc":
                    U.wait_done(act, key)
                    act.wait_ge(s["sm_dve"], 4 * i + 2)
                    for t in range(NT):
                        act.activation(cut(ex, t=NT)[:, t, :], cut(bank, t=NT)[:, t, :], ACT.Exp, scale=MEM_SCALE,
                                       bias=smc[:, 16 + 2 * i + t:17 + 2 * i + t],
                                       accum_out=smc[:, 32 + 2 * i + t:33 + 2 * i + t]).then_inc(s["sm_act"], 1)
                elif kind == "pT":
                    U.wait_done(act, key)
                    act.activation(pTs, bank[:, :], ACT.Copy).then_inc(s["pt_ev"], 1)
                elif kind == "pv":
                    U.wait_done(act, key)
                    act.activation(cut(mT, h=4)[:, i, :], bank[:, 0:256], ACT.Copy).then_inc(s["pv_ev"], 1)
                elif kind == "yT":
                    if i == 0:
                        for st in range(8):
                            act.wait_ge(s["y_dve"], 2 * st + 2 if st < 4 else 8 + 4 * (st - 4) + 4)
                            if st >= 2:
                                act.wait_ge(s["g_act"], st - 1)
                            act.activation(sq[st % 2], cut(zs, t=NT)[:, st // 4, GW * (st % 4):GW * (st % 4) + GW], ACT.Square,
                                           accum_out=gss[:, st:st + 1]).then_inc(s["g_act"], 1)
                        act.wait_ge(s["g_dve"], 1)
                        act.activation(gss[:, :], gss[:, :], ACT.Sqrt).then_inc(s["g_act"], 1)
                    U.wait_done(act, key)
                    for jj in range(2):
                        j = 2 * i + jj
                        act.activation(cut(yT, j=12)[:, j, :], bank[:, jj * 256:(jj + 1) * 256], ACT.Copy,
                                       scale=c.f("gnorm", j, j + 1)).then_inc(s["yT_ev"], 1)
                if kind == "z" and i == 5:
                    act.wait_ge(ld_mem, 32)
                    act.wait_ge(c.units_done, U.at["xT", 3] + 1)
                    norm_squares(c, act, mem, 2, s["m_act"])
                    act.wait_ge(s["m_dve"], 1)
                    act.activation(c.norm_r[:, 2:4], c.norm_ss[:, 2:4], ACT.Sqrt).then_inc(s["m_act"], 1)
            R.act(act)

        @block.gpsimd
        def _(pool):
            n = [0]

            def step(ins):
                n[0] += 1
                ins.then_inc(s["pool_x"], 1)

            pool.wait_ge(s["dt_dve"], 17)
            pool.wait_ge(s["ac_act"], 2)
            pool.wait_ge(ld_small, 16)
            pool.wait_ge(s["conv_act"], NCONV)
            for st, (ch, gr) in enumerate(steps):
                pool.wait_ge(s["xtok_ev"], 3 * ch + 3)
                if st >= 2:
                    pool.wait_ge(c.units_done, U.at["yd", st - 2] + 1)
                    pool.wait_ge(s["y_dve"], 2 * (st - 2) + 1 if st - 2 < 4 else 8 + 4 * (st - 6) + 3)
                x = cut(xtok, t=NT)[:, ch, GW * gr:GW * gr + GW]
                step(pool.tensor_tensor(heads(xdt[st % 2][:, :]), heads(x),
                                        spread_last(cut(dt, t=NT)[:, ch, HG * gr:HG * gr + HG], HP), ALU.mult))
                if ch == 0:
                    pool.wait_ge(s["pool_x"], n[0])
                    step(pool.tensor_tensor(heads(xw[st % 2][:, :]), heads(xdt[st % 2][:, :]),
                                            spread_last(toend[:, HG * gr:HG * gr + HG], HP), ALU.mult))
                step(pool.tensor_tensor(heads(xd[st % 2][:, :]), heads(x),
                                        spread_last(c.f("d_skip", HG * gr, HG * gr + HG), HP), ALU.mult))

        def pool_done(st, what):
            base = 3 * st if st < 4 else 12 + 2 * (st - 4)
            return base + {"xdt": 1, "xw": 2, "xd": 3 if st < 4 else 2}[what]

        @block.tensor
        def _(pe):
            for key in order:
                kind, i = key
                out = U.bank(key)
                if kind != "out":
                    U.wait_free(pe, key)
                if kind == "xT":
                    if i == 0:
                        pe.wait_ge(ld_small, 16)
                        pe.wait_ge(s["x_dve"], 4)
                    norm_T_units(c, pe, out, i)
                elif kind == "memT":
                    if i == 0:
                        pe.wait_ge(s["m_dve"], 4)
                    norm_T_units(c, pe, out, i)
                elif kind == "dt":
                    pe.wait_ge(s["xT_ev"], 8)
                    for t in range(NT):
                        for k in range(KD):
                            ins = pe.matmul(out[:, 24 * t:24 * t + 24], cut(xnT, k=KD)[:, k, t * P:(t + 1) * P],
                                            cut(c.f("dt_w"), k=KD)[:, k, :], start=(k == 0), stop=(k == KD - 1))
                    ins.then_inc(c.units_done, 1)
                elif kind in ("conv", "q", "mk"):
                    n = {"conv": i // 4, "q": 8, "mk": 9}[kind]
                    if i % 4 == 0:
                        c.wait_tile(pe, n)
                    if kind == "mk" and i == 0:
                        pe.wait_ge(s["memT_ev"], 8)
                    w, x = c.cols_tile(n), cut(memnT if kind == "mk" else xnT, k=KD)
                    project(c, pe, out[:, 0:256], lambda k: w[:, k, P * (i % 4):P * (i % 4) + P], lambda k: x[:, k, :])
                elif kind in ("z", "mv"):
                    n = 5 + i // 2 if kind == "z" else 10
                    if i % 2 == 0:
                        c.wait_tile(pe, n)
                    w, x, t = c.cols_tile(n), cut(memnT if kind == "mv" else xnT, k=KD), i % 2
                    project(c, pe, out[:, :], lambda k: x[:, k, t * P:(t + 1) * P], lambda k: w[:, k, :])
                elif kind == "xtok":
                    ch, j = i // 3, 4 * (i % 3)
                    pe.wait_ge(s["conv_act"], j + 4)
                    transposes(c, pe, out, [cut(xbcT, j=NCONV)[:, j + q, ch * P:(ch + 1) * P] for q in range(4)])
                elif kind == "bt":
                    pe.wait_ge(s["conv_act"], NCONV)
                    transposes(c, pe, out, [cut(xbcT, j=NCONV)[:, 12 + q, 0:P] for q in range(4)])
                elif kind == "ac":
                    pe.wait_ge(s["dt_dve"], 17)
                    for ch in range(NT):
                        pe.matmul(out[:, 24 * ch:24 * ch + 24], c.f("tri"), cut(adt, t=NT)[:, ch, :], start=True, stop=True)
                    pe.matmul(out[:, 48:72], c.f("ones"), cut(adt, t=NT)[:, 0, :], start=True, stop=True).then_inc(c.units_done, 1)
                elif kind == "cb":
                    ch, gr = steps[i]
                    x = cut(xbcT, j=NCONV)
                    pe.matmul(out[:, 0:P], x[:, 12 + gr, ch * P:(ch + 1) * P], x[:, 16 + gr, ch * P:(ch + 1) * P],
                              start=True, stop=True).then_inc(c.units_done, 1)
                elif kind == "A":
                    ch, gr = steps[i // 2]
                    for hh in range(3):
                        hd = HG * gr + 3 * (i % 2) + hh
                        ins = pe.matmul(out[:, hh * P:(hh + 1) * P], cut(adt, t=NT)[:, ch, hd:hd + 1].broadcast_to([P, P]),
                                        c.f("tri"), start=True, stop=True)
                    ins.then_inc(c.units_done, 1)
                elif kind == "sc":
                    pe.wait_ge(s["q_ev"], i + 1)
                    pe.wait_ge(s["mk_ev"], i + 1)
                    attend_scores(c, pe, out, qT, mkT, i)
                elif kind == "pT":
                    pe.wait_ge(s["sm_dve"], 4 * i + 4)
                    transposes(c, pe, out, [cut(ex, t=NT)[:, t, m * P:(m + 1) * P] for m in range(2) for t in range(NT)])
                elif kind == "pv":
                    pe.wait_ge(s["pt_ev"], i + 1)
                    pe.wait_ge(s["mv_ev"], 2)
                    attend_values(c, pe, out, mv, pTs, i)
                elif kind == "st":
                    pe.wait_ge(s["bt_ev"], 1)
                    pe.wait_ge(s["pool_x"], pool_done(i, "xw"))
                    pe.matmul(out[:, 0:GW], cut(bt, g=4)[:, i, :], xw[i % 2][:, :], start=True, stop=True).then_inc(c.units_done, 1)
                elif kind == "yo":
                    pe.wait_ge(s["st_ev"], i + 1)
                    pe.matmul(out[:, 0:GW], cut(xbcT, j=NCONV)[:, 16 + i, P:2 * P], cut(state, g=4)[:, i, :],
                              start=True, stop=True).then_inc(c.units_done, 1)
                elif kind == "yd":
                    pe.wait_ge(s["m_dve2"], 2 * i + 2)
                    pe.wait_ge(s["pool_x"], pool_done(i, "xdt"))
                    for hd in range(HG):
                        ins = pe.matmul(out[:, hd * HP:(hd + 1) * HP], cut(E[(2 * i + hd // 3) % 4], h=3)[:, hd % 3, :],
                                        xdt[i % 2][:, hd * HP:(hd + 1) * HP], start=True, stop=True)
                    ins.then_inc(c.units_done, 1)
                elif kind == "yT":
                    pe.wait_ge(s["g_dve"], 10)
                    transposes(c, pe, out, [cut(zs, t=NT)[:, ch, (2 * i + jj) * P:(2 * i + jj + 1) * P]
                                            for jj in range(2) for ch in range(NT)])
                elif kind == "out":
                    if i:
                        continue
                    for q in range(4):
                        U.wait_free(pe, ("out", q))
                    pe.wait_ge(s["yT_ev"], 12)
                    pe.wait_ge(s["pv_ev"], 4)
                    for n in range(4):
                        c.wait_tile(pe, 11 + n)
                        for j in range(4):
                            jj = 4 * n + j
                            src = cut(yT, j=12)[:, jj, :] if jj < 12 else cut(mT, h=4)[:, jj - 12, :]
                            for q in range(4):
                                t, half = q // 2, q % 2
                                ins = pe.matmul(U.bank(("out", q))[:, :], src[:, t * P:(t + 1) * P],
                                                c.rows_tile(11 + n)[:, j, 512 * half:512 * half + 512],
                                                start=(jj == 0), stop=(jj == 15))
                                if jj == 15:
                                    ins.then_inc(c.units_done, 1)
                        if n < 3:
                            ins.then_inc(s["out_tile"], 1)
                else:
                    R.pe(pe, key)

        @block.vector
        def _(dve):
            def chain(signal, start=0):
                n = [start]

                def step(ins):
                    n[0] += 1
                    ins.then_inc(signal, 1)
                    dve.wait_ge(signal, n[0])
                return step

            dve.memset(c.pos[:, :], -1.0)
            dve.memset(c.gates[:, :], 0.0)
            dve.wait_ge(s["x_act"], 2)
            dve.tensor_scalar(c.norm_ss[:, 0:2], c.norm_ss[:, 0:2], 1.0 / D, EPS, ALU.mult, ALU.add).then_inc(s["x_dve"], 1)
            dve.wait_ge(s["x_act"], 3)
            dve.reciprocal(c.norm_r[:, 0:2], c.norm_r[:, 0:2]).then_inc(s["x_dve"], 1)
            dve.wait_ge(s["x_dve"], 2)
            norm_scaled(c, dve, c.h, 0, s["x_dve"], 2)
            y_step = chain(s["y_dve"])

            def decay_scores(i):
                dve.wait_ge(s["exp_act"], i + 1)
                dve.tensor_tensor(cut(E[i % 4], h=3), cut(E[i % 4], h=3), spread_mid(cbm[(i // 2) % 2][:, :], 3),
                                  ALU.mult).then_inc(s["m_dve2"], 1)

            for key in order:
                kind, i = key
                bank = U.bank(key)
                if kind == "dt":
                    step = chain(s["dt_dve"])
                    U.wait_done(dve, key)
                    dve.wait_ge(ld_small, 16)
                    step(dve.tensor_tensor(cut(dtx, t=NT), cut(bank[:, 0:48], t=NT), spread_mid(c.f("dt_bias"), NT), ALU.add))
                    step(dve.scalar_tensor_tensor(out=t_[:, :], in0=dtx[:, :], scalar=-1.0, in1=dtx[:, :], op0=ALU.mult, op1=ALU.max))
                    dve.wait_ge(s["dt_act"], 2)
                    step(dve.tensor_scalar(s_[:, :], t_[:, :], 2.0, None, ALU.add))
                    step(dve.reciprocal(s_[:, :], s_[:, :]))
                    step(dve.tensor_tensor(s_[:, :], s_[:, :], t_[:, :], ALU.mult))
                    step(dve.tensor_tensor(s2[:, :], s_[:, :], s_[:, :], ALU.mult))
                    step(dve.tensor_scalar(t_[:, :], s2[:, :], 1.0 / 15, None, ALU.mult))
                    for q in (13, 11, 9, 7, 5, 3):
                        step(dve.scalar_tensor_tensor(out=t_[:, :], in0=t_[:, :], scalar=1.0 / q, in1=s2[:, :], op0=ALU.add, op1=ALU.mult))
                    step(dve.scalar_tensor_tensor(out=t_[:, :], in0=t_[:, :], scalar=1.0, in1=s_[:, :], op0=ALU.add, op1=ALU.mult))
                    step(dve.tensor_scalar(dt[:, :], dtx[:, :], 0.0, None, ALU.max))
                    step(dve.scalar_tensor_tensor(out=dt[:, :], in0=t_[:, :], scalar=2.0, in1=dt[:, :], op0=ALU.mult, op1=ALU.add))
                    step(dve.scalar_tensor_tensor(out=cut(adt, t=NT), in0=cut(dt, t=NT), scalar=-1.0, in1=spread_mid(ea[:, :], NT),
                                                  op0=ALU.mult, op1=ALU.mult))
                elif kind == "conv":
                    step = chain(s["conv_dve"], 4 * i)
                    U.wait_done(dve, key)
                    if i >= 3:
                        dve.wait_ge(s["conv_act"], i - 2)
                    a = cut(acc, b=3)[:, i % 3, :]
                    step(dve.tensor_scalar(a, bank[:, 0:SEQ], c.f("conv_w", 4 * i + 3, 4 * i + 4), c.f("conv_b", i, i + 1), ALU.mult, ALU.add))
                    for back in (1, 2, 3):
                        step(dve.scalar_tensor_tensor(out=a[:, back:], in0=bank[:, 0:SEQ - back], scalar=c.f("conv_w", 4 * i + 3 - back, 4 * i + 4 - back),
                                                      in1=a[:, back:], op0=ALU.mult, op1=ALU.add))
                elif kind == "ac":
                    U.wait_done(dve, key)
                    step = chain(s["ac_dve"])
                    step(dve.tensor_copy(acum[:, :], bank[:, 0:48]))
                    step(dve.tensor_tensor(toend[:, :], bank[:, 48:72], acum[:, 0:24], ALU.subtract))
                elif kind == "z" and i == 5:
                    dve.wait_ge(s["m_act"], 2)
                    dve.tensor_scalar(c.norm_ss[:, 2:4], c.norm_ss[:, 2:4], 1.0 / D, EPS, ALU.mult, ALU.add).then_inc(s["m_dve"], 1)
                    dve.wait_ge(s["m_act"], 3)
                    dve.reciprocal(c.norm_r[:, 2:4], c.norm_r[:, 2:4]).then_inc(s["m_dve"], 1)
                    dve.wait_ge(s["m_dve"], 2)
                    norm_scaled(c, dve, mem, 2, s["m_dve"], 2)
                elif kind == "cb":
                    U.wait_done(dve, key)
                    dve.tensor_tensor(cbm[i % 2][:, :], bank[:, 0:P], c.f("tri"), ALU.mult).then_inc(s["cb_dve"], 1)
                elif kind == "A":
                    ch, gr = steps[i // 2]
                    U.wait_done(dve, key)
                    if i >= 4:
                        dve.wait_ge(c.units_done, U.at["yd", (i - 4) // 2] + 1)
                    for hh in range(3):
                        hd = 24 * ch + HG * gr + 3 * (i % 2) + hh
                        dve.tensor_scalar(cut(E[i % 4], h=3)[:, hh, :], cut(bank[:, 0:GW], h=3)[:, hh, :], acum[:, hd:hd + 1], 0.0,
                                          ALU.subtract, ALU.min).then_inc(s["seg_dve"], 1)
                    if i == 0:
                        dve.wait_ge(s["cb_dve"], 1)
                    else:
                        dve.wait_ge(s["cb_dve"], (i - 1) // 2 + 1)
                        decay_scores(i - 1)
                    if i == 15:
                        decay_scores(15)
                elif kind == "sc":
                    U.wait_done(dve, key)
                    step = chain(s["sm_dve"], 4 * i)
                    if i:
                        dve.wait_ge(c.units_done, U.at["pT", i - 1] + 1)
                    step(dve.tensor_reduce(smc[:, 2 * i:2 * i + 2], cut(bank, t=NT), X, ALU.max))
                    step(dve.tensor_scalar(smc[:, 16 + 2 * i:18 + 2 * i], smc[:, 2 * i:2 * i + 2], -MEM_SCALE, None, ALU.mult))
                elif kind == "pT":
                    step = chain(s["sm_dve"], 4 * i + 2)
                    dve.wait_ge(s["sm_act"], 2 * i + 2)
                    step(dve.reciprocal(smc[:, 48 + 2 * i:50 + 2 * i], smc[:, 32 + 2 * i:34 + 2 * i]))
                    step(dve.tensor_tensor(cut(ex, t=NT), cut(ex, t=NT), spread_last(smc[:, 48 + 2 * i:50 + 2 * i], 256), ALU.mult))
                elif kind == "yd":
                    ch, gr = steps[i]
                    z = cut(zs, t=NT)[:, ch, GW * gr:GW * gr + GW]
                    if ch:
                        yo = ("yo", gr)
                        U.wait_done(dve, yo)
                        y_step(dve.tensor_tensor(heads(yt[:, :]), heads(U.bank(yo)[:, 0:GW]), spread_last(eac[:, HG * gr:HG * gr + HG], HP), ALU.mult))
                    U.wait_done(dve, key)
                    dve.wait_ge(s["pool_x"], pool_done(i, "xd"))
                    if ch:
                        y_step(dve.tensor_tensor(yt[:, :], bank[:, 0:GW], yt[:, :], ALU.add))
                        y_step(dve.tensor_tensor(yt[:, :], xd[i % 2][:, :], yt[:, :], ALU.add))
                    else:
                        dve.wait_ge(s["z_ev"], 6)
                        y_step(dve.tensor_tensor(yt[:, :], bank[:, 0:GW], xd[i % 2][:, :], ALU.add))
                    y_step(dve.tensor_tensor(z, z, yt[:, :], ALU.mult))
                elif kind == "yT" and i == 0:
                    step = chain(s["g_dve"])
                    dve.wait_ge(s["g_act"], 8)
                    step(dve.tensor_scalar(gss[:, :], gss[:, :], 1.0 / GW, EPS, ALU.mult, ALU.add))
                    dve.wait_ge(s["g_act"], 9)
                    step(dve.reciprocal(gss[:, :], gss[:, :]))
                    for st, (ch, gr) in enumerate(steps):
                        z = cut(zs, t=NT)[:, ch, GW * gr:GW * gr + GW]
                        dve.tensor_scalar(z, z, gss[:, st:st + 1], None, ALU.mult).then_inc(s["g_dve"], 1)
                elif kind == "out":
                    U.wait_done(dve, key)
                    hv = cut(c.h, t=NT)[:, i // 2, 512 * (i % 2):512 * (i % 2) + 512]
                    dve.tensor_tensor(hv, hv, bank[:, :], ALU.add).then_inc(s["h_new"], 1)
            R.dve(dve)


class Experts:

    SEMS = ("pick gated gathered xg_ready gu_done silu_done hid_ready turned turned_ready down_done gates_turned gates_ready "
            "y_ready scattered gu0_loaded gu1_loaded down0_loaded down1_loaded")
    PAIRS = NE // 2
    HALF = WT // 2

    def __init__(self, c, layer, ctx):
        self.c, self.layer = c, layer
        sb = lambda name, n: c.sb(f"e{layer}_{name}", n, ctx)
        self.pick = sb("pick", NT * 2 * TOKS)
        self.gated = sb("gated", NT * 2 * TOKS)
        self.xg = sb("xg", KD * 2 * TOKS)
        self.silu = sb("silu", DE)
        self.hid = sb("hid", DE)
        self.turned = sb("turned", DE)
        self.gates_T = sb("gates_T", SEQ)
        self.y = [sb(f"y{i}", 512) for i in range(2)]
        self.sums, (self.b_gate, self.b_up, self.b_gather, self.b_turn) = c.banks[0:4], c.banks[4:8]
        self.b_down = [self.b_gate, self.b_up]

    def tile(self, n):
        at = (2 * FIRST_SLOT[self.layer] + n) % (2 * SLOTS) * self.HALF
        return self.c.ring[:, at:at + self.HALF]

    def weights(self, e, what, half):
        w = self.c.ins["w_" + what][self.layer, bass.ds(e, 1)]
        if what == "down":
            return w[:, 256 * half:256 * half + 256, :].rearrange("o (j p) c -> (o p) j c", p=P)
        return w.rearrange("o (p k) c -> (o p) k c", k=KD)[:, 4 * half:4 * half + 4, :]

    def load_tile(self, sp, s, p, n):
        q = n // 2 % 2 if n < 8 else n % 2
        if n < 8:
            half, what = n // 4, ("gate", "up")[n % 2]
            dst, loaded = cut(self.tile(n), k=4), s[f"gu{half}_loaded"]
        else:
            half, what = (n - 8) // 2, "down"
            dst, loaded = cut(self.tile(n), j=2), s[f"down{half}_loaded"]
        sp.dma_start(dst, self.weights(p * 2 + q, what, half)).then_inc(loaded, 16)

    def rounds(self, eng, body):
        body(0)
        most = eng.value_load(self.c.most[0:1, 0:1], min_val=0, max_val=SEQ)
        for rnd in range(1, ROUNDS):
            with eng.If(most > rnd * TOKS):
                body(rnd)
        eng.nop()

    def block(self):
        c, layer, PAIRS = self.c, self.layer, self.PAIRS
        sets = experts_sems(c)
        with c.nc.Block() as block:

            @block.sync
            def _(sp):
                def body(rnd):
                    s = sets[rnd]
                    if rnd:
                        sp.wait_ge(sets[rnd - 1]["down_done"], 2 * PAIRS)
                        for n in range(12):
                            self.load_tile(sp, s, 0, n)
                    with sp.Fori(0, PAIRS - 1) as i:
                        for half in range(2):
                            sp.wait_ge(s["gu_done"], i * 2 + (1 + half))
                            for n in range(4):
                                self.load_tile(sp, s, i + 1, 4 * half + n)
                        for half in range(2):
                            sp.wait_ge(s["down_done"], i * 2 + (1 + half))
                            for n in range(2):
                                self.load_tile(sp, s, i + 1, 8 + 2 * half + n)
                    sp.wait_ge(s["gu_done"], 2 * PAIRS)
                    if rnd:
                        sp.wait_ge(s["down_done"], 2 * PAIRS)

                self.rounds(sp, body)
                if layer == 0:
                    s = sets[0]
                    for n in range(SLOTS):
                        if n >= 4:
                            sp.wait_ge(s["down_done"], 2 * PAIRS - 5 + n)
                        c.load_mixer_tile(sp, TILES_A + n)

            @block.vector
            def _(dve):
                def body(rnd):
                    s = sets[rnd]
                    iota = c.f("iota", rnd * TOKS, (rnd + 1) * TOKS)

                    def pick(p):
                        for t in range(NT):
                            for q in range(2):
                                dve.tensor_scalar(self.pick[:, (2 * t + q) * TOKS:(2 * t + q + 1) * TOKS], iota,
                                                  c.pos[:, bass.ds(p * 2 + (t * NE + q), 1)], None, ALU.is_equal).then_inc(s["pick"], 1)

                    def gated(p):
                        for t in range(NT):
                            for q in range(2):
                                at = bass.ds(p * 2 + (t * NE + q), 1)
                                dve.tensor_scalar(self.gated[:, (2 * t + q) * TOKS:(2 * t + q + 1) * TOKS], iota, c.pos[:, at],
                                                  c.gates[:, at], ALU.is_equal, ALU.mult).then_inc(s["gated"], 1)

                    def gathered(half):
                        dve.tensor_tensor(cut(self.xg[:, 512 * half:512 * half + 512], k=4), cut(self.b_gather, k=4),
                                          spread_last(c.f(f"ffn_norm{layer}", 4 * half, 4 * half + 4), 2 * TOKS), ALU.mult).then_inc(s["xg_ready"], 1)

                    def pair(p, last=False):
                        gated(p)
                        if not last:
                            pick(p + 1)
                        dve.wait_ge(s["silu_done"], p + 1)
                        dve.tensor_tensor(self.hid[:, :], self.silu[:, :], self.b_up[:, :], ALU.mult).then_inc(s["hid_ready"], 1)
                        if not last:
                            dve.wait_ge(s["gathered"], p * 2 + 3)
                            gathered(0)
                        dve.wait_ge(s["down_done"], p * 2 + 2)
                        dve.tensor_copy(self.y[1][:, :], self.b_down[1][:, :]).then_inc(s["y_ready"], 1)
                        if not last:
                            dve.wait_ge(s["gathered"], p * 2 + 4)
                            gathered(1)

                    if rnd:
                        dve.wait_ge(sets[rnd - 1]["scattered"], 1)
                    pick(0)
                    for half in range(2):
                        dve.wait_ge(s["gathered"], half + 1)
                        gathered(half)
                    with dve.Fori(0, PAIRS - 1) as i:
                        pair(i)
                    pair(PAIRS - 1, last=True)
                    dve.wait_ge(s["scattered"], 1)

                self.rounds(dve, body)
                for q in range(4):
                    dve.tensor_tensor(c.h[:, 512 * q:512 * q + 512], c.h[:, 512 * q:512 * q + 512], self.sums[q][:, :], ALU.add)

            @block.scalar
            def _(act):
                def body(rnd):
                    s = sets[rnd]
                    if rnd:
                        act.wait_ge(sets[rnd - 1]["scattered"], 1)
                    with act.Fori(0, PAIRS) as i:
                        act.wait_ge(s["gu_done"], i * 2 + 2)
                        act.activation(self.silu[:, :], self.b_gate[:, :], ACT.Silu).then_inc(s["silu_done"], 1)
                        act.wait_ge(s["turned"], i + 1)
                        for half in range(2):
                            act.activation(self.turned[:, 256 * half:256 * half + 256], self.b_turn[:, 256 * half:256 * half + 256],
                                           ACT.Copy).then_inc(s["turned_ready"], 1)
                        act.wait_ge(s["down_done"], i * 2 + 2)
                        act.activation(self.y[0][:, :], self.b_down[0][:, :], ACT.Copy).then_inc(s["y_ready"], 1)
                        act.wait_ge(s["gates_turned"], i + 1)
                        act.activation(self.gates_T[:, :], self.b_turn[:, 0:SEQ], ACT.Copy).then_inc(s["gates_ready"], 1)

                self.rounds(act, body)

            @block.tensor
            def _(pe):
                def body(rnd):
                    s = sets[rnd]
                    xs = c.xs[:, :].rearrange("q (t k p) -> q t k p", t=NT, k=KD)

                    def gather(half):
                        for k in range(4):
                            for t in range(NT):
                                ins = pe.matmul(self.b_gather[:, k * P:(k + 1) * P], xs[:, t, 4 * half + k, :], cut(self.pick, t=NT)[:, t, :],
                                                start=(t == 0), stop=(t == NT - 1))
                        ins.then_inc(s["gathered"], 1)

                    def pair(p, first=False, last=False):
                        for half in range(2):
                            pe.wait_ge(s["xg_ready"], p * 2 + (half + 1))
                            pe.wait_ge(s[f"gu{half}_loaded"], p * 64 + 64)
                            for k in range(4):
                                for w, bank in enumerate((self.b_gate, self.b_up)):
                                    for q in range(2):
                                        ins = pe.matmul(bank[q * TOKS:(q + 1) * TOKS, :], self.xg[:, (4 * half + k) * P + q * TOKS:(4 * half + k) * P + (q + 1) * TOKS],
                                                        cut(self.tile(4 * half + 2 * q + w), k=4)[:, k, :],
                                                        start=(half == 0 and k == 0), stop=(half == 1 and k == 3))
                            ins.then_inc(s["gu_done"], 1)
                        if not last:
                            pe.wait_ge(s["pick"], p * 4 + 8)
                            gather(0)
                        pe.wait_ge(s["hid_ready"], p + 1)
                        for j in range(4):
                            ins = pe.transpose(self.b_turn[:, j * P:(j + 1) * P], self.hid[:, j * P:(j + 1) * P], c.f("ident"))
                        ins.then_inc(s["turned"], 1)
                        for half in range(2):
                            pe.wait_ge(s["turned_ready"], p * 2 + (half + 1))
                            pe.wait_ge(s[f"down{half}_loaded"], p * 32 + 32)
                            for j in range(2):
                                for out in range(2):
                                    for q in range(2):
                                        at = (2 * half + j) * P + q * TOKS
                                        ins = pe.matmul(self.b_down[out][q * TOKS:(q + 1) * TOKS, :], self.turned[:, at:at + TOKS],
                                                        cut(self.tile(8 + 2 * half + q), j=2)[:, j, 512 * out:512 * out + 512],
                                                        start=(half == 0 and j == 0), stop=(half == 1 and j == 1))
                            ins.then_inc(s["down_done"], 1)
                        pe.wait_ge(s["gated"], p * 4 + 4)
                        for t in range(NT):
                            ins = pe.transpose(self.b_turn[:, t * P:(t + 1) * P], cut(self.gated, t=NT)[:, t, :], c.f("ident"))
                        ins.then_inc(s["gates_turned"], 1)
                        if not last:
                            pe.wait_ge(s["xg_ready"], p * 2 + 3)
                            gather(1)
                        pe.wait_ge(s["y_ready"], p * 2 + 2)
                        pe.wait_ge(s["gates_ready"], p + 1)
                        for t in range(NT):
                            for out in range(2):
                                ins = pe.matmul(self.sums[2 * t + out][:, :], self.gates_T[:, t * P:(t + 1) * P], self.y[out][:, :],
                                                start=first, stop=last, skip_group_check=True)
                        if last:
                            ins.then_inc(s["scattered"], 1)

                    pe.wait_ge(s["pick"], 4)
                    gather(0)
                    pe.wait_ge(s["xg_ready"], 1)
                    gather(1)
                    pair(0, first=(rnd == 0))
                    with pe.Fori(1, PAIRS - 1) as i:
                        pair(i)
                    pair(PAIRS - 1, last=True)

                self.rounds(pe, body)

            if layer == 0:
                @block.gpsimd
                def _(pool):
                    c.clear(pool, "mixer")


def experts_sems(c):
    return [c.sems(f"experts_round{r}", Experts.SEMS) for r in range(ROUNDS)]


def first_pair_loader(c, layer):
    E = Experts.__new__(Experts)
    E.c, E.layer = c, layer
    s = experts_sems(c)[0]

    def load(sp, i):
        for n in (2 * i, 2 * i + 1):
            E.load_tile(sp, s, 0, n)

    return load


def moe(c, layer):
    with ExitStack() as ctx:
        Experts(c, layer, ctx).block()


def mixer_b(c):
    g = c.ins
    names = ("x_act x_dve xT_ev xk_dve kv_ev kr_dve kT_ev q_ev qr_dve qT_ev qm_ev m_act m_dve memT_ev mk_ev mv_ev as_dve as_act "
             "an_dve aT_ev av_ev sm_dve sm_act pt_ev pv_ev out_tile " + Router.SEMS)
    s = c.sems("mixer", names)
    ld_mem, cleared = c.sem("b_ld_mem"), c.sem("b_cleared")
    with ExitStack() as ctx:
        sb = lambda name, n: c.sb("b_" + name, n, ctx)
        xnT, xkT, memnT = sb("xnT", KD * SEQ), sb("xkT", KD * SEQ), sb("memnT", KD * SEQ)
        mem = memnT
        qtok, qT = sb("qtok", NT * 1024), sb("qT", 8 * SEQ)
        attT = qtok
        kd, vt, kT = sb("kd", NT * 512), sb("vt", NT * 256), sb("kT", 4 * SEQ)
        mkT, mv, qmT = sb("mkT", 1024), sb("mv", 1024), sb("qmT", 1024)
        mT = qmT
        ex, pTs = sb("ex", 512), sb("pTs", 512)
        ee = [sb(f"ee{i}", 512) for i in range(3)]
        aTs = [sb(f"aTs{i}", 512) for i in range(2)]
        rot_c, rot_s = sb("rot_c", P), sb("rot_s", P)
        smc = sb("smc", 64)
        col = sb("col", 16 * 12)

        parts = [(t, kv, odd) for t in range(NT) for kv in range(KV_HEADS) for odd in range(2)]
        NA = len(parts)
        width = lambda n: P if parts[n][0] == 0 else 2 * P
        order = [("xT", i) for i in range(4)] + [("kv", t) for t in range(NT)] + [("q", i) for i in range(4)]
        order += [("kT", t) for t in range(NT)] + [("qT", i) for i in range(4)]
        fill = [("qm", h) for h in range(4)] + [("memT", i) for i in range(4)] + [("mk", h) for h in range(4)] + [("mv", m) for m in range(2)]
        fill += [(kind, h) for h in range(4) for kind in ("sc", "pT", "pv")]
        for n in range(NA + 2):
            if n < NA:
                order += [("as", n)]
            order += fill[2 * n:2 * n + 1]
            if 1 <= n <= NA:
                order += [("aT", n - 1)]
            order += fill[2 * n + 1:2 * n + 2]
            if n >= 2:
                order += [("av", n - 2)]
        order += [("out", i) for i in range(4)] + Router.UNITS

        def freed(kind, i):
            if kind in ("x2T", "router", "places"):
                return Router.freed(s, kind, i)
            return {"xT": (s["xk_dve"], i + 1), "kv": (s["kv_ev"], 2 * i + 2), "q": (s["q_ev"], i + 1), "kT": (s["kT_ev"], i + 1),
                    "qT": (s["qT_ev"], i + 1), "qm": (s["qm_ev"], i + 1), "memT": (s["memT_ev"], 2 * i + 2), "mk": (s["mk_ev"], i + 1),
                    "mv": (s["mv_ev"], i + 1), "as": (s["as_dve"], 5 * i + 1), "aT": (s["aT_ev"], i + 1), "av": (s["av_ev"], i + 1),
                    "sc": (s["sm_act"], 2 * i + 2), "pT": (s["pt_ev"], i + 1), "pv": (s["pv_ev"], i + 1),
                    "out": (s["h_new"], i + 1)}[kind]

        U = Units(c, order, freed)
        R = Router(c, U, s, 1, xnT, memnT)

        def tile_used(n):
            last = [("kv", 1), ("q", 1), ("q", 3), ("qm", 3), ("mk", 3), ("mv", 1)]
            if n - B0 < 6:
                return c.units_done, U.at[last[n - B0]] + 1
            if n - B0 < 8:
                return s["out_tile"], n - B0 - 5
            return c.units_done, U.at["out", 3] + 1

        def kd_heads(t, dup):
            return kd[:, :].rearrange("p (t h d c) -> p t h d c", t=NT, h=KV_HEADS, d=2)[:, t, :, dup, :]

        block = ctx.enter_context(c.nc.Block())

        @block.sync
        def _(sp):
            for t in range(NT):
                sp.dma_start(cut(mem, t=NT)[:, t, :], g["mem"][0, t * P:(t + 1) * P, :]).then_inc(ld_mem, 16)
            first_pair = first_pair_loader(c, 1)
            for n in range(B0 + SLOTS, B0 + TILES_B + SLOTS):
                sp.wait_ge(*tile_used(n - SLOTS))
                if n < B0 + TILES_B:
                    c.load_mixer_tile(sp, n)
                else:
                    sp.wait_ge(cleared, 1)
                    first_pair(sp, n - B0 - TILES_B)

        @block.gpsimd
        def _(pool):
            c.clear(pool, *(f"experts_round{r}" for r in range(ROUNDS)))
            pool.nop().then_inc(cleared, 1)

        @block.scalar
        def _(act):
            norm_squares(c, act, c.h, 0, s["x_act"])
            act.wait_ge(s["x_dve"], 1)
            act.activation(c.norm_r[:, 0:2], c.norm_ss[:, 0:2], ACT.Sqrt).then_inc(s["x_act"], 1)
            for key in order:
                kind, i = key
                if kind in ("out", "x2T", "router", "places"):
                    continue
                bank = U.bank(key)
                if kind == "qm" and i == 0:
                    act.wait_ge(ld_mem, 32)
                    act.wait_ge(c.units_done, U.at["xT", 3] + 1)
                    norm_squares(c, act, mem, 2, s["m_act"])
                    act.wait_ge(s["m_dve"], 1)
                    act.activation(c.norm_r[:, 2:4], c.norm_ss[:, 2:4], ACT.Sqrt).then_inc(s["m_act"], 1)
                if kind in ("xT", "memT"):
                    U.wait_done(act, key)
                    if kind == "memT" and i == 0:
                        act.wait_ge(s["m_dve"], 4)
                    dst, w = (xnT, "b_norm") if kind == "xT" else (memnT, "mem_norm1")
                    for kk in range(2):
                        k = 2 * i + kk
                        act.activation(cut(dst, k=KD)[:, k, :], bank[:, kk * 256:(kk + 1) * 256], ACT.Copy,
                                       scale=c.f(w, k, k + 1)).then_inc(s[kind + "_ev"], 1)
                elif kind == "as":
                    act.wait_ge(s["as_dve"], 5 * i + 5)
                    w = width(i)
                    k = 12 * i
                    for q in range(2):
                        act.activation(ee[i % 3][:, q * w:(q + 1) * w], ee[i % 3][:, q * w:(q + 1) * w], ACT.Exp,
                                       bias=col[:, k + 2 + q:k + 3 + q], accum_out=col[:, k + 4 + q:k + 5 + q]).then_inc(s["as_act"], 1)
                    act.activation(col[:, k + 6:k + 8], col[:, k + 6:k + 8], ACT.Exp).then_inc(s["as_act"], 1)
                elif kind == "sc":
                    U.wait_done(act, key)
                    act.wait_ge(s["sm_dve"], 4 * i + 2)
                    for t in range(NT):
                        act.activation(cut(ex, t=NT)[:, t, :], cut(bank, t=NT)[:, t, :], ACT.Exp, scale=MEM_SCALE,
                                       bias=smc[:, 16 + 2 * i + t:17 + 2 * i + t],
                                       accum_out=smc[:, 32 + 2 * i + t:33 + 2 * i + t]).then_inc(s["sm_act"], 1)
                else:
                    U.wait_done(act, key)
                    if kind == "kv":
                        act.activation(cut(vt, t=NT)[:, i, :], bank[:, 256:512], ACT.Copy).then_inc(s["kv_ev"], 1)
                        act.activation(kd_heads(i, 0), cut(bank[:, 0:256], h=4), ACT.Copy).then_inc(s["kv_ev"], 1)
                    elif kind == "q":
                        act.activation(cut(qtok, t=NT)[:, i % 2, 512 * (i // 2):512 * (i // 2) + 512], bank[:, :], ACT.Copy).then_inc(s["q_ev"], 1)
                    elif kind == "kT":
                        act.activation(cut(kT, g=4)[:, :, i * P:(i + 1) * P], cut(bank, g=4), ACT.Copy).then_inc(s["kT_ev"], 1)
                    elif kind == "qT":
                        act.activation(cut(qT, g=8)[:, 4 * (i // 2):4 * (i // 2) + 4, (i % 2) * P:(i % 2) * P + P], cut(bank, g=4),
                                       ACT.Copy).then_inc(s["qT_ev"], 1)
                    elif kind == "qm":
                        act.activation(cut(qmT, h=4)[:, i, :], bank[:, 0:256], ACT.Copy).then_inc(s["qm_ev"], 1)
                    elif kind == "mk":
                        act.activation(cut(mkT, h=4)[:, i, :], bank[:, 0:256], ACT.Copy).then_inc(s["mk_ev"], 1)
                    elif kind == "mv":
                        act.activation(cut(mv, m=2)[:, i, :], bank[:, :], ACT.Copy).then_inc(s["mv_ev"], 1)
                    elif kind == "aT":
                        if i >= 2:
                            act.wait_ge(c.units_done, U.at["av", i - 2] + 1)
                        act.activation(aTs[i % 2][:, 0:2 * width(i)], bank[:, 0:2 * width(i)], ACT.Copy).then_inc(s["aT_ev"], 1)
                    elif kind == "av":
                        t, kv, odd = parts[i]
                        r = slice(64 * odd, 64 * odd + 64)
                        act.activation(cut(attT, j=8)[r, 2 * kv:2 * kv + 2, t * P:(t + 1) * P], cut(bank[r, 0:256], j=2),
                                       ACT.Copy).then_inc(s["av_ev"], 1)
                    elif kind == "pT":
                        act.activation(pTs[:, :], bank[:, :], ACT.Copy).then_inc(s["pt_ev"], 1)
                    elif kind == "pv":
                        act.activation(cut(mT, h=4)[:, i, :], bank[:, 0:256], ACT.Copy).then_inc(s["pv_ev"], 1)
            R.act(act)

        @block.tensor
        def _(pe):
            for key in order:
                kind, i = key
                out = U.bank(key)
                if kind != "out":
                    U.wait_free(pe, key)
                if kind in ("xT", "memT"):
                    if i == 0:
                        pe.wait_ge(s["x_dve" if kind == "xT" else "m_dve"], 4)
                    norm_T_units(c, pe, out, i)
                elif kind in ("kv", "q", "mv"):
                    n = B0 + {"kv": 0, "q": 1 + i // 2, "mv": 5}[kind]
                    t = i % 2
                    if t == 0:
                        c.wait_tile(pe, n)
                    if key == ("kv", 0):
                        pe.wait_ge(s["xk_dve"], 4)
                    w, x = c.cols_tile(n), cut({"kv": xkT, "q": xnT, "mv": memnT}[kind], k=KD)
                    project(c, pe, out[:, :], lambda k: x[:, k, t * P:(t + 1) * P], lambda k: w[:, k, :])
                elif kind in ("qm", "mk"):
                    n = B0 + (3 if kind == "qm" else 4)
                    if i == 0:
                        c.wait_tile(pe, n)
                        if kind == "mk":
                            pe.wait_ge(s["memT_ev"], 8)
                    w, x = c.cols_tile(n), cut(memnT if kind == "mk" else xnT, k=KD)
                    project(c, pe, out[:, 0:256], lambda k: w[:, k, P * i:P * i + P], lambda k: x[:, k, :])
                elif kind == "kT":
                    pe.wait_ge(s["kr_dve"], 5 * i + 5)
                    transposes(c, pe, out, [kd[:, 512 * i + P * q:512 * i + P * q + P] for q in range(4)])
                elif kind == "qT":
                    pe.wait_ge(s["qr_dve"], 4 * i + 4)
                    at = 1024 * (i % 2) + 512 * (i // 2)
                    transposes(c, pe, out, [qtok[:, at + P * q:at + P * q + P] for q in range(4)])
                elif kind == "as":
                    t, kv, odd = parts[i]
                    r, w = slice(64 * odd, 64 * odd + 64), width(i)
                    pe.wait_ge(s["qT_ev"], 4)
                    pe.wait_ge(s["kT_ev"], 2)
                    for q in range(2):
                        ins = pe.matmul(out[:, q * w:(q + 1) * w], cut(qT, g=8)[r, 2 * kv + q, t * P:(t + 1) * P], cut(kT, g=4)[r, kv, 0:w],
                                        start=True, stop=True)
                    ins.then_inc(c.units_done, 1)
                elif kind == "aT":
                    pe.wait_ge(s["an_dve"], 3 * i + 3)
                    transposes(c, pe, out, [ee[i % 3][:, q * P:(q + 1) * P] for q in range(2 * width(i) // P)])
                elif kind == "av":
                    t, kv, odd = parts[i]
                    r, nb = slice(64 * odd, 64 * odd + 64), width(i) // P
                    pe.wait_ge(s["aT_ev"], i + 1)
                    for q in range(2):
                        for m in range(nb):
                            ins = pe.matmul(out[r, q * P:(q + 1) * P], cut(vt, t=NT)[:, m, 64 * kv:64 * kv + 64],
                                            aTs[i % 2][:, (q * nb + m) * P:(q * nb + m + 1) * P], start=(m == 0), stop=(m == nb - 1))
                    ins.then_inc(c.units_done, 1)
                elif kind == "sc":
                    pe.wait_ge(s["qm_ev"], i + 1)
                    pe.wait_ge(s["mk_ev"], i + 1)
                    attend_scores(c, pe, out, qmT, mkT, i)
                elif kind == "pT":
                    pe.wait_ge(s["sm_dve"], 4 * i + 4)
                    transposes(c, pe, out, [cut(ex, t=NT)[:, t, m * P:(m + 1) * P] for m in range(2) for t in range(NT)])
                elif kind == "pv":
                    pe.wait_ge(s["pt_ev"], i + 1)
                    pe.wait_ge(s["mv_ev"], 2)
                    attend_values(c, pe, out, mv, pTs, i)
                elif kind == "out":
                    if i:
                        continue
                    for q in range(4):
                        U.wait_free(pe, ("out", q))
                    pe.wait_ge(s["av_ev"], NA)
                    pe.wait_ge(s["pv_ev"], 4)
                    for n in range(3):
                        c.wait_tile(pe, B0 + 6 + n)
                        for j in range(4):
                            jj = 4 * n + j
                            src = cut(attT, j=8)[:, jj, :] if jj < 8 else cut(mT, h=4)[:, jj - 8, :]
                            for q in range(4):
                                t, half = q // 2, q % 2
                                ins = pe.matmul(U.bank(("out", q))[:, :], src[:, t * P:(t + 1) * P],
                                                c.rows_tile(B0 + 6 + n)[:, j, 512 * half:512 * half + 512],
                                                start=(jj == 0), stop=(jj == 11))
                                if jj == 11:
                                    ins.then_inc(c.units_done, 1)
                        if n < 2:
                            ins.then_inc(s["out_tile"], 1)
                else:
                    R.pe(pe, key)

        @block.vector
        def _(dve):
            def chain(signal, start=0):
                n = [start]

                def step(ins):
                    n[0] += 1
                    ins.then_inc(signal, 1)
                    dve.wait_ge(signal, n[0])
                return step

            def turn(step, x, t, heads):
                a, b = cut(rot_c[:, 0:16 * heads], h=heads), cut(rot_s[:, 0:16 * heads], h=heads)
                step(dve.tensor_tensor(a, x[:, :, 0:16], spread_mid(c.f("cos", 16 * t, 16 * t + 16), heads), ALU.mult))
                step(dve.tensor_tensor(b, x[:, :, 0:16], spread_mid(c.f("sin", 16 * t, 16 * t + 16), heads), ALU.mult))
                step(dve.tensor_tensor(x[:, :, 0:8], a[:, :, 0:8], b[:, :, 8:16], ALU.subtract))
                step(dve.tensor_tensor(x[:, :, 8:16], a[:, :, 8:16], b[:, :, 0:8], ALU.add))

            dve.wait_ge(s["x_act"], 2)
            dve.tensor_scalar(c.norm_ss[:, 0:2], c.norm_ss[:, 0:2], 1.0 / D, EPS, ALU.mult, ALU.add).then_inc(s["x_dve"], 1)
            dve.wait_ge(s["x_act"], 3)
            dve.reciprocal(c.norm_r[:, 0:2], c.norm_r[:, 0:2]).then_inc(s["x_dve"], 1)
            dve.wait_ge(s["x_dve"], 2)
            norm_scaled(c, dve, c.h, 0, s["x_dve"], 2)
            for key in order:
                kind, i = key
                bank = U.bank(key)
                if kind == "qm" and i == 0:
                    dve.wait_ge(s["m_act"], 2)
                    dve.tensor_scalar(c.norm_ss[:, 2:4], c.norm_ss[:, 2:4], 1.0 / D, EPS, ALU.mult, ALU.add).then_inc(s["m_dve"], 1)
                    dve.wait_ge(s["m_act"], 3)
                    dve.reciprocal(c.norm_r[:, 2:4], c.norm_r[:, 2:4]).then_inc(s["m_dve"], 1)
                    dve.wait_ge(s["m_dve"], 2)
                    norm_scaled(c, dve, mem, 2, s["m_dve"], 2)
                elif kind == "xT":
                    dve.wait_ge(s["xT_ev"], 2 * i + 2)
                    dve.tensor_tensor(cut(xkT, k=KD)[:, 2 * i:2 * i + 2, :], cut(bank, k=2), spread_last(c.f("kv_norm", 2 * i, 2 * i + 2), SEQ),
                                      ALU.mult).then_inc(s["xk_dve"], 1)
                elif kind == "kv":
                    step = chain(s["kr_dve"], 5 * i)
                    dve.wait_ge(s["kv_ev"], 2 * i + 2)
                    turn(step, kd_heads(i, 0), i, KV_HEADS)
                    step(dve.tensor_copy(kd_heads(i, 1), kd_heads(i, 0)))
                elif kind == "q":
                    dve.wait_ge(s["q_ev"], i + 1)
                    at = 1024 * (i % 2) + 512 * (i // 2)
                    turn(chain(s["qr_dve"], 4 * i), cut(qtok[:, at:at + 512], h=8), i % 2, 8)
                elif kind == "as":
                    t, kv, odd = parts[i]
                    w = width(i)
                    step = chain(s["as_dve"], 5 * i)
                    U.wait_done(dve, key)
                    if i >= 3:
                        dve.wait_ge(c.units_done, U.at["aT", i - 3] + 1)
                    mask = c.f("band_cur") if t == 0 else c.small[:, AT["band_prev"][0]:AT["band_prev"][0] + 2 * P]
                    e, k = cut(ee[i % 3][:, 0:2 * w], q=2), 12 * i
                    sinks = c.f("sinks", 4 * kv + odd, 4 * kv + odd + 3)[:, ::2]
                    step(dve.scalar_tensor_tensor(out=e, in0=cut(bank[:, 0:2 * w], q=2), scalar=ATT_SCALE, in1=spread_mid(mask, 2),
                                                  op0=ALU.mult, op1=ALU.add))
                    step(dve.tensor_reduce(col[:, k:k + 2], e, X, ALU.max))
                    step(dve.tensor_tensor(col[:, k:k + 2], col[:, k:k + 2], sinks, ALU.max))
                    step(dve.tensor_scalar(col[:, k + 2:k + 4], col[:, k:k + 2], -1.0, None, ALU.mult))
                    step(dve.tensor_tensor(col[:, k + 6:k + 8], sinks, col[:, k:k + 2], ALU.subtract))
                elif kind == "aT":
                    w, k = width(i), 12 * i
                    step = chain(s["an_dve"], 3 * i)
                    dve.wait_ge(s["as_act"], 3 * i + 3)
                    step(dve.tensor_tensor(col[:, k + 8:k + 10], col[:, k + 4:k + 6], col[:, k + 6:k + 8], ALU.add))
                    step(dve.reciprocal(col[:, k + 8:k + 10], col[:, k + 8:k + 10]))
                    e = cut(ee[i % 3][:, 0:2 * w], q=2)
                    step(dve.tensor_tensor(e, e, spread_last(col[:, k + 8:k + 10], w), ALU.mult))
                elif kind == "sc":
                    U.wait_done(dve, key)
                    step = chain(s["sm_dve"], 4 * i)
                    if i:
                        dve.wait_ge(c.units_done, U.at["pT", i - 1] + 1)
                    step(dve.tensor_reduce(smc[:, 2 * i:2 * i + 2], cut(bank, t=NT), X, ALU.max))
                    step(dve.tensor_scalar(smc[:, 16 + 2 * i:18 + 2 * i], smc[:, 2 * i:2 * i + 2], -MEM_SCALE, None, ALU.mult))
                elif kind == "pT":
                    step = chain(s["sm_dve"], 4 * i + 2)
                    dve.wait_ge(s["sm_act"], 2 * i + 2)
                    step(dve.reciprocal(smc[:, 48 + 2 * i:50 + 2 * i], smc[:, 32 + 2 * i:34 + 2 * i]))
                    step(dve.tensor_tensor(cut(ex, t=NT), cut(ex, t=NT), spread_last(smc[:, 48 + 2 * i:50 + 2 * i], 256), ALU.mult))
                elif kind == "out":
                    U.wait_done(dve, key)
                    hv = cut(c.h, t=NT)[:, i // 2, 512 * (i % 2):512 * (i % 2) + 512]
                    dve.tensor_tensor(hv, hv, bank[:, :], ALU.add).then_inc(s["h_new"], 1)
            R.dve(dve)


def final_norm(c):
    s = c.sems("f", "ld act dve")
    stored = [c.sem(f"f_stored{t}") for t in range(NT)]
    with ExitStack() as ctx:
        w = c.sb("f_w", D, ctx)
        with c.nc.Block() as block:

            @block.sync
            def _(sp):
                sp.dma_start(w[:, :], c.ins["final_norm_w"].rearrange("(o n) -> o n", o=1).broadcast_to([P, D])).then_inc(s["ld"], 16)
                for t in range(NT):
                    sp.wait_ge(s["dve"], 3 + t)
                    sp.dma_start(c.out[0, t * P:(t + 1) * P, :], cut(c.h, t=NT)[:, t, :]).then_inc(stored[t], 16)
                for t in range(NT):
                    sp.wait_ge(stored[t], 16)

            @block.scalar
            def _(act):
                norm_squares(c, act, c.h, 0, s["act"])
                act.wait_ge(s["dve"], 1)
                act.activation(c.norm_r[:, 0:2], c.norm_ss[:, 0:2], ACT.Sqrt).then_inc(s["act"], 1)

            @block.vector
            def _(dve):
                dve.wait_ge(s["act"], 2)
                dve.tensor_scalar(c.norm_ss[:, 0:2], c.norm_ss[:, 0:2], 1.0 / D, EPS, ALU.mult, ALU.add).then_inc(s["dve"], 1)
                dve.wait_ge(s["act"], 3)
                dve.reciprocal(c.norm_r[:, 0:2], c.norm_r[:, 0:2]).then_inc(s["dve"], 1)
                dve.wait_ge(s["dve"], 2)
                dve.wait_ge(s["ld"], 16)
                for t in range(NT):
                    hv = cut(c.h, t=NT)[:, t, :]
                    dve.scalar_tensor_tensor(out=hv, in0=hv, scalar=c.norm_r[:, t:t + 1], in1=w[:, :], op0=ALU.mult,
                                             op1=ALU.mult).then_inc(s["dve"], 1)


def build(nc, ins, out):
    with ExitStack() as ctx:
        c = Core(nc, ins, out, ctx)
        mixer_a(c)
        moe(c, 0)
        mixer_b(c)
        moe(c, 1)
        final_norm(c)


INPUTS = ["x", "mem", "a_in_w", "a_out_w", "w_kv", "b_in_w", "b_out_w", "mem_w_kv", "w_gate", "w_up", "w_down", "final_norm_w"]


def pack_small(v):
    a = np.zeros((P, SMALL), np.float32)

    def put(name, x):
        at, w = AT[name]
        a[:, at:at + w] = x

    def by_row(w):
        return np.asarray(w).reshape(P, -1)

    i = np.arange(P)
    put("ident", np.eye(P))
    put("tri", i[:, None] <= i[None, :])
    put("ones", 1.0)
    put("iota", np.arange(ROUNDS * TOKS)[None, :])
    put("band_prev", np.where(i[None, :] > i[:, None], 0.0, NEG))
    put("band_cur", np.where(i[None, :] <= i[:, None], 0.0, NEG))
    put("index8", np.arange(EG)[None, :] - 100.0)
    freq = np.float32(500000.0) ** (np.float32(-2.0) * np.arange(HALF_ROT, dtype=np.float32) / np.float32(2 * HALF_ROT))
    angle = np.arange(SEQ, dtype=np.float32)[:, None] * freq[None, :].astype(np.float32)
    for name, fn in (("cos", np.cos), ("sin", np.sin)):
        table = np.concatenate([fn(angle), fn(angle)], axis=1).astype(np.float32)
        put(name, table.reshape(NT, P, 16).transpose(1, 0, 2).reshape(P, NT * 16))
    put("a_norm", by_row(v["a_norm_w"][0]))
    put("kv_norm", by_row(v["kv_norm_w"]))
    put("b_norm", by_row(v["b_norm_w"][0]))
    for n in (0, 1):
        put(f"mem_norm{n}", by_row(v["mem_norm_w"][n]))
        put(f"ffn_norm{n}", by_row(v["ffn_norm_w"][n]))
        put(f"route_b{n}", np.concatenate([v["router_group_b"][n], v["router_expert_b"][n]])[None, :])
        put(f"route_w{n}", by_row(np.concatenate([v["router_group_w"][n], v["router_expert_w"][n]], axis=1)))
    put("conv_w", np.asarray(v["a_conv_w"][0]).reshape(4, NCONV, P).transpose(2, 1, 0).reshape(P, NCONV * 4))
    put("conv_b", np.asarray(v["a_conv_b"][0]).reshape(NCONV, P).T)
    put("gnorm", np.asarray(v["a_gnorm_w"][0]).reshape(INNER // P, P).T)
    put("dt_bias", np.asarray(v["a_dt_bias"][0])[None, :])
    put("a_log", np.asarray(v["a_a_log"][0])[None, :])
    put("d_skip", np.asarray(v["a_d_skip"][0])[None, :])
    put("sinks", np.asarray(v["b_sinks"][0])[None, :])
    put("dt_w", by_row(np.asarray(v["a_in_w"][0])[:, INNER + CONV_CH:INNER + CONV_CH + SSD_HEADS]))
    return a


def kernel(**inputs):
    import concourse.bacc as bacc
    from concourse.bass_utils import run_bass_kernel_spmd

    nc = bacc.Bacc("TRN2", target_bir_lowering=False, num_devices=1)
    arrays = {name: np.ascontiguousarray(inputs[name]) for name in INPUTS}
    arrays["small"] = pack_small({k: np.asarray(x) for k, x in inputs.items()})
    aps = {}
    for name, a in arrays.items():
        aps[name] = nc.dram_tensor(f"in_{name}", a.shape, mybir.dt.from_np(a.dtype), kind="ExternalInput").ap()
    out = nc.dram_tensor("out", (1, SEQ, D), F32, kind="ExternalOutput").ap()
    build(nc, aps, out)
    result = run_bass_kernel_spmd(nc, [{f"in_{name}": a for name, a in arrays.items()}], core_ids=[0])
    return result.results[0]["out"]
```

```python
from contextlib import ExitStack

import numpy as np

import concourse.bass as bass
from concourse import mybir

F32 = mybir.dt.float32
I32 = mybir.dt.int32
ALU = mybir.AluOpType
ACT = mybir.ActivationFunctionType
X = mybir.AxisListType.X

P = 128
D = 1024
KD = D // P
SEQ = 256
NT = SEQ // P
EPS = 1e-6
SSD_HEADS, SSD_GROUPS, HP = 24, 4, 64
HG = SSD_HEADS // SSD_GROUPS
INNER = SSD_HEADS * HP
GW = INNER // SSD_GROUPS
CONV_CH = INNER + 2 * SSD_GROUPS * P
NCONV = CONV_CH // P
MEM_HEADS = 4
MEM_SCALE = float(P) ** -0.5
Q_HEADS, KV_HEADS, HD, HALF_ROT = 16, 4, 64, 8
ATT_SCALE = float(HD) ** -0.5
NG, EG = 4, 8
NE = NG * EG
DE = D // 2
NEG = -1e30
SLOTS = 6
WT = 4096
TOKS = 64
ROUNDS = SEQ // TOKS
NBANK = 8

FIELDS = [("ident", P), ("tri", P), ("ones", P), ("iota", ROUNDS * TOKS), ("band_prev", P), ("band_cur", P),
          ("index8", EG), ("cos", NT * 16), ("sin", NT * 16),
          ("a_norm", KD), ("mem_norm0", KD), ("mem_norm1", KD), ("kv_norm", KD), ("b_norm", KD),
          ("ffn_norm0", KD), ("ffn_norm1", KD), ("conv_w", NCONV * 4), ("conv_b", NCONV), ("gnorm", INNER // P),
          ("dt_bias", SSD_HEADS), ("a_log", SSD_HEADS), ("d_skip", SSD_HEADS), ("sinks", Q_HEADS),
          ("route_b0", NG + NE), ("route_b1", NG + NE), ("route_w0", KD * (NG + NE)), ("route_w1", KD * (NG + NE)),
          ("dt_w", KD * SSD_HEADS)]
AT = {}
_n = 0
for _f, _w in FIELDS:
    AT[_f] = (_n, _w)
    _n += _w
SMALL = _n

TILES_A, TILES_B = 15, 7
B0 = TILES_A
FIRST_SLOT = [TILES_A % SLOTS, (TILES_A + TILES_B) % SLOTS]


def cut(ap, **sizes):
    (name, size), = sizes.items()
    return ap.rearrange(f"p ({name} z) -> p {name} z", **{name: size})


def spread_last(ap, n):
    return ap.rearrange("p (a o) -> p a o", o=1).broadcast_to([ap.shape[0], ap.shape[1], n])


def spread_mid(ap, n):
    return ap.rearrange("p (o a) -> p o a", o=1).broadcast_to([ap.shape[0], n, ap.shape[1]])


class Core:

    def __init__(self, nc, ins, out, ctx):
        self.nc, self.ins, self.out, self.ctx = nc, ins, out, ctx
        self.ring = self.sb("ring", SLOTS * WT)
        self.small = self.sb("small", SMALL)
        self.h = self.sb("h", NT * D)
        self.xs = self.sb("xs", NT * D)
        self.norm_ss = self.sb("norm_ss", 8)
        self.norm_r = self.sb("norm_r", 8)
        self.pos = self.sb("pos", NT * NE)
        self.gates = self.sb("gates", NT * NE)
        self.most = ctx.enter_context(nc.sbuf_tensor("most", [P, 1], I32))
        self.banks = [ctx.enter_context(nc.psum_tensor(f"bank{i}", [P, 512], F32)) for i in range(NBANK)]
        self.units_done = self.sem("units_done")
        self.w_loaded = [self.sem(f"w_loaded{i}") for i in range(SLOTS)]
        self.late = self.sb("late", 2 * WT)
        self.late_loaded = self.sem("late_loaded")
        self.first_unit = 0
        self.of_stage = {}

    def sb(self, name, n, ctx=None):
        return (ctx or self.ctx).enter_context(self.nc.sbuf_tensor(name, [P, n], F32))

    def carve_late(self, *sizes):
        assert sum(sizes) <= 2 * WT
        return [self.late[:, sum(sizes[:i]):sum(sizes[:i + 1])] for i in range(len(sizes))]

    def memory_weights(self, i):
        return self.ins["mem_w_kv"][1].rearrange("(p k) c -> p k c", k=KD)[:, :, 512 * i:512 * i + 512]

    def sem(self, name):
        return self.ctx.enter_context(self.nc.semaphore(name))

    def sems(self, stage, names):
        for n in names.split():
            if (stage, n) not in self.of_stage:
                self.of_stage[stage, n] = self.sem(f"{stage}_{n}")
        return {n: self.of_stage[stage, n] for n in names.split()}

    def clear(self, eng, *stages):
        for (stage, _), sem in self.of_stage.items():
            if stage in stages:
                eng.sem_clear(sem)

    def f(self, name, a=0, b=None):
        at, w = AT[name]
        return self.small[:, at + a:at + (w if b is None else b)]

    def slot(self, n):
        s = n % SLOTS
        return self.ring[:, s * WT:(s + 1) * WT]

    def cols_tile(self, n):
        return cut(self.slot(n), k=KD)

    def rows_tile(self, n):
        return cut(self.slot(n), j=4)

    def wait_tile(self, eng, n):
        eng.wait_ge(self.w_loaded[n % SLOTS], 16 * (n // SLOTS + 1))

    def source(self, n):
        def cols(w, i):
            return w.rearrange("(p k) c -> p k c", k=KD)[:, :, 512 * i:512 * i + 512]

        def rows(w, i):
            return w[512 * i:512 * i + 512, :].rearrange("(j p) c -> p j c", p=P)

        g = self.ins
        if n < TILES_A:
            in_w, mem_kv, out_w = g["a_in_w"][0], g["mem_w_kv"][0], g["a_out_w"][0]
            at_q = INNER + CONV_CH + SSD_HEADS
            if n < 5:
                return cols(in_w[:, INNER:], n)
            if n < 8:
                return cols(in_w, n - 5)
            if n == 8:
                return cols(in_w[:, at_q:at_q + 512], 0)
            if n < 11:
                return cols(mem_kv, n - 9)
            return rows(out_w, (n - 11 + 3) % 4)
        n -= B0
        in_w, out_w = g["b_in_w"][0], g["b_out_w"][0]
        if n == 0:
            return cols(g["w_kv"], 0)
        if n < 4:
            return cols(in_w, n - 1)
        return rows(out_w, (n - 4 + 2) % 3)

    def load_mixer_tile(self, sp, n):
        src = self.source(n)
        dst = self.rows_tile(n) if src.shape[1] == 4 else self.cols_tile(n)
        sp.dma_start(dst, src).then_inc(self.w_loaded[n % SLOTS], 16)


class Units:

    def __init__(self, core, order, freed, holds=None):
        self.core, self.freed = core, freed
        holds = holds or {}
        units = [key for key in order if key not in holds]
        self.at = {key: core.first_unit + i for i, key in enumerate(units)}
        assert len(self.at) == len(units)
        core.first_unit += len(units)
        held = [key for keys in holds.values() for key in keys]
        free, user, self.of, self.before = list(range(NBANK)), {}, {}, {}
        for key in order:
            for k in holds.get(key, [key]):
                if k not in self.of:
                    bank = self.of[k] = free.pop(0)
                    self.before[k] = user.get(bank)
                    user[bank] = k
                    if k not in held:
                        free.append(bank)
            if held and key == held[-1]:
                free += [self.of[k] for k in held]

    def bank(self, key):
        return self.core.banks[self.of[key]]

    def wait_free(self, pe, key):
        if self.before[key]:
            pe.wait_ge(*self.freed(*self.before[key]))

    def wait_done(self, eng, key):
        eng.wait_ge(self.core.units_done, self.at[key] + 1)


def transposes(c, pe, out, blocks, last_inc=True):
    for i, block in enumerate(blocks):
        ins = pe.transpose(out[:, i * P:(i + 1) * P], block, c.f("ident"))
    if last_inc:
        ins.then_inc(c.units_done, 1)


def attend_scores(c, pe, out, qT, kT, h):
    for t in range(NT):
        ins = pe.matmul(out[:, t * 256:(t + 1) * 256], cut(qT, h=4)[:, h, t * P:(t + 1) * P], cut(kT, h=4)[:, h, :],
                        start=True, stop=True)
    ins.then_inc(c.units_done, 1)


def attend_values(c, pe, out, v, pT, h):
    for m in range(2):
        ins = pe.matmul(out[:, 0:256], cut(v, m=2)[:, m, h * P:(h + 1) * P], cut(pT, m=2)[:, m, :],
                        start=(m == 0), stop=(m == 1))
    ins.then_inc(c.units_done, 1)


def memory_rows(c, pe, U, s, mT, n, h):
    if h == 0:
        for q in range(4):
            U.wait_free(pe, ("out", q))
        c.wait_tile(pe, n)
    pe.wait_ge(s["pv_ev"], h + 1)
    for q in range(4):
        ins = pe.matmul(U.bank(("out", q))[:, :], cut(mT, h=4)[:, h, (q // 2) * P:(q // 2) * P + P],
                        c.rows_tile(n)[:, h, 512 * (q % 2):512 * (q % 2) + 512], start=(h == 0), stop=False)
    if h == 3:
        ins.then_inc(s["out_tile"], 1)


def out_rows(c, pe, U, s, src, n, tiles, t):
    for m in range(tiles):
        if t == 0:
            c.wait_tile(pe, n + m)
        for j in range(4):
            for half in range(2):
                last = m == tiles - 1 and j == 3
                ins = pe.matmul(U.bank(("out", 2 * t + half))[:, :], src(4 * m + j), c.rows_tile(n + m)[:, j, 512 * half:512 * half + 512],
                                start=False, stop=last)
                if last:
                    ins.then_inc(c.units_done, 1)
        if t == 1 and m < tiles - 1:
            ins.then_inc(s["out_tile"], 1)


def project(c, pe, out, lhsT, rhs, n=KD):
    for k in range(n):
        ins = pe.matmul(out, lhsT(k), rhs(k), start=(k == 0), stop=(k == n - 1))
    ins.then_inc(c.units_done, 1)


class Norm:

    def __init__(self, c, src, at, by_act, by_dve, xs=None):
        self.c, self.src, self.by_act, self.by_dve = c, cut(src, t=NT), by_act, by_dve
        self.xs = cut((c.xs if xs is None else xs)[:, :], t=NT)
        self.ss, self.r = ([v[:, at + t:at + t + 1] for t in range(NT)] for v in (c.norm_ss, c.norm_r))

    def warm(self, act):
        act.activation(self.c.norm_r[:, 6:7], self.c.norm_ss[:, 4:5], ACT.Sqrt)

    def act(self, act, t, steps=3):
        act.activation(self.xs[:, t, :], self.src[:, t, :], ACT.Square, accum_out=self.ss[t]).then_inc(self.by_act, 1)
        act.wait_ge(self.by_dve, steps * t + 1)
        act.activation(self.r[t], self.ss[t], ACT.Sqrt).then_inc(self.by_act, 1)

    def dve(self, dve, t):
        dve.wait_ge(self.by_act, 2 * t + 1)
        dve.tensor_scalar(self.ss[t], self.ss[t], 1.0 / D, EPS, ALU.mult, ALU.add).then_inc(self.by_dve, 1)
        dve.wait_ge(self.by_act, 2 * t + 2)
        dve.reciprocal(self.r[t], self.r[t]).then_inc(self.by_dve, 1)
        dve.wait_ge(self.by_dve, 3 * t + 2)
        dve.tensor_scalar(self.xs[:, t, :].rearrange("q (k p) -> q p k", k=KD), self.src[:, t, :].rearrange("q (p k) -> q p k", k=KD),
                          self.r[t], None, ALU.mult).then_inc(self.by_dve, 1)


def finish_h(c, dve, t, signal):
    for q in (2 * t, 2 * t + 1):
        hq = c.h[:, 512 * q:512 * q + 512]
        dve.tensor_tensor(hq, hq, c.banks[q][:, :], ALU.add).then_inc(signal, 1)


def norm_T_units(c, pe, out, i, xs=None):
    xs = (c.xs if xs is None else xs)[:, :].rearrange("q (t k p) -> q t k p", t=NT, k=KD)
    transposes(c, pe, out, [xs[:, t, 2 * i + kk, :] for kk in range(2) for t in range(NT)])



class Router:

    NORMED = [("x2T", 0), ("x2T", 1), ("router", 0)]
    UNITS = NORMED + [("x2T", 2), ("x2T", 3), ("router", 1), ("places", 0)]
    SEMS = "h_new n2_act n2_dve x2T_ev rw_ready rt_dve rt_act"
    KINDS = ("x2T", "router", "places")
    LOGITS, GROUP_LOGITS, MASK, TOP_TWO, PLACES = 2, 4, 25, 26, 39

    def __init__(self, c, U, s, layer, xnT, work):
        self.c, self.U, self.s, self.layer, self.xnT = c, U, s, layer, xnT
        self.norm = Norm(c, c.h, 4, s["n2_act"], s["n2_dve"])
        w = [NT * (NG + NE), NT * NG, NT * NE, NT * NG] + [NT * EG] * 5 + [16 * NT, NT * NE, 1]
        (self.lg, self.ge, self.sel, self.g1, self.ig, self.ig2, self.eq, self.o1, self.o2, self.col, self.mask,
         self.mf) = (work[:, sum(w[:i]):sum(w[:i + 1])] for i in range(len(w)))

    @staticmethod
    def freed(s, kind, i):
        return {"x2T": (s["x2T_ev"], i + 1), "router": (s["rt_dve"], i + 1), "places": (s["rt_dve"], Router.PLACES)}[kind]

    def pool(self, pool):
        c, w = self.c, self.c.f(f"route_w{self.layer}")
        pool.tensor_tensor(cut(w, k=KD), cut(w, k=KD), spread_last(c.f(f"ffn_norm{self.layer}"), NG + NE), ALU.mult).then_inc(self.s["rw_ready"], 1)

    def act(self, act, key):
        c, U, s = self.c, self.U, self.s
        kind, i = key
        if kind == "out" and i % 2:
            act.wait_ge(s["h_new"], i + 1)
            self.norm.act(act, i // 2)
        elif kind == "x2T":
            U.wait_done(act, key)
            act.activation(cut(self.xnT, k=KD)[:, 4 * (i % 2):4 * (i % 2) + 4, P * (i // 2):P * (i // 2) + P], cut(U.bank(key), k=4),
                           ACT.Copy).then_inc(s["x2T_ev"], 1)
        elif kind == "places":
            act.wait_ge(s["rt_dve"], self.GROUP_LOGITS)
            act.activation(self.ge[:, :], self.ge[:, :], ACT.Exp).then_inc(s["rt_act"], 1)
            act.wait_ge(s["rt_dve"], self.TOP_TWO)
            act.activation(self.col[:, 16:18], self.col[:, 14:16], ACT.Exp).then_inc(s["rt_act"], 1)

    def pe(self, pe, key):
        c, U, s = self.c, self.U, self.s
        kind, i = key
        out = U.bank(key)
        if kind == "x2T":
            t, half = i // 2, i % 2
            pe.wait_ge(s["n2_dve"], 3 * t + 3)
            xs = c.xs[:, :].rearrange("q (t k p) -> q t k p", t=NT, k=KD)
            transposes(c, pe, out, [xs[:, t, 4 * half + k, :] for k in range(4)])
        elif kind == "router":
            pe.wait_ge(s["x2T_ev"], 2 * i + 2)
            pe.wait_ge(s["rw_ready"], 1)
            for k in range(KD):
                ins = pe.matmul(out[:, 0:NG + NE], cut(self.xnT, k=KD)[:, k, i * P:(i + 1) * P],
                                cut(c.f(f"route_w{self.layer}"), k=KD)[:, k, :], start=(k == 0), stop=(k == KD - 1))
            ins.then_inc(c.units_done, 1)
        else:
            pe.wait_ge(s["rt_dve"], self.MASK)
            m = cut(self.mask, t=NT)
            pe.matmul(out[:, 0:NE], c.f("tri"), m[:, 0, :], start=True, stop=True)
            pe.matmul(out[:, NE:2 * NE], c.f("ones"), m[:, 0, :], start=True, stop=False)
            pe.matmul(out[:, NE:2 * NE], c.f("tri"), m[:, 1, :], start=False, stop=True)
            pe.matmul(out[:, 2 * NE:3 * NE], c.f("ones"), m[:, 0, :], start=True, stop=False)
            pe.matmul(out[:, 2 * NE:3 * NE], c.f("ones"), m[:, 1, :], start=False, stop=True).then_inc(c.units_done, 1)

    def dve(self, dve, key):
        c, U, s = self.c, self.U, self.s
        kind, i = key
        if kind == "out":
            U.wait_done(dve, key)
            hq = c.h[:, 512 * i:512 * i + 512]
            dve.tensor_tensor(hq, hq, U.bank(key)[:, :], ALU.add).then_inc(s["h_new"], 1)
            if i % 2:
                self.norm.dve(dve, i // 2)
        elif kind == "router":
            U.wait_done(dve, key)
            dve.tensor_tensor(cut(self.lg, t=NT)[:, i, :], U.bank(key)[:, 0:NG + NE], c.f(f"route_b{self.layer}"), ALU.add).then_inc(s["rt_dve"], 1)
            if i == NT - 1:
                self.choose(dve)

    def choose(self, dve):
        c, U, s = self.c, self.U, self.s
        n = [self.LOGITS]

        def step(ins, used_next=True):
            n[0] += 1
            ins.then_inc(s["rt_dve"], 1)
            if used_next:
                dve.wait_ge(s["rt_dve"], n[0])

        dve.wait_ge(s["rt_dve"], self.LOGITS)
        col = self.col
        gm, gi, m1, m2, i1, i2, gs, dd, ed, w1, w2 = (col[:, 2 * i:2 * i + 2] for i in range(11))
        lg, ge, g1, ig, ig2, eq, o1, o2 = (cut(v, t=NT) for v in (self.lg, self.ge, self.g1, self.ig, self.ig2, self.eq,
                                                                  self.o1, self.o2))
        sel, mask, gates, pos = cut(self.sel, t=NT), cut(self.mask, t=NT), cut(c.gates, t=NT), cut(c.pos, t=NT)
        index4, index8 = spread_mid(c.f("index8", 0, NG), NT), spread_mid(c.f("index8"), NT)
        step(dve.tensor_reduce(gm, lg[:, :, 0:NG], X, ALU.max))
        step(dve.tensor_tensor(ge, lg[:, :, 0:NG], spread_last(gm, NG), ALU.subtract), used_next=False)
        assert n[0] == self.GROUP_LOGITS
        step(dve.tensor_tensor(g1, lg[:, :, 0:NG], spread_last(gm, NG), ALU.is_ge))
        step(dve.tensor_tensor(g1, g1, index4, ALU.mult))
        step(dve.tensor_reduce(gi, g1, X, ALU.min))
        step(dve.tensor_tensor(g1, index4, spread_last(gi, NG), ALU.is_equal))
        for t in range(NT):
            step(dve.tensor_tensor(cut(sel[:, t, :], g=NG), cut(lg[:, t, NG:], g=NG), spread_last(g1[:, t, :], EG), ALU.mult), t == NT - 1)
        step(dve.tensor_reduce(ig, self.sel[:, :].rearrange("p (t g e) -> p t e g", t=NT, g=NG), X, ALU.add))
        for m, i_, o, src in ((m1, i1, o1, ig), (m2, i2, o2, ig2)):
            step(dve.tensor_reduce(m, src, X, ALU.max))
            step(dve.tensor_tensor(eq, src, spread_last(m, EG), ALU.is_ge))
            step(dve.tensor_tensor(eq, eq, index8, ALU.mult))
            step(dve.tensor_reduce(i_, eq, X, ALU.min))
            step(dve.tensor_tensor(o, index8, spread_last(i_, EG), ALU.is_equal))
            if src is ig:
                step(dve.scalar_tensor_tensor(out=self.ig2[:, :], in0=self.o1[:, :], scalar=NEG, in1=self.ig[:, :],
                                              op0=ALU.mult, op1=ALU.add))
        step(dve.tensor_tensor(eq, o1, o2, ALU.add))
        for t in range(NT):
            step(dve.tensor_tensor(cut(mask[:, t, :], g=NG), spread_last(g1[:, t, :], EG), spread_mid(eq[:, t, :], NG), ALU.mult), False)
        assert n[0] == self.MASK
        step(dve.tensor_tensor(dd, m2, m1, ALU.subtract))
        assert n[0] == self.TOP_TWO
        dve.wait_ge(s["rt_act"], 1)
        step(dve.tensor_reduce(gs, ge, X, ALU.add))
        step(dve.reciprocal(gs, gs), used_next=False)
        dve.wait_ge(s["rt_act"], 2)
        step(dve.tensor_scalar(w2, ed, 1.0, None, ALU.add))
        step(dve.reciprocal(w1, w2))
        step(dve.tensor_tensor(w1, w1, gs, ALU.mult))
        step(dve.tensor_tensor(w2, w1, ed, ALU.mult), used_next=False)
        step(dve.tensor_tensor(o1, o1, spread_last(w1, EG), ALU.mult))
        step(dve.tensor_tensor(o2, o2, spread_last(w2, EG), ALU.mult))
        step(dve.tensor_tensor(ig, o1, o2, ALU.add))
        for t in range(NT):
            step(dve.tensor_tensor(cut(gates[:, t, :], g=NG), spread_last(g1[:, t, :], EG), spread_mid(ig[:, t, :], NG), ALU.mult), False)
        key = ("places", 0)
        U.wait_done(dve, key)
        step(dve.tensor_reduce(self.mf[:, :], U.bank(key)[:, 2 * NE:3 * NE], X, ALU.max))
        step(dve.tensor_tensor(pos[:, :, :], cut(U.bank(key)[:, 0:NT * NE], t=NT), mask, ALU.mult), used_next=False)
        assert n[0] == self.PLACES
        dve.tensor_copy(c.most[:, :], self.mf[:, :])


def mixer_a(c):
    ctx = ExitStack()
    g = c.ins
    names = ("x_act x_dve xT_ev dt_dve dt_act conv_dve conv_act z_ev q_ev m_act m_dve memT_ev mk_ev mv_ev xtok_ev bt_ev "
             "ac_dve ac_act cb_dve seg_dve exp_act m_dve2 pool_x st_ev y_dve sm_max sm_dve sm_act pt_ev pv_ev g_act g_dve yT_act yT_dve "
             "out_tile " + Router.SEMS)
    s = c.sems("mixer", names)
    ld_small = c.sem("ld_small")
    ld_x, ld_mem = ([c.sem(f"ld_{n}{t}") for t in range(NT)] for n in ("x", "mem"))
    with ctx:
        sb = lambda name, n: c.sb("a_" + name, n, ctx)
        xbcT = sb("xbcT", NCONV * SEQ)
        zs, xtok, xdt, xd, bt = c.carve_late(NT * INNER, NT * INNER, 2 * GW, 2 * GW, 512)
        xdt, xd = ([v[:, i * GW:(i + 1) * GW] for i in range(2)] for v in (xdt, xd))
        xnT, memnT = sb("xnT", KD * SEQ), sb("memnT", KD * SEQ)
        mem = memnT
        mkT, mv, qT = sb("mkT", 1024), sb("mv", 1024), sb("qT", 1024)
        mT = qT
        acc = sb("acc", 3 * SEQ)
        E = [c.xs[:, GW * i:GW * i + GW] for i in range(4)]
        yt = c.xs[:, 4 * GW:5 * GW]
        cbm = [sb(f"cbm{i}", P) for i in range(2)]
        xw = [acc[:, i * GW:(i + 1) * GW] for i in range(2)]
        sq = xw
        state, ex, pTs = xbcT[:, 0:4 * GW], [xbcT[:, 4 * GW + 512 * i:4 * GW + 512 * i + 512] for i in range(2)], xbcT[:, 4 * GW + 1024:4 * GW + 1536]
        yT = xbcT[:, 0:12 * SEQ]
        dtb = [sb(f"dt{i}", 2 * SSD_HEADS) for i in range(6)]
        dtx, t_, s_, s2, dt, adt = dtb
        ea, eac, toend, acum = sb("ea", 24), sb("eac", 24), sb("toend", 24), sb("acum", 48)
        smc = sb("smc", 64)
        gss = sb("gss", 8)

        steps = [(ch, gr) for ch in range(NT) for gr in range(SSD_GROUPS)]
        order = [("xT", i) for i in range(4)] + [("dt", 0)]
        order += [("conv", j) for j in range(NCONV)]
        order += [("z", 0), ("xtok", 0), ("xtok", 1), ("xtok", 2), ("bt", 0), ("ac", 0), ("z", 1), ("xtok", 3), ("xtok", 4), ("xtok", 5)]
        order += [("z", 2)] + [("memT", i) for i in range(4)] + [("z", 3), ("z", 4)]
        between = [[("z", 5)], [("q", 0)], [("q", 1)], [("q", 2), ("q", 3)], [("mk", 0)], [("mv", 0), ("sc", 0)], [("mv", 1), ("pT", 0)],
                   [("mk", 1), ("pv", 0), ("sc", 1)], [("mk", 2), ("pT", 1), ("sc", 2)]]
        for i in range(len(steps) + 1):
            if i < 8:
                order += [("cb", i), ("A", 2 * i), ("A", 2 * i + 1)]
            order += between[i]
            if i >= 1:
                order += [("st", i - 1)] if i <= 4 else [("yo", i - 5)]
                order += [("yd", i - 1)]
        order += [("mk", 3), ("pv", 1), ("pT", 2), ("sc", 3), ("pv", 2), ("outm", 0), ("pT", 3), ("outm", 1), ("pv", 3), ("outm", 2), ("outm", 3)]
        order += [("yT", i) for i in range(8)] + [("out", i) for i in range(4)] + Router.UNITS
        holds = {("outm", h): [("out", i) for i in range(4)] for h in range(4)}

        def freed(kind, i):
            if kind in Router.KINDS:
                return Router.freed(s, kind, i)
            if kind == "yT":
                return s["yT_dve" if i % 2 else "yT_act"], i // 2 + 1 if i % 2 else 3 * (i // 2) + 3
            return {"xT": (s["xT_ev"], 2 * i + 2), "dt": (s["dt_dve"], 1), "conv": (s["conv_dve"], 4 * i + 4),
                    "xtok": (s["xtok_ev"], i + 1), "bt": (s["bt_ev"], 1), "ac": (s["ac_dve"], 2), "z": (s["z_ev"], i + 1),
                    "q": (s["q_ev"], i + 1), "memT": (s["memT_ev"], 2 * i + 2), "mk": (s["mk_ev"], i + 1),
                    "mv": (s["mv_ev"], i + 1), "cb": (s["cb_dve"], i + 1), "A": (s["seg_dve"], 3 * i + 3),
                    "sc": (s["sm_act"], 2 * i + 2), "pT": (s["pt_ev"], i + 1), "pv": (s["pv_ev"], i + 1),
                    "st": (s["st_ev"], i + 1), "yo": (s["y_dve"], 8 + 4 * i + 1),
                    "yd": (s["y_dve"], 2 * i + 1 if i < 4 else 8 + 4 * (i - 4) + 2),
                    "out": (s["h_new"], i + 1)}[kind]

        U = Units(c, order, freed, holds)
        R = Router(c, U, s, 0, xnT, memnT)

        def tile_used(n):
            if n < 5:
                return c.units_done, U.at["conv", 4 * n + 3] + 1
            if n < 8:
                return c.units_done, U.at["z", 2 * (n - 5) + 1] + 1
            last = {8: ("q", 3), 9: ("mk", 3), 10: ("mv", 1)}
            if n in last:
                return c.units_done, U.at[last[n]] + 1
            if n < 14:
                return s["out_tile"], n - 10
            return c.units_done, U.at["out", 3] + 1

        def heads(ap, n=HG):
            return cut(ap, h=n)

        x_norm = Norm(c, c.h, 0, s["x_act"], s["x_dve"])
        mem_norm = Norm(c, mem, 2, s["m_act"], s["m_dve"])
        squares_at = {("yd", 5): [0, 1, 2], ("yd", 6): [3, 4], ("yd", 7): [5], ("outm", 0): [6, 7]}
        first_pair = first_pair_loader(c, 0)
        block = ctx.enter_context(c.nc.Block())

        @block.sync
        def _(sp):
            for t in range(NT):
                sp.dma_start(cut(c.h, t=NT)[:, t, :], g["x"][0, t * P:(t + 1) * P, :]).then_inc(ld_x[t], 16)
            sp.dma_start(c.small[:, :], g["small"]).then_inc(ld_small, 16)
            for n in range(2):
                c.load_mixer_tile(sp, n)
            for t in range(NT):
                sp.dma_start(cut(mem, t=NT)[:, t, :], g["mem"][0, t * P:(t + 1) * P, :]).then_inc(ld_mem[t], 16)
            for n in range(2, TILES_A + SLOTS):
                if n == TILES_A + 3:
                    sp.wait_ge(c.units_done, U.at["yT", 7] + 1)
                    for i in range(2):
                        sp.dma_start(cut(c.late[:, WT * i:WT * i + WT], k=KD), c.memory_weights(i)).then_inc(c.late_loaded, 16)
                if n >= SLOTS:
                    sp.wait_ge(*tile_used(n - SLOTS))
                if n < TILES_A:
                    c.load_mixer_tile(sp, n)
                else:
                    first_pair(sp, n - TILES_A)

        @block.scalar
        def _(act):
            for t in range(NT):
                act.wait_ge(ld_x[t], 16)
                x_norm.act(act, t)
            for key in order:
                kind, i = key
                if kind in ("out",) + Router.KINDS:
                    R.act(act, key)
                    continue
                if key in squares_at:
                    act.wait_ge(c.units_done, U.at["st", 3] + 1)
                    for st in squares_at[key]:
                        act.wait_ge(s["y_dve"], 2 * st + 2 if st < 4 else 8 + 4 * (st - 4) + 4)
                        if st >= 2:
                            act.wait_ge(s["g_act"], st - 1)
                        act.activation(sq[st % 2], cut(zs, t=NT)[:, st // 4, GW * (st % 4):GW * (st % 4) + GW], ACT.Square,
                                       accum_out=gss[:, st:st + 1]).then_inc(s["g_act"], 1)
                if key == ("outm", 1):
                    act.wait_ge(s["g_dve"], 1)
                    act.activation(gss[:, :], gss[:, :], ACT.Sqrt).then_inc(s["g_act"], 1)
                if kind == "outm":
                    continue
                bank = U.bank(key)
                if kind in ("xT", "memT"):
                    U.wait_done(act, key)
                    if i == 0:
                        if kind == "xT":
                            act.wait_ge(ld_small, 16)
                        else:
                            act.wait_ge(s["m_dve"], 6)
                    dst, w = (xnT, "a_norm") if kind == "xT" else (memnT, "mem_norm0")
                    for kk in range(2):
                        k = 2 * i + kk
                        act.activation(cut(dst, k=KD)[:, k, :], bank[:, kk * 256:(kk + 1) * 256], ACT.Copy,
                                       scale=c.f(w, k, k + 1)).then_inc(s[kind + "_ev"], 1)
                elif kind == "dt":
                    act.wait_ge(s["dt_dve"], 2)
                    act.activation(t_[:, :], t_[:, :], ACT.Exp, scale=-1.0).then_inc(s["dt_act"], 1)
                    act.activation(ea[:, :], c.f("a_log"), ACT.Exp).then_inc(s["dt_act"], 1)
                elif kind == "conv":
                    act.wait_ge(s["conv_dve"], 4 * i + 4)
                    act.activation(cut(xbcT, j=NCONV)[:, i, :], cut(acc, b=3)[:, i % 3, :], ACT.Silu).then_inc(s["conv_act"], 1)
                elif kind == "z":
                    U.wait_done(act, key)
                    act.activation(cut(zs, t=NT)[:, i % 2, 512 * (i // 2):512 * (i // 2) + 512], bank[:, :], ACT.Silu).then_inc(s["z_ev"], 1)
                elif kind == "xtok":
                    U.wait_done(act, key)
                    act.activation(cut(xtok, t=NT)[:, i // 3, 512 * (i % 3):512 * (i % 3) + 512], bank[:, :], ACT.Copy).then_inc(s["xtok_ev"], 1)
                elif kind == "bt":
                    U.wait_done(act, key)
                    act.activation(bt[:, :], bank[:, :], ACT.Copy).then_inc(s["bt_ev"], 1)
                elif kind == "ac":
                    act.wait_ge(s["ac_dve"], 2)
                    act.activation(eac[:, :], acum[:, 24:48], ACT.Exp).then_inc(s["ac_act"], 1)
                    act.activation(toend[:, :], toend[:, :], ACT.Exp).then_inc(s["ac_act"], 1)
                elif kind == "q":
                    U.wait_done(act, key)
                    act.activation(cut(qT, h=4)[:, i, :], bank[:, 0:256], ACT.Copy).then_inc(s["q_ev"], 1)
                elif kind == "mk":
                    U.wait_done(act, key)
                    act.activation(cut(mkT, h=4)[:, i, :], bank[:, 0:256], ACT.Copy).then_inc(s["mk_ev"], 1)
                elif kind == "mv":
                    U.wait_done(act, key)
                    act.activation(cut(mv, m=2)[:, i, :], bank[:, :], ACT.Copy).then_inc(s["mv_ev"], 1)
                elif kind == "A":
                    act.wait_ge(s["seg_dve"], 3 * i + 3)
                    act.activation(E[i % 4][:, :], E[i % 4][:, :], ACT.Exp).then_inc(s["exp_act"], 1)
                elif kind == "st":
                    U.wait_done(act, key)
                    act.activation(cut(state, g=4)[:, i, :], bank[:, 0:GW], ACT.Copy).then_inc(s["st_ev"], 1)
                elif kind == "sc":
                    U.wait_done(act, key)
                    act.wait_ge(s["sm_max"], 2 * i + 2)
                    for t in range(NT):
                        act.activation(cut(ex[i % 2], t=NT)[:, t, :], cut(bank, t=NT)[:, t, :], ACT.Exp, scale=MEM_SCALE,
                                       bias=smc[:, 16 + 2 * i + t:17 + 2 * i + t],
                                       accum_out=smc[:, 32 + 2 * i + t:33 + 2 * i + t]).then_inc(s["sm_act"], 1)
                elif kind == "pT":
                    U.wait_done(act, key)
                    act.activation(pTs, bank[:, :], ACT.Copy).then_inc(s["pt_ev"], 1)
                elif kind == "pv":
                    U.wait_done(act, key)
                    act.activation(cut(mT, h=4)[:, i, :], bank[:, 0:256], ACT.Copy).then_inc(s["pv_ev"], 1)
                elif kind == "yT" and i % 2 == 0:
                    U.wait_done(act, key)
                    for b in range(3):
                        j = 3 * (i % 4) + b
                        act.activation(cut(yT, t=NT)[:, i // 4, j * P:(j + 1) * P], bank[:, b * P:(b + 1) * P], ACT.Copy,
                                       scale=c.f("gnorm", j, j + 1)).then_inc(s["yT_act"], 1)
                if key == ("z", 0):
                    act.wait_ge(c.units_done, U.at["xT", 3] + 1)
                    for t in range(NT):
                        act.wait_ge(ld_mem[t], 16)
                        mem_norm.act(act, t)

        @block.gpsimd
        def _(pool):
            n = [0]

            def step(ins):
                n[0] += 1
                ins.then_inc(s["pool_x"], 1)

            pool.wait_ge(ld_small, 16)
            R.pool(pool)
            pool.wait_ge(s["dt_dve"], 17)
            pool.wait_ge(s["ac_act"], 2)
            pool.wait_ge(s["conv_act"], NCONV)
            for st, (ch, gr) in enumerate(steps):
                pool.wait_ge(s["xtok_ev"], 3 * ch + 3)
                if st >= 2:
                    pool.wait_ge(c.units_done, U.at["yd", st - 2] + 1)
                    pool.wait_ge(s["y_dve"], 2 * (st - 2) + 1 if st - 2 < 4 else 8 + 4 * (st - 6) + 3)
                x = cut(xtok, t=NT)[:, ch, GW * gr:GW * gr + GW]
                step(pool.tensor_tensor(heads(xdt[st % 2][:, :]), heads(x),
                                        spread_last(cut(dt, t=NT)[:, ch, HG * gr:HG * gr + HG], HP), ALU.mult))
                if ch == 0:
                    pool.wait_ge(s["pool_x"], n[0])
                    step(pool.tensor_tensor(heads(xw[st % 2][:, :]), heads(xdt[st % 2][:, :]),
                                            spread_last(toend[:, HG * gr:HG * gr + HG], HP), ALU.mult))
                step(pool.tensor_tensor(heads(xd[st % 2][:, :]), heads(x),
                                        spread_last(c.f("d_skip", HG * gr, HG * gr + HG), HP), ALU.mult))

        def pool_done(st, what):
            base = 3 * st if st < 4 else 12 + 2 * (st - 4)
            return base + {"xdt": 1, "xw": 2, "xd": 3 if st < 4 else 2}[what]

        @block.tensor
        def _(pe):
            for key in order:
                kind, i = key
                if kind == "outm":
                    memory_rows(c, pe, U, s, mT, TILES_A - 4, i)
                    continue
                out = U.bank(key)
                if kind != "out":
                    U.wait_free(pe, key)
                if kind == "xT":
                    if i == 0:
                        pe.wait_ge(ld_small, 16)
                        pe.wait_ge(s["x_dve"], 6)
                    norm_T_units(c, pe, out, i)
                elif kind == "memT":
                    if i == 0:
                        pe.wait_ge(s["m_dve"], 6)
                    norm_T_units(c, pe, out, i)
                elif kind == "dt":
                    pe.wait_ge(s["xT_ev"], 8)
                    for t in range(NT):
                        for k in range(KD):
                            ins = pe.matmul(out[:, 24 * t:24 * t + 24], cut(xnT, k=KD)[:, k, t * P:(t + 1) * P],
                                            cut(c.f("dt_w"), k=KD)[:, k, :], start=(k == 0), stop=(k == KD - 1))
                    ins.then_inc(c.units_done, 1)
                elif kind in ("conv", "q", "mk"):
                    n = {"conv": i // 4, "q": 8, "mk": 9}[kind]
                    if i % 4 == 0:
                        c.wait_tile(pe, n)
                    if kind == "mk" and i == 0:
                        pe.wait_ge(s["memT_ev"], 8)
                    w, x = c.cols_tile(n), cut(memnT if kind == "mk" else xnT, k=KD)
                    project(c, pe, out[:, 0:256], lambda k: w[:, k, P * (i % 4):P * (i % 4) + P], lambda k: x[:, k, :])
                elif kind in ("z", "mv"):
                    n = 5 + i // 2 if kind == "z" else 10
                    if i % 2 == 0:
                        c.wait_tile(pe, n)
                    w, x, t = c.cols_tile(n), cut(memnT if kind == "mv" else xnT, k=KD), i % 2
                    project(c, pe, out[:, :], lambda k: x[:, k, t * P:(t + 1) * P], lambda k: w[:, k, :])
                elif kind == "xtok":
                    ch, j = i // 3, 4 * (i % 3)
                    pe.wait_ge(s["conv_act"], j + 4)
                    transposes(c, pe, out, [cut(xbcT, j=NCONV)[:, j + q, ch * P:(ch + 1) * P] for q in range(4)])
                elif kind == "bt":
                    pe.wait_ge(s["conv_act"], NCONV)
                    transposes(c, pe, out, [cut(xbcT, j=NCONV)[:, 12 + q, 0:P] for q in range(4)])
                elif kind == "ac":
                    pe.wait_ge(s["dt_dve"], 17)
                    for ch in range(NT):
                        pe.matmul(out[:, 24 * ch:24 * ch + 24], c.f("tri"), cut(adt, t=NT)[:, ch, :], start=True, stop=True)
                    pe.matmul(out[:, 48:72], c.f("ones"), cut(adt, t=NT)[:, 0, :], start=True, stop=True).then_inc(c.units_done, 1)
                elif kind == "cb":
                    ch, gr = steps[i]
                    x = cut(xbcT, j=NCONV)
                    pe.matmul(out[:, 0:P], x[:, 12 + gr, ch * P:(ch + 1) * P], x[:, 16 + gr, ch * P:(ch + 1) * P],
                              start=True, stop=True).then_inc(c.units_done, 1)
                elif kind == "A":
                    ch, gr = steps[i // 2]
                    for hh in range(3):
                        hd = HG * gr + 3 * (i % 2) + hh
                        ins = pe.matmul(out[:, hh * P:(hh + 1) * P], cut(adt, t=NT)[:, ch, hd:hd + 1].broadcast_to([P, P]),
                                        c.f("tri"), start=True, stop=True)
                    ins.then_inc(c.units_done, 1)
                elif kind == "sc":
                    pe.wait_ge(s["q_ev"], i + 1)
                    pe.wait_ge(s["mk_ev"], i + 1)
                    attend_scores(c, pe, out, qT, mkT, i)
                elif kind == "pT":
                    pe.wait_ge(s["sm_dve"], 2 * i + 2)
                    transposes(c, pe, out, [cut(ex[i % 2], t=NT)[:, t, m * P:(m + 1) * P] for m in range(2) for t in range(NT)])
                elif kind == "pv":
                    pe.wait_ge(s["pt_ev"], i + 1)
                    pe.wait_ge(s["mv_ev"], 2)
                    attend_values(c, pe, out, mv, pTs, i)
                elif kind == "st":
                    pe.wait_ge(s["bt_ev"], 1)
                    pe.wait_ge(s["pool_x"], pool_done(i, "xw"))
                    pe.matmul(out[:, 0:GW], cut(bt, g=4)[:, i, :], xw[i % 2][:, :], start=True, stop=True).then_inc(c.units_done, 1)
                elif kind == "yo":
                    pe.wait_ge(s["st_ev"], i + 1)
                    pe.matmul(out[:, 0:GW], cut(xbcT, j=NCONV)[:, 16 + i, P:2 * P], cut(state, g=4)[:, i, :],
                              start=True, stop=True).then_inc(c.units_done, 1)
                elif kind == "yd":
                    pe.wait_ge(s["m_dve2"], 2 * i + 2)
                    pe.wait_ge(s["pool_x"], pool_done(i, "xdt"))
                    for hd in range(HG):
                        ins = pe.matmul(out[:, hd * HP:(hd + 1) * HP], cut(E[(2 * i + hd // 3) % 4], h=3)[:, hd % 3, :],
                                        xdt[i % 2][:, hd * HP:(hd + 1) * HP], start=True, stop=True)
                    ins.then_inc(c.units_done, 1)
                elif kind == "yT":
                    pe.wait_ge(s["g_dve"], 3 + i)
                    transposes(c, pe, out, [cut(zs, t=NT)[:, i // 4, (3 * (i % 4) + b) * P:(3 * (i % 4) + b + 1) * P] for b in range(3)])
                elif kind == "out":
                    if i % 2 == 0:
                        t = i // 2
                        pe.wait_ge(s["yT_act"], 6 * t + 6)
                        pe.wait_ge(s["yT_dve"], 2 * t + 2)
                        out_rows(c, pe, U, s, lambda j: cut(yT, t=NT)[:, t, j * P:(j + 1) * P], TILES_A - 3, 3, t)
                else:
                    R.pe(pe, key)

        @block.vector
        def _(dve):
            def chain(signal, start=0):
                n = [start]

                def step(ins):
                    n[0] += 1
                    ins.then_inc(signal, 1)
                    dve.wait_ge(signal, n[0])
                return step

            for t in range(NT):
                x_norm.dve(dve, t)
            y_step = chain(s["y_dve"])

            def decay_scores(i):
                dve.wait_ge(s["exp_act"], i + 1)
                dve.tensor_tensor(cut(E[i % 4], h=3), cut(E[i % 4], h=3), spread_mid(cbm[(i // 2) % 2][:, :], 3),
                                  ALU.mult).then_inc(s["m_dve2"], 1)

            for key in order:
                kind, i = key
                if kind in ("out",) + Router.KINDS:
                    R.dve(dve, key)
                    continue
                if key == ("outm", 1):
                    step = chain(s["g_dve"])
                    dve.wait_ge(s["g_act"], 8)
                    step(dve.tensor_scalar(gss[:, :], gss[:, :], 1.0 / GW, EPS, ALU.mult, ALU.add))
                    dve.wait_ge(s["g_act"], 9)
                    step(dve.reciprocal(gss[:, :], gss[:, :]))
                    for st, (ch, gr) in enumerate(steps):
                        z = cut(zs, t=NT)[:, ch, GW * gr:GW * gr + GW]
                        dve.tensor_scalar(z, z, gss[:, st:st + 1], None, ALU.mult).then_inc(s["g_dve"], 1)
                if kind == "outm":
                    continue
                bank = U.bank(key)
                if kind == "dt":
                    step = chain(s["dt_dve"])
                    U.wait_done(dve, key)
                    dve.wait_ge(ld_small, 16)
                    step(dve.tensor_tensor(cut(dtx, t=NT), cut(bank[:, 0:48], t=NT), spread_mid(c.f("dt_bias"), NT), ALU.add))
                    step(dve.scalar_tensor_tensor(out=t_[:, :], in0=dtx[:, :], scalar=-1.0, in1=dtx[:, :], op0=ALU.mult, op1=ALU.max))
                    dve.wait_ge(s["dt_act"], 2)
                    step(dve.tensor_scalar(s_[:, :], t_[:, :], 2.0, None, ALU.add))
                    step(dve.reciprocal(s_[:, :], s_[:, :]))
                    step(dve.tensor_tensor(s_[:, :], s_[:, :], t_[:, :], ALU.mult))
                    step(dve.tensor_tensor(s2[:, :], s_[:, :], s_[:, :], ALU.mult))
                    step(dve.tensor_scalar(t_[:, :], s2[:, :], 1.0 / 15, None, ALU.mult))
                    for q in (13, 11, 9, 7, 5, 3):
                        step(dve.scalar_tensor_tensor(out=t_[:, :], in0=t_[:, :], scalar=1.0 / q, in1=s2[:, :], op0=ALU.add, op1=ALU.mult))
                    step(dve.scalar_tensor_tensor(out=t_[:, :], in0=t_[:, :], scalar=1.0, in1=s_[:, :], op0=ALU.add, op1=ALU.mult))
                    step(dve.tensor_scalar(dt[:, :], dtx[:, :], 0.0, None, ALU.max))
                    step(dve.scalar_tensor_tensor(out=dt[:, :], in0=t_[:, :], scalar=2.0, in1=dt[:, :], op0=ALU.mult, op1=ALU.add))
                    step(dve.scalar_tensor_tensor(out=cut(adt, t=NT), in0=cut(dt, t=NT), scalar=-1.0, in1=spread_mid(ea[:, :], NT),
                                                  op0=ALU.mult, op1=ALU.mult))
                elif kind == "conv":
                    step = chain(s["conv_dve"], 4 * i)
                    U.wait_done(dve, key)
                    if i >= 3:
                        dve.wait_ge(s["conv_act"], i - 2)
                    a = cut(acc, b=3)[:, i % 3, :]
                    step(dve.tensor_scalar(a, bank[:, 0:SEQ], c.f("conv_w", 4 * i + 3, 4 * i + 4), c.f("conv_b", i, i + 1), ALU.mult, ALU.add))
                    for back in (1, 2, 3):
                        step(dve.scalar_tensor_tensor(out=a[:, back:], in0=bank[:, 0:SEQ - back], scalar=c.f("conv_w", 4 * i + 3 - back, 4 * i + 4 - back),
                                                      in1=a[:, back:], op0=ALU.mult, op1=ALU.add))
                elif kind == "ac":
                    U.wait_done(dve, key)
                    step = chain(s["ac_dve"])
                    step(dve.tensor_copy(acum[:, :], bank[:, 0:48]))
                    step(dve.tensor_tensor(toend[:, :], bank[:, 48:72], acum[:, 0:24], ALU.subtract))
                elif key == ("z", 0):
                    for t in range(NT):
                        mem_norm.dve(dve, t)
                elif kind == "cb":
                    U.wait_done(dve, key)
                    dve.tensor_tensor(cbm[i % 2][:, :], bank[:, 0:P], c.f("tri"), ALU.mult).then_inc(s["cb_dve"], 1)
                elif kind == "A":
                    ch, gr = steps[i // 2]
                    U.wait_done(dve, key)
                    if i >= 4:
                        dve.wait_ge(c.units_done, U.at["yd", (i - 4) // 2] + 1)
                    for hh in range(3):
                        hd = 24 * ch + HG * gr + 3 * (i % 2) + hh
                        dve.tensor_scalar(cut(E[i % 4], h=3)[:, hh, :], cut(bank[:, 0:GW], h=3)[:, hh, :], acum[:, hd:hd + 1], 0.0,
                                          ALU.subtract, ALU.min).then_inc(s["seg_dve"], 1)
                    if i == 0:
                        dve.wait_ge(s["cb_dve"], 1)
                    else:
                        dve.wait_ge(s["cb_dve"], (i - 1) // 2 + 1)
                        decay_scores(i - 1)
                    if i == 15:
                        decay_scores(15)
                elif kind == "sc":
                    U.wait_done(dve, key)
                    step = chain(s["sm_max"], 2 * i)
                    if i >= 2:
                        dve.wait_ge(c.units_done, U.at["pT", i - 2] + 1)
                    step(dve.tensor_reduce(smc[:, 2 * i:2 * i + 2], cut(bank, t=NT), X, ALU.max))
                    step(dve.tensor_scalar(smc[:, 16 + 2 * i:18 + 2 * i], smc[:, 2 * i:2 * i + 2], -MEM_SCALE, None, ALU.mult))
                elif kind == "pT":
                    step = chain(s["sm_dve"], 2 * i)
                    dve.wait_ge(s["sm_act"], 2 * i + 2)
                    step(dve.reciprocal(smc[:, 48 + 2 * i:50 + 2 * i], smc[:, 32 + 2 * i:34 + 2 * i]))
                    step(dve.tensor_tensor(cut(ex[i % 2], t=NT), cut(ex[i % 2], t=NT), spread_last(smc[:, 48 + 2 * i:50 + 2 * i], 256), ALU.mult))
                elif kind == "yd":
                    ch, gr = steps[i]
                    z = cut(zs, t=NT)[:, ch, GW * gr:GW * gr + GW]
                    if ch:
                        yo = ("yo", gr)
                        U.wait_done(dve, yo)
                        y_step(dve.tensor_tensor(heads(yt[:, :]), heads(U.bank(yo)[:, 0:GW]), spread_last(eac[:, HG * gr:HG * gr + HG], HP), ALU.mult))
                    U.wait_done(dve, key)
                    dve.wait_ge(s["pool_x"], pool_done(i, "xd"))
                    if ch:
                        y_step(dve.tensor_tensor(yt[:, :], bank[:, 0:GW], yt[:, :], ALU.add))
                        y_step(dve.tensor_tensor(yt[:, :], xd[i % 2][:, :], yt[:, :], ALU.add))
                    else:
                        dve.wait_ge(s["z_ev"], 6)
                        y_step(dve.tensor_tensor(yt[:, :], bank[:, 0:GW], xd[i % 2][:, :], ALU.add))
                    y_step(dve.tensor_tensor(z, z, yt[:, :], ALU.mult))
                elif kind == "yT" and i % 2:
                    U.wait_done(dve, key)
                    at = 3 * (i % 4)
                    dve.tensor_tensor(cut(cut(yT, t=NT)[:, i // 4, at * P:(at + 3) * P], b=3), cut(bank[:, 0:3 * P], b=3),
                                      spread_last(c.f("gnorm", at, at + 3), P), ALU.mult).then_inc(s["yT_dve"], 1)


class ExpertTiles:

    HALF = WT // 2

    def __init__(self, c, layer):
        self.c, self.layer = c, layer

    def late_tile(self, n):
        return self.c.late[:, n * self.HALF:(n + 1) * self.HALF]

    def tile(self, n):
        at = (2 * FIRST_SLOT[self.layer] + n) % (2 * SLOTS) * self.HALF
        return self.c.ring[:, at:at + self.HALF]

    def weights(self, e, what, half):
        w = self.c.ins["w_" + what][self.layer, bass.ds(e, 1)]
        if what == "down":
            return w[:, 256 * half:256 * half + 256, :].rearrange("o (j p) c -> (o p) j c", p=P)
        return w.rearrange("o (p k) c -> (o p) k c", k=KD)[:, 4 * half:4 * half + 4, :]

    def load_tile(self, sp, s, p, n):
        q = n % 2
        if n < 8:
            half, what = n // 4, ("gate", "up")[n // 2 % 2]
            dst, loaded = cut(self.tile(n), k=4), s[f"gu{half}_loaded"]
        else:
            half, what = (n - 8) // 2, "down"
            dst, loaded = cut(self.tile(n), j=2), s[f"down{half}_loaded"]
        sp.dma_start(dst, self.weights(p * 2 + q, what, half)).then_inc(loaded, 16)

    def load_second_pair(self, sp):
        for w, what in enumerate(("gate", "up")):
            for q in range(2):
                sp.dma_start(cut(self.late_tile(2 * w + q), k=4), self.weights(2 + q, what, 0)).then_inc(self.c.late_loaded, 16)


class Experts(ExpertTiles):

    SEMS = ("pick gated gathered xg_ready gu_done silu_done hid_ready turned turned_ready down_done gates_turned gates_ready "
            "y_ready scattered gu0_loaded gu1_loaded down0_loaded down1_loaded")
    PAIRS = NE // 2

    def __init__(self, c, layer, ctx):
        super().__init__(c, layer)
        sb = lambda name, n: c.sb(f"e{layer}_{name}", n, ctx)
        self.pick = sb("pick", NT * 2 * TOKS)
        self.gated = sb("gated", NT * 2 * TOKS)
        self.xg = sb("xg", KD * 2 * TOKS)
        self.silu = sb("silu", DE)
        self.hid = sb("hid", DE)
        self.turned = sb("turned", DE)
        self.gates_T = sb("gates_T", SEQ)
        self.y = [sb(f"y{i}", 512) for i in range(2)]
        self.sums, (self.b_gate, self.b_up, self.b_gather, self.b_turn) = c.banks[0:4], c.banks[4:8]
        self.b_down = [self.b_gate, self.b_up]
        self.memory = MemoryAhead(self, ctx) if layer == 0 else None

    def rounds(self, eng, body):
        body(0)
        most = eng.value_load(self.c.most[0:1, 0:1], min_val=0, max_val=SEQ)
        for rnd in range(1, ROUNDS):
            with eng.If(most > rnd * TOKS):
                body(rnd)
        eng.nop()

    def block(self):
        c, layer, PAIRS, memory = self.c, self.layer, self.PAIRS, self.memory
        ahead = lambda rnd: memory is not None and rnd == 0
        second = lambda rnd: layer == 1 and rnd == 0
        sets = experts_sems(c)
        with c.nc.Block() as block:

            @block.sync
            def _(sp):
                def body(rnd):
                    s = sets[rnd]
                    if rnd:
                        sp.wait_ge(sets[rnd - 1]["down_done"], 2 * PAIRS)
                        for n in range(12):
                            self.load_tile(sp, s, 0, n)

                    def gate_up(p, half, of=None):
                        for w in range(2):
                            sp.wait_ge(s["gu_done"], (p - 1 if of is None else of) * 4 + (2 * half + w + 1))
                            for q in range(2):
                                self.load_tile(sp, s, p, 4 * half + 2 * w + q)

                    def down(p):
                        for half in range(2):
                            sp.wait_ge(s["down_done"], p * 2 + (half - 1))
                            for n in range(2):
                                self.load_tile(sp, s, p, 8 + 2 * half + n)

                    if second(rnd):
                        gate_up(2, 0, of=0)
                        gate_up(1, 1)
                        down(1)
                        with sp.Fori(2, PAIRS - 1) as p:
                            gate_up(p, 1)
                            down(p)
                            gate_up(p + 1, 0)
                        gate_up(PAIRS - 1, 1)
                        down(PAIRS - 1)
                    else:
                        with sp.Fori(1, PAIRS) as p:
                            gate_up(p, 0)
                            gate_up(p, 1)
                            down(p)
                    sp.wait_ge(s["gu_done"], 4 * PAIRS)
                    if rnd:
                        sp.wait_ge(s["down_done"], 2 * PAIRS)

                if memory:
                    memory.load(sp)
                self.rounds(sp, body)
                if layer == 0:
                    s = sets[0]
                    for n in range(SLOTS):
                        if n >= 4:
                            sp.wait_ge(s["down_done"], 2 * PAIRS - 5 + n)
                        c.load_mixer_tile(sp, TILES_A + n)

            @block.vector
            def _(dve):
                def body(rnd):
                    s = sets[rnd]
                    iota = c.f("iota", rnd * TOKS, (rnd + 1) * TOKS)

                    def pick(p):
                        for t in range(NT):
                            for q in range(2):
                                dve.tensor_scalar(self.pick[:, (2 * t + q) * TOKS:(2 * t + q + 1) * TOKS], iota,
                                                  c.pos[:, bass.ds(p * 2 + (t * NE + q), 1)], None, ALU.is_equal).then_inc(s["pick"], 1)

                    def gated(p):
                        for t in range(NT):
                            for q in range(2):
                                at = bass.ds(p * 2 + (t * NE + q), 1)
                                dve.tensor_scalar(self.gated[:, (2 * t + q) * TOKS:(2 * t + q + 1) * TOKS], iota, c.pos[:, at],
                                                  c.gates[:, at], ALU.is_equal, ALU.mult).then_inc(s["gated"], 1)

                    def gathered(half):
                        dve.tensor_tensor(cut(self.xg[:, 512 * half:512 * half + 512], k=4), cut(self.b_gather, k=4),
                                          spread_last(c.f(f"ffn_norm{layer}", 4 * half, 4 * half + 4), 2 * TOKS), ALU.mult).then_inc(s["xg_ready"], 1)

                    def pair(p, last=False):
                        gated(p)
                        if not last:
                            pick(p + 1)
                        dve.wait_ge(s["silu_done"], p + 1)
                        dve.tensor_tensor(self.hid[:, :], self.silu[:, :], self.b_up[:, :], ALU.mult).then_inc(s["hid_ready"], 1)
                        if not last:
                            dve.wait_ge(s["gathered"], p * 2 + 3)
                            gathered(0)
                        dve.wait_ge(s["down_done"], p * 2 + 2)
                        dve.tensor_copy(self.y[1][:, :], self.b_down[1][:, :]).then_inc(s["y_ready"], 1)
                        if not last:
                            dve.wait_ge(s["gathered"], p * 2 + 4)
                            gathered(1)

                    if rnd:
                        dve.wait_ge(sets[rnd - 1]["scattered"], 1)
                    pick(0)
                    for half in range(2):
                        dve.wait_ge(s["gathered"], half + 1)
                        gathered(half)
                    pair(0)
                    if ahead(rnd):
                        for t in range(NT):
                            memory.norm.dve(dve, t)
                    with dve.Fori(1, PAIRS - 1) as i:
                        pair(i)
                    pair(PAIRS - 1, last=True)
                    dve.wait_ge(s["scattered"], 1)

                self.rounds(dve, body)

            @block.scalar
            def _(act):
                def body(rnd):
                    s = sets[rnd]
                    if rnd:
                        act.wait_ge(sets[rnd - 1]["scattered"], 1)

                    def pair(p):
                        act.wait_ge(s["gu_done"], p * 4 + 4)
                        act.activation(self.silu[:, :], self.b_gate[:, :], ACT.Silu).then_inc(s["silu_done"], 1)
                        act.wait_ge(s["turned"], p + 1)
                        for half in range(2):
                            act.activation(self.turned[:, 256 * half:256 * half + 256], self.b_turn[:, 256 * half:256 * half + 256],
                                           ACT.Copy).then_inc(s["turned_ready"], 1)
                        act.wait_ge(s["down_done"], p * 2 + 2)
                        act.activation(self.y[0][:, :], self.b_down[0][:, :], ACT.Copy).then_inc(s["y_ready"], 1)
                        act.wait_ge(s["gates_turned"], p + 1)
                        act.activation(self.gates_T[:, :], self.b_turn[:, 0:SEQ], ACT.Copy).then_inc(s["gates_ready"], 1)

                    start = 0
                    if ahead(rnd):
                        pair(0)
                        for t in range(NT):
                            act.wait_ge(memory.ld[t], 16)
                            memory.norm.act(act, t)
                        start = memory.PAIRS + 1
                        for p in range(1, start):
                            memory.act(act, p)
                            pair(p)
                    with act.Fori(start, PAIRS) as i:
                        pair(i)

                self.rounds(act, body)

            @block.tensor
            def _(pe):
                def body(rnd):
                    s = sets[rnd]
                    xs = c.xs[:, :].rearrange("q (t k p) -> q t k p", t=NT, k=KD)

                    def gather(half):
                        for k in range(4):
                            for t in range(NT):
                                ins = pe.matmul(self.b_gather[:, k * P:(k + 1) * P], xs[:, t, 4 * half + k, :], cut(self.pick, t=NT)[:, t, :],
                                                start=(t == 0), stop=(t == NT - 1))
                        ins.then_inc(s["gathered"], 1)

                    def pair(p, first=False, last=False, side=False):
                        for half in range(2):
                            pe.wait_ge(s["xg_ready"], p * 2 + (half + 1))
                            late = second(rnd) and half == 0 and static(p, 1)
                            if late:
                                pe.wait_ge(c.late_loaded, 32 + 64)
                            elif second(rnd) and half == 0 and not static(p, 0):
                                pe.wait_ge(s["gu0_loaded"], p * 64)
                            else:
                                pe.wait_ge(s[f"gu{half}_loaded"], p * 64 + 64)
                            for w, bank in enumerate((self.b_gate, self.b_up)):
                                for k in range(4):
                                    for q in range(2):
                                        ins = pe.matmul(bank[q * TOKS:(q + 1) * TOKS, :], self.xg[:, (4 * half + k) * P + q * TOKS:(4 * half + k) * P + (q + 1) * TOKS],
                                                        cut(self.late_tile(2 * w + q) if late else self.tile(4 * half + 2 * w + q), k=4)[:, k, :],
                                                        start=(half == 0 and k == 0), stop=(half == 1 and k == 3))
                                ins.then_inc(s["gu_done"], 1)
                            if half == 0 and side:
                                pe.wait_ge(s["xg_ready"], p * 2 + 2)
                                memory.pe(pe, p)
                        if side:
                            pe.wait_ge(memory.ev, memory.banks_free[p])
                        if not last:
                            pe.wait_ge(s["pick"], p * 4 + 8)
                            gather(0)
                        pe.wait_ge(s["hid_ready"], p + 1)
                        for j in range(4):
                            ins = pe.transpose(self.b_turn[:, j * P:(j + 1) * P], self.hid[:, j * P:(j + 1) * P], c.f("ident"))
                        ins.then_inc(s["turned"], 1)
                        for half in range(2):
                            pe.wait_ge(s["turned_ready"], p * 2 + (half + 1))
                            pe.wait_ge(s[f"down{half}_loaded"], p * 32 + 32)
                            for j in range(2):
                                for out in range(2):
                                    for q in range(2):
                                        at = (2 * half + j) * P + q * TOKS
                                        ins = pe.matmul(self.b_down[out][q * TOKS:(q + 1) * TOKS, :], self.turned[:, at:at + TOKS],
                                                        cut(self.tile(8 + 2 * half + q), j=2)[:, j, 512 * out:512 * out + 512],
                                                        start=(half == 0 and j == 0), stop=(half == 1 and j == 1))
                            ins.then_inc(s["down_done"], 1)
                        pe.wait_ge(s["gated"], p * 4 + 4)
                        for t in range(NT):
                            ins = pe.transpose(self.b_turn[:, t * P:(t + 1) * P], cut(self.gated, t=NT)[:, t, :], c.f("ident"))
                        ins.then_inc(s["gates_turned"], 1)
                        if not last:
                            pe.wait_ge(s["xg_ready"], p * 2 + 3)
                            gather(1)
                        pe.wait_ge(s["y_ready"], p * 2 + 2)
                        pe.wait_ge(s["gates_ready"], p + 1)
                        for t in range(NT):
                            for out in range(2):
                                ins = pe.matmul(self.sums[2 * t + out][:, :], self.gates_T[:, t * P:(t + 1) * P], self.y[out][:, :],
                                                start=first, stop=last, skip_group_check=True)
                        if last:
                            ins.then_inc(s["scattered"], 1)

                    pe.wait_ge(s["pick"], 4)
                    gather(0)
                    pe.wait_ge(s["xg_ready"], 1)
                    gather(1)
                    pair(0, first=(rnd == 0))
                    start = 1
                    if second(rnd):
                        pair(1)
                        start = 2
                    if ahead(rnd):
                        start = memory.PAIRS + 1
                        for p in range(1, start):
                            pair(p, side=True)
                    with pe.Fori(start, PAIRS - 1) as i:
                        pair(i)
                    pair(PAIRS - 1, last=True)

                self.rounds(pe, body)

            if layer == 0:
                @block.gpsimd
                def _(pool):
                    c.clear(pool, "mixer")


def static(p, value):
    return isinstance(p, int) and p == value


class MemoryAhead:

    PAIRS = 6

    def __init__(self, E, ctx):
        c = self.c = E.c
        self.raw, self.xs, self.memnT = (c.sb(f"m1_{n}", NT * D, ctx) for n in ("raw", "xs", "memnT"))
        self.ld = [c.sem(f"m1_ld{t}") for t in range(NT)]
        self.norm = Norm(c, self.raw, 2, c.sem("m1_by_act"), c.sem("m1_by_dve"), self.xs)
        self.done, self.ev = c.sem("m1_done"), c.sem("m1_ev")
        self.bank = [E.b_gather, E.b_turn]
        self.banks_free = {1: 4, 2: 8, 3: 9, 4: 10, 5: 11, 6: 12}

    def load(self, sp):
        for t in range(NT):
            sp.dma_start(cut(self.raw, t=NT)[:, t, :], self.c.ins["mem"][0, t * P:(t + 1) * P, :]).then_inc(self.ld[t], 16)

    def pe(self, pe, p):
        c, x = self.c, cut(self.memnT, k=KD)
        if p <= 2:
            if p == 1:
                pe.wait_ge(self.norm.by_dve, 6)
            xs = self.xs[:, :].rearrange("q (t k p) -> q t k p", t=NT, k=KD)
            for b in range(2):
                i = 2 * (p - 1) + b
                blocks = [xs[:, t, 2 * i + kk, :] for kk in range(2) for t in range(NT)]
                for q, block in enumerate(blocks):
                    ins = pe.transpose(self.bank[b][:, q * P:(q + 1) * P], block, c.f("ident"))
                ins.then_inc(self.done, 1)
            return
        if p == 3:
            pe.wait_ge(self.ev, 8)
            pe.wait_ge(c.late_loaded, 32)
        w = cut(c.late[:, WT * ((p - 3) // 2):WT * ((p - 3) // 2) + WT], k=KD)
        if p <= 4:
            for h in (0, 1):
                at = P * (2 * (p - 3) + h)
                for k in range(KD):
                    ins = pe.matmul(self.bank[0][:, 256 * h:256 * h + 256], w[:, k, at:at + P], x[:, k, :], start=(k == 0), stop=(k == KD - 1))
        else:
            for k in range(KD):
                ins = pe.matmul(self.bank[0][:, :], x[:, k, P * (p - 5):P * (p - 4)], w[:, k, :], start=(k == 0), stop=(k == KD - 1))
        ins.then_inc(self.done, 1)

    def act(self, act, p):
        c = self.c
        if p <= 2:
            for b in range(2):
                i = 2 * (p - 1) + b
                act.wait_ge(self.done, i + 1)
                for kk in range(2):
                    k = 2 * i + kk
                    act.activation(cut(self.memnT, k=KD)[:, k, :], self.bank[b][:, kk * 256:(kk + 1) * 256], ACT.Copy,
                                   scale=c.f("mem_norm1", k, k + 1)).then_inc(self.ev, 1)
            return
        act.wait_ge(self.done, p + 2)
        dst = (c.mkT1, c.mv1)[(p - 3) // 2][:, 512 * ((p - 3) % 2):512 * ((p - 3) % 2) + 512]
        act.activation(dst, self.bank[0][:, :], ACT.Copy).then_inc(self.ev, 1)


def experts_sems(c):
    return [c.sems(f"experts_round{r}", Experts.SEMS) for r in range(ROUNDS)]


def first_pair_loader(c, layer):
    tiles = ExpertTiles(c, layer)
    s = experts_sems(c)[0]

    def load(sp, i):
        for n in (2 * i, 2 * i + 1):
            tiles.load_tile(sp, s, 0, n)

    return load


def moe(c, layer):
    with ExitStack() as ctx:
        Experts(c, layer, ctx).block()


def mixer_b(c):
    names = ("h_whole x_act x_dve xT_ev xk_dve kv_ev kr_dve kT_ev q_ev qr_dve qT_ev qm_ev as_dve as_act "
             "an_dve an_pool aT_ev av_ev sm_max sm_dve sm_act pt_ev pv_ev out_tile " + Router.SEMS)
    s = c.sems("mixer", names)
    cleared = c.sem("b_cleared")
    with ExitStack() as ctx:
        sb = lambda name, n: c.sb("b_" + name, n, ctx)
        xkT, qT, kd, kT, ee = c.carve_late(KD * SEQ, 8 * SEQ, NT * 512, 4 * SEQ, 4 * 512)
        ee = [ee[:, 512 * i:512 * i + 512] for i in range(4)]
        xnT, qtok = sb("xnT", KD * SEQ), sb("qtok", NT * 1024)
        attT = qtok
        vt, qmT = sb("vt", NT * 256), sb("qmT", 1024)
        mkT, mv = c.mkT1, c.mv1
        mT = qmT
        ex, pTs = [sb(f"ex{i}", 512) for i in range(2)], sb("pTs", 512)
        aTs = [sb(f"aTs{i}", 512) for i in range(2)]
        rot_c, rot_s = sb("rot_c", P), sb("rot_s", P)
        smc = sb("smc", 64)
        col = sb("col", 16 * 12)

        parts = [(t, kv, odd) for pair in range(2) for t in range(NT) for kv in (2 * pair, 2 * pair + 1) for odd in range(2)]
        NA = len(parts)
        width = lambda n: P if parts[n][0] == 0 else 2 * P
        order = [("xT", i) for i in range(4)] + [("kv", 0), ("kv", 1), ("q", 0), ("q", 1), ("kT", 0), ("kT", 1), ("qm", 0), ("qT", 0), ("qT", 1)]
        between = [[("q", 2)], [("q", 3)], [("qm", 1)], [("qT", 2)], [("qT", 3)], [("sc", 0)], [("sc", 1), ("qm", 2)], [("pT", 0)],
                   [("pv", 0), ("sc", 2)], [("pT", 1), ("qm", 3)], [("pv", 1), ("sc", 3)], [("pT", 2)], [("pv", 2)], [("pT", 3)], [("pv", 3)],
                   [("outm", 0)], [("outm", 1)], [("outm", 2)], [("outm", 3)]]
        for n in range(NA + 3):
            if n < NA:
                order += [("as", n)]
            order += between[n]
            if 2 <= n < NA + 2:
                order += [("aT", n - 2)]
            if n >= 3:
                order += [("av", n - 3)]
        order += [("out", i) for i in range(4)] + Router.UNITS
        holds = {("outm", h): [("out", i) for i in range(4)] for h in range(4)}

        def freed(kind, i):
            if kind in Router.KINDS:
                return Router.freed(s, kind, i)
            return {"xT": (s["xk_dve"], i + 1), "kv": (s["kv_ev"], 2 * i + 2), "q": (s["q_ev"], i + 1), "kT": (s["kT_ev"], i + 1),
                    "qT": (s["qT_ev"], i + 1), "qm": (s["qm_ev"], i + 1), "as": (s["as_dve"], 5 * i + 1), "aT": (s["aT_ev"], i + 1),
                    "av": (s["av_ev"], i + 1), "sc": (s["sm_act"], 2 * i + 2), "pT": (s["pt_ev"], i + 1), "pv": (s["pv_ev"], i + 1),
                    "out": (s["h_new"], i + 1)}[kind]

        U = Units(c, order, freed, holds)
        R = Router(c, U, s, 1, xnT, sb("work", 512))
        norm = Norm(c, c.h, 0, s["x_act"], s["x_dve"])

        def tile_used(n):
            last = [("kv", 1), ("q", 1), ("q", 3), ("qm", 3)]
            if n - B0 < 4:
                return c.units_done, U.at[last[n - B0]] + 1
            if n - B0 < 6:
                return s["out_tile"], n - B0 - 3
            return c.units_done, U.at["out", 3] + 1

        def kd_heads(t, dup):
            return kd[:, :].rearrange("p (t h d c) -> p t h d c", t=NT, h=KV_HEADS, d=2)[:, t, :, dup, :]

        block = ctx.enter_context(c.nc.Block())

        @block.sync
        def _(sp):
            first_pair = first_pair_loader(c, 1)
            for n in range(B0 + SLOTS, B0 + TILES_B + SLOTS):
                if n == B0 + TILES_B + 3:
                    sp.wait_ge(c.units_done, U.at["aT", NA - 1] + 1)
                    ExpertTiles(c, 1).load_second_pair(sp)
                sp.wait_ge(*tile_used(n - SLOTS))
                if n < B0 + TILES_B:
                    c.load_mixer_tile(sp, n)
                else:
                    sp.wait_ge(cleared, 1)
                    first_pair(sp, n - B0 - TILES_B)

        @block.gpsimd
        def _(pool):
            c.clear(pool, *(f"experts_round{r}" for r in range(ROUNDS)))
            pool.nop().then_inc(cleared, 1)
            R.pool(pool)
            for i in range(NA):
                pool.wait_ge(s["an_dve"], 2 * i + 2)
                w, k = width(i), 12 * i
                e = cut(ee[i % 4][:, 0:2 * w], q=2)
                pool.tensor_tensor(e, e, spread_last(col[:, k + 8:k + 10], w), ALU.mult).then_inc(s["an_pool"], 1)

        @block.scalar
        def _(act):
            norm.warm(act)
            for t in range(NT):
                act.wait_ge(s["h_whole"], 2 * t + 2)
                norm.act(act, t)
            for key in order:
                kind, i = key
                if kind in ("out",) + Router.KINDS:
                    R.act(act, key)
                    continue
                if kind == "outm":
                    continue
                bank = U.bank(key)
                if kind == "xT":
                    U.wait_done(act, key)
                    for kk in range(2):
                        k = 2 * i + kk
                        act.activation(cut(xnT, k=KD)[:, k, :], bank[:, kk * 256:(kk + 1) * 256], ACT.Copy,
                                       scale=c.f("b_norm", k, k + 1)).then_inc(s["xT_ev"], 1)
                elif kind == "as":
                    act.wait_ge(s["as_dve"], 5 * i + 5)
                    w = width(i)
                    k = 12 * i
                    for q in range(2):
                        act.activation(ee[i % 4][:, q * w:(q + 1) * w], ee[i % 4][:, q * w:(q + 1) * w], ACT.Exp,
                                       bias=col[:, k + 2 + q:k + 3 + q], accum_out=col[:, k + 4 + q:k + 5 + q]).then_inc(s["as_act"], 1)
                    act.activation(col[:, k + 6:k + 8], col[:, k + 6:k + 8], ACT.Exp).then_inc(s["as_act"], 1)
                elif kind == "sc":
                    U.wait_done(act, key)
                    act.wait_ge(s["sm_max"], 2 * i + 2)
                    for t in range(NT):
                        act.activation(cut(ex[i % 2], t=NT)[:, t, :], cut(bank, t=NT)[:, t, :], ACT.Exp, scale=MEM_SCALE,
                                       bias=smc[:, 16 + 2 * i + t:17 + 2 * i + t],
                                       accum_out=smc[:, 32 + 2 * i + t:33 + 2 * i + t]).then_inc(s["sm_act"], 1)
                else:
                    U.wait_done(act, key)
                    if kind == "kv":
                        act.activation(cut(vt, t=NT)[:, i, :], bank[:, 256:512], ACT.Copy).then_inc(s["kv_ev"], 1)
                        act.activation(kd_heads(i, 0), cut(bank[:, 0:256], h=4), ACT.Copy).then_inc(s["kv_ev"], 1)
                    elif kind == "q":
                        act.activation(cut(qtok, t=NT)[:, i % 2, 512 * (i // 2):512 * (i // 2) + 512], bank[:, :], ACT.Copy).then_inc(s["q_ev"], 1)
                    elif kind == "kT":
                        act.activation(cut(kT, g=4)[:, :, i * P:(i + 1) * P], cut(bank, g=4), ACT.Copy).then_inc(s["kT_ev"], 1)
                    elif kind == "qT":
                        act.activation(cut(qT, g=8)[:, 4 * (i // 2):4 * (i // 2) + 4, (i % 2) * P:(i % 2) * P + P], cut(bank, g=4),
                                       ACT.Copy).then_inc(s["qT_ev"], 1)
                    elif kind == "qm":
                        act.activation(cut(qmT, h=4)[:, i, :], bank[:, 0:256], ACT.Copy).then_inc(s["qm_ev"], 1)
                    elif kind == "aT":
                        if i >= 2:
                            act.wait_ge(c.units_done, U.at["av", i - 2] + 1)
                        act.activation(aTs[i % 2][:, 0:2 * width(i)], bank[:, 0:2 * width(i)], ACT.Copy).then_inc(s["aT_ev"], 1)
                    elif kind == "av":
                        t, kv, odd = parts[i]
                        r = slice(64 * odd, 64 * odd + 64)
                        act.activation(cut(attT, j=8)[r, 2 * kv:2 * kv + 2, t * P:(t + 1) * P], cut(bank[r, 0:256], j=2),
                                       ACT.Copy).then_inc(s["av_ev"], 1)
                    elif kind == "pT":
                        act.activation(pTs[:, :], bank[:, :], ACT.Copy).then_inc(s["pt_ev"], 1)
                    elif kind == "pv":
                        act.activation(cut(mT, h=4)[:, i, :], bank[:, 0:256], ACT.Copy).then_inc(s["pv_ev"], 1)

        @block.tensor
        def _(pe):
            for key in order:
                kind, i = key
                if kind == "outm":
                    memory_rows(c, pe, U, s, mT, B0 + 4, i)
                    continue
                out = U.bank(key)
                if kind != "out":
                    U.wait_free(pe, key)
                if kind == "xT":
                    if i == 0:
                        pe.wait_ge(s["x_dve"], 6)
                    norm_T_units(c, pe, out, i)
                elif kind in ("kv", "q"):
                    n = B0 + (0 if kind == "kv" else 1 + i // 2)
                    t = i % 2
                    if t == 0:
                        c.wait_tile(pe, n)
                    if key == ("kv", 0):
                        pe.wait_ge(s["xk_dve"], 4)
                    if key == ("q", 0):
                        pe.wait_ge(s["xT_ev"], 8)
                    w, x = c.cols_tile(n), cut(xkT if kind == "kv" else xnT, k=KD)
                    project(c, pe, out[:, :], lambda k: x[:, k, t * P:(t + 1) * P], lambda k: w[:, k, :])
                elif kind == "qm":
                    n = B0 + 3
                    if i == 0:
                        c.wait_tile(pe, n)
                    w, x = c.cols_tile(n), cut(xnT, k=KD)
                    project(c, pe, out[:, 0:256], lambda k: w[:, k, P * i:P * i + P], lambda k: x[:, k, :])
                elif kind == "kT":
                    pe.wait_ge(s["kr_dve"], 5 * i + 5)
                    transposes(c, pe, out, [kd[:, 512 * i + P * q:512 * i + P * q + P] for q in range(4)])
                elif kind == "qT":
                    pe.wait_ge(s["qr_dve"], 4 * i + 4)
                    at = 1024 * (i % 2) + 512 * (i // 2)
                    transposes(c, pe, out, [qtok[:, at + P * q:at + P * q + P] for q in range(4)])
                elif kind == "as":
                    t, kv, odd = parts[i]
                    r, w = slice(64 * odd, 64 * odd + 64), width(i)
                    pe.wait_ge(s["qT_ev"], 2 if kv < 2 else 4)
                    pe.wait_ge(s["kT_ev"], 2)
                    for q in range(2):
                        ins = pe.matmul(out[:, q * w:(q + 1) * w], cut(qT, g=8)[r, 2 * kv + q, t * P:(t + 1) * P], cut(kT, g=4)[r, kv, 0:w],
                                        start=True, stop=True)
                    ins.then_inc(c.units_done, 1)
                elif kind == "aT":
                    pe.wait_ge(s["an_pool"], i + 1)
                    transposes(c, pe, out, [ee[i % 4][:, q * P:(q + 1) * P] for q in range(2 * width(i) // P)])
                elif kind == "av":
                    t, kv, odd = parts[i]
                    r, nb = slice(64 * odd, 64 * odd + 64), width(i) // P
                    pe.wait_ge(s["aT_ev"], i + 1)
                    for q in range(2):
                        for m in range(nb):
                            ins = pe.matmul(out[r, q * P:(q + 1) * P], cut(vt, t=NT)[:, m, 64 * kv:64 * kv + 64],
                                            aTs[i % 2][:, (q * nb + m) * P:(q * nb + m + 1) * P], start=(m == 0), stop=(m == nb - 1))
                    ins.then_inc(c.units_done, 1)
                elif kind == "sc":
                    pe.wait_ge(s["qm_ev"], i + 1)
                    attend_scores(c, pe, out, qmT, mkT, i)
                elif kind == "pT":
                    pe.wait_ge(s["sm_dve"], 2 * i + 2)
                    transposes(c, pe, out, [cut(ex[i % 2], t=NT)[:, t, m * P:(m + 1) * P] for m in range(2) for t in range(NT)])
                elif kind == "pv":
                    pe.wait_ge(s["pt_ev"], i + 1)
                    attend_values(c, pe, out, mv, pTs, i)
                elif kind == "out":
                    if i % 2 == 0:
                        t = i // 2
                        if t == 0:
                            pe.wait_ge(s["av_ev"], NA)
                        out_rows(c, pe, U, s, lambda j: cut(attT, j=8)[:, j, t * P:(t + 1) * P], B0 + 5, 2, t)
                else:
                    R.pe(pe, key)

        @block.vector
        def _(dve):
            def chain(signal, start=0):
                n = [start]

                def step(ins):
                    n[0] += 1
                    ins.then_inc(signal, 1)
                    dve.wait_ge(signal, n[0])
                return step

            def turn(step, x, t, heads):
                a, b = cut(rot_c[:, 0:16 * heads], h=heads), cut(rot_s[:, 0:16 * heads], h=heads)
                step(dve.tensor_tensor(a, x[:, :, 0:16], spread_mid(c.f("cos", 16 * t, 16 * t + 16), heads), ALU.mult))
                step(dve.tensor_tensor(b, x[:, :, 0:16], spread_mid(c.f("sin", 16 * t, 16 * t + 16), heads), ALU.mult))
                step(dve.tensor_tensor(x[:, :, 0:8], a[:, :, 0:8], b[:, :, 8:16], ALU.subtract))
                step(dve.tensor_tensor(x[:, :, 8:16], a[:, :, 8:16], b[:, :, 0:8], ALU.add))

            def inverse(i):
                k = 12 * i
                step = chain(s["an_dve"], 2 * i)
                dve.wait_ge(s["as_act"], 3 * i + 3)
                step(dve.tensor_tensor(col[:, k + 8:k + 10], col[:, k + 4:k + 6], col[:, k + 6:k + 8], ALU.add))
                step(dve.reciprocal(col[:, k + 8:k + 10], col[:, k + 8:k + 10]))

            def memory_softmax(i):
                step = chain(s["sm_dve"], 2 * i)
                dve.wait_ge(s["sm_act"], 2 * i + 2)
                step(dve.reciprocal(smc[:, 48 + 2 * i:50 + 2 * i], smc[:, 32 + 2 * i:34 + 2 * i]))
                step(dve.tensor_tensor(cut(ex[i % 2], t=NT), cut(ex[i % 2], t=NT), spread_last(smc[:, 48 + 2 * i:50 + 2 * i], 256), ALU.mult))

            for t in range(NT):
                finish_h(c, dve, t, s["h_whole"])
            for t in range(NT):
                norm.dve(dve, t)
            for key in order:
                kind, i = key
                if kind in ("out",) + Router.KINDS:
                    R.dve(dve, key)
                    continue
                if kind == "outm":
                    continue
                bank = U.bank(key)
                if kind == "xT":
                    dve.wait_ge(s["xT_ev"], 2 * i + 2)
                    dve.tensor_tensor(cut(xkT, k=KD)[:, 2 * i:2 * i + 2, :], cut(bank, k=2), spread_last(c.f("kv_norm", 2 * i, 2 * i + 2), SEQ),
                                      ALU.mult).then_inc(s["xk_dve"], 1)
                elif kind == "kv":
                    step = chain(s["kr_dve"], 5 * i)
                    dve.wait_ge(s["kv_ev"], 2 * i + 2)
                    turn(step, kd_heads(i, 0), i, KV_HEADS)
                    step(dve.tensor_copy(kd_heads(i, 1), kd_heads(i, 0)))
                elif kind == "q":
                    dve.wait_ge(s["q_ev"], i + 1)
                    at = 1024 * (i % 2) + 512 * (i // 2)
                    turn(chain(s["qr_dve"], 4 * i), cut(qtok[:, at:at + 512], h=8), i % 2, 8)
                elif kind == "as":
                    if i >= 2:
                        inverse(i - 2)
                    for kind2, h in between[i]:
                        if kind2 == "pT":
                            memory_softmax(h)
                    t, kv, odd = parts[i]
                    w = width(i)
                    step = chain(s["as_dve"], 5 * i)
                    U.wait_done(dve, key)
                    if i >= 4:
                        dve.wait_ge(c.units_done, U.at["aT", i - 4] + 1)
                    mask = c.f("band_cur") if t == 0 else c.small[:, AT["band_prev"][0]:AT["band_prev"][0] + 2 * P]
                    e, k = cut(ee[i % 4][:, 0:2 * w], q=2), 12 * i
                    sinks = c.f("sinks", 4 * kv + odd, 4 * kv + odd + 3)[:, ::2]
                    step(dve.scalar_tensor_tensor(out=e, in0=cut(bank[:, 0:2 * w], q=2), scalar=ATT_SCALE, in1=spread_mid(mask, 2),
                                                  op0=ALU.mult, op1=ALU.add))
                    step(dve.tensor_reduce(col[:, k:k + 2], e, X, ALU.max))
                    step(dve.tensor_tensor(col[:, k:k + 2], col[:, k:k + 2], sinks, ALU.max))
                    step(dve.tensor_scalar(col[:, k + 2:k + 4], col[:, k:k + 2], -1.0, None, ALU.mult))
                    step(dve.tensor_tensor(col[:, k + 6:k + 8], sinks, col[:, k:k + 2], ALU.subtract))
                elif kind == "aT" and i >= NA - 2:
                    inverse(i)
                elif kind == "sc":
                    U.wait_done(dve, key)
                    step = chain(s["sm_max"], 2 * i)
                    if i >= 2:
                        dve.wait_ge(c.units_done, U.at["pT", i - 2] + 1)
                    step(dve.tensor_reduce(smc[:, 2 * i:2 * i + 2], cut(bank, t=NT), X, ALU.max))
                    step(dve.tensor_scalar(smc[:, 16 + 2 * i:18 + 2 * i], smc[:, 2 * i:2 * i + 2], -MEM_SCALE, None, ALU.mult))


def final_norm(c):
    s = c.sems("final", "ld h_whole act dve done")
    stored = [c.sem(f"stored{t}") for t in range(NT)]
    norm = Norm(c, c.h, 0, s["act"], s["dve"])
    with ExitStack() as ctx:
        w = c.sb("f_w", D, ctx)
        with c.nc.Block() as block:

            @block.sync
            def _(sp):
                sp.dma_start(w[:, :], c.ins["final_norm_w"].rearrange("(o n) -> o n", o=1).broadcast_to([P, D])).then_inc(s["ld"], 16)
                for t in range(NT):
                    sp.wait_ge(s["done"], t + 1)
                    sp.dma_start(c.out[0, t * P:(t + 1) * P, :], cut(c.h, t=NT)[:, t, :]).then_inc(stored[t], 16)
                for t in range(NT):
                    sp.wait_ge(stored[t], 16)

            @block.scalar
            def _(act):
                norm.warm(act)
                for t in range(NT):
                    act.wait_ge(s["h_whole"], 2 * t + 2)
                    norm.act(act, t, steps=2)

            @block.vector
            def _(dve):
                for t in range(NT):
                    finish_h(c, dve, t, s["h_whole"])
                dve.wait_ge(s["ld"], 16)
                for t in range(NT):
                    dve.wait_ge(s["act"], 2 * t + 1)
                    dve.tensor_scalar(norm.ss[t], norm.ss[t], 1.0 / D, EPS, ALU.mult, ALU.add).then_inc(s["dve"], 1)
                    dve.wait_ge(s["act"], 2 * t + 2)
                    dve.reciprocal(norm.r[t], norm.r[t]).then_inc(s["dve"], 1)
                    dve.wait_ge(s["dve"], 2 * t + 2)
                    hv = cut(c.h, t=NT)[:, t, :]
                    dve.scalar_tensor_tensor(out=hv, in0=hv, scalar=norm.r[t], in1=w[:, :], op0=ALU.mult,
                                             op1=ALU.mult).then_inc(s["done"], 1)


def build(nc, ins, out):
    with ExitStack() as ctx:
        c = Core(nc, ins, out, ctx)
        mixer_a(c)
        with ExitStack() as between:
            c.mkT1, c.mv1 = c.sb("mkT1", 1024, between), c.sb("mv1", 1024, between)
            moe(c, 0)
            mixer_b(c)
        moe(c, 1)
        final_norm(c)


INPUTS = ["x", "mem", "a_in_w", "a_out_w", "w_kv", "b_in_w", "b_out_w", "mem_w_kv", "w_gate", "w_up", "w_down", "final_norm_w"]


def pack_small(v):
    a = np.zeros((P, SMALL), np.float32)

    def put(name, x):
        at, w = AT[name]
        a[:, at:at + w] = x

    def by_row(w):
        return np.asarray(w).reshape(P, -1)

    i = np.arange(P)
    put("ident", np.eye(P))
    put("tri", i[:, None] <= i[None, :])
    put("ones", 1.0)
    put("iota", 1 + np.arange(ROUNDS * TOKS)[None, :])
    put("band_prev", np.where(i[None, :] > i[:, None], 0.0, NEG))
    put("band_cur", np.where(i[None, :] <= i[:, None], 0.0, NEG))
    put("index8", np.arange(EG)[None, :] - 100.0)
    freq = np.float32(500000.0) ** (np.float32(-2.0) * np.arange(HALF_ROT, dtype=np.float32) / np.float32(2 * HALF_ROT))
    angle = np.arange(SEQ, dtype=np.float32)[:, None] * freq[None, :].astype(np.float32)
    for name, fn in (("cos", np.cos), ("sin", np.sin)):
        table = np.concatenate([fn(angle), fn(angle)], axis=1).astype(np.float32)
        put(name, table.reshape(NT, P, 16).transpose(1, 0, 2).reshape(P, NT * 16))
    put("a_norm", by_row(v["a_norm_w"][0]))
    put("kv_norm", by_row(v["kv_norm_w"]))
    put("b_norm", by_row(v["b_norm_w"][0]))
    for n in (0, 1):
        put(f"mem_norm{n}", by_row(v["mem_norm_w"][n]))
        put(f"ffn_norm{n}", by_row(v["ffn_norm_w"][n]))
        put(f"route_b{n}", np.concatenate([v["router_group_b"][n], v["router_expert_b"][n]])[None, :])
        put(f"route_w{n}", by_row(np.concatenate([v["router_group_w"][n], v["router_expert_w"][n]], axis=1)))
    put("conv_w", np.asarray(v["a_conv_w"][0]).reshape(4, NCONV, P).transpose(2, 1, 0).reshape(P, NCONV * 4))
    put("conv_b", np.asarray(v["a_conv_b"][0]).reshape(NCONV, P).T)
    put("gnorm", np.asarray(v["a_gnorm_w"][0]).reshape(INNER // P, P).T)
    put("dt_bias", np.asarray(v["a_dt_bias"][0])[None, :])
    put("a_log", np.asarray(v["a_a_log"][0])[None, :])
    put("d_skip", np.asarray(v["a_d_skip"][0])[None, :])
    put("sinks", np.asarray(v["b_sinks"][0])[None, :])
    put("dt_w", by_row(np.asarray(v["a_in_w"][0])[:, INNER + CONV_CH:INNER + CONV_CH + SSD_HEADS]))
    return a


def kernel(**inputs):
    import concourse.bacc as bacc
    from concourse.bass_utils import run_bass_kernel_spmd

    nc = bacc.Bacc("TRN2", target_bir_lowering=False, num_devices=1)
    arrays = {name: np.ascontiguousarray(inputs[name]) for name in INPUTS}
    arrays["small"] = pack_small({k: np.asarray(x) for k, x in inputs.items()})
    aps = {}
    for name, a in arrays.items():
        aps[name] = nc.dram_tensor(f"in_{name}", a.shape, mybir.dt.from_np(a.dtype), kind="ExternalInput").ap()
    out = nc.dram_tensor("out", (1, SEQ, D), F32, kind="ExternalOutput").ap()
    build(nc, aps, out)
    result = run_bass_kernel_spmd(nc, [{f"in_{name}": a for name, a in arrays.items()}], core_ids=[0])
    return result.results[0]["out"]
```
